# Optimizing a Trainium2 kernel written in Bass

```python
import math
import jax, jax.numpy as jnp
from jax import lax
import numpy as np

D_MODEL = 2048
BATCH = 1
SEQ = 256
DEPTH = 4

N_MIXERS = 3
N_SSD_LAYERS = (DEPTH + 2) // 3
N_MLA_LAYERS = (DEPTH + 1) // 3
N_GDN_LAYERS = DEPTH // 3
DEEPNORM_ALPHA = (2.0 * DEPTH) ** 0.25
DEEPNORM_BETA = (8.0 * DEPTH) ** -0.25
LN_EPS = 1e-5
RMS_EPS = 1e-6

SSD_D_INNER = 2 * D_MODEL
SSD_HEAD_DIM = 64
SSD_N_HEADS = SSD_D_INNER // SSD_HEAD_DIM
SSD_N_GROUPS = 8
SSD_D_STATE = 128
SSD_CONV = 4
SSD_CHUNK = 128
SSD_CONV_DIM = SSD_D_INNER + 2 * SSD_N_GROUPS * SSD_D_STATE
SSD_PROJ = SSD_D_INNER + SSD_CONV_DIM + SSD_N_HEADS

MLA_N_HEADS = D_MODEL // 128
MLA_Q_RANK = 768
MLA_KV_RANK = 512
MLA_NOPE = 128
MLA_ROPE = 64
MLA_V = 128
MLA_GATE = MLA_N_HEADS * MLA_V
MLA_PROJ = MLA_Q_RANK + MLA_KV_RANK + MLA_ROPE + MLA_GATE
MLA_Q_BLOCK = 128
ROPE_THETA = 10000.0

GDN_N_QK_HEADS = 16
GDN_N_V_HEADS = 32
GDN_DK = 128
GDN_DV = 128
GDN_KEY_DIM = GDN_N_QK_HEADS * GDN_DK
GDN_VAL_DIM = GDN_N_V_HEADS * GDN_DV
GDN_CONV = 4
GDN_CHUNK = 64
GDN_CONV_DIM = 2 * GDN_KEY_DIM + GDN_VAL_DIM
GDN_PROJ = GDN_CONV_DIM + GDN_VAL_DIM + 2 * GDN_N_V_HEADS

kernel_name = "hybrid_ssd_mla_gdn_deepnorm"

def _layernorm(x, g, b):
    xf = x.astype(jnp.float32)
    mu = jnp.mean(xf, -1, keepdims=True)
    var = jnp.mean(jnp.square(xf - mu), -1, keepdims=True)
    return ((xf - mu) * lax.rsqrt(var + LN_EPS) * g + b).astype(x.dtype)

def _rmsnorm(x, w):
    xf = x.astype(jnp.float32)
    return (xf * lax.rsqrt(jnp.mean(xf * xf, -1, keepdims=True) + RMS_EPS) * w).astype(x.dtype)

def _l2norm(x):
    xf = x.astype(jnp.float32)
    return xf * lax.rsqrt(jnp.sum(xf * xf, -1, keepdims=True) + RMS_EPS)

def _causal_dwconv(x, w):
    K, C = w.shape
    return lax.conv_general_dilated(
        x, w[:, None, :].astype(x.dtype), window_strides=(1,), padding=[(K - 1, 0)],
        dimension_numbers=("NWC", "WIO", "NWC"), feature_group_count=C)

def _rope(x, cos, sin):
    x1, x2 = jnp.split(x, 2, axis=-1)
    return jnp.concatenate([x1 * cos - x2 * sin, x1 * sin + x2 * cos], axis=-1)

def _ssd_mixer(u, in_w, conv_w, conv_b, dt_bias, a_log, d_skip, norm_w, out_w):
    f32 = jnp.float32
    Bsz, S, _ = u.shape
    G, N, H, P, L = SSD_N_GROUPS, SSD_D_STATE, SSD_N_HEADS, SSD_HEAD_DIM, SSD_CHUNK
    R = H // G
    nc = S // L
    proj = u @ in_w
    z, xbc, dt = jnp.split(proj, [SSD_D_INNER, SSD_D_INNER + SSD_CONV_DIM], axis=-1)
    xbc = jax.nn.silu(_causal_dwconv(xbc, conv_w) + conv_b)
    xs, Bm, Cm = jnp.split(xbc, [SSD_D_INNER, SSD_D_INNER + G * N], axis=-1)
    dt = jax.nn.softplus(dt.astype(f32) + dt_bias.astype(f32))
    A = -jnp.exp(a_log.astype(f32)).reshape(G, R)
    x_c = xs.astype(f32).reshape(Bsz, nc, L, G, R, P)
    B_c = Bm.astype(f32).reshape(Bsz, nc, L, G, N)
    C_c = Cm.astype(f32).reshape(Bsz, nc, L, G, N)
    dt_c = dt.reshape(Bsz, nc, L, G, R)
    xdt = x_c * dt_c[..., None]
    a_cs = jnp.moveaxis(jnp.cumsum(dt_c * A, axis=2), 2, -1)
    causal = jnp.tril(jnp.ones((L, L), dtype=bool))
    decay = jnp.exp(jnp.where(causal, a_cs[..., :, None] - a_cs[..., None, :], -jnp.inf))
    cb = jnp.einsum("bclgn,bcsgn->bcgls", C_c, B_c)
    y_diag = jnp.einsum("bcgrls,bcsgrp->bclgrp", cb[:, :, :, None] * decay, xdt)
    decay_states = jnp.moveaxis(jnp.exp(a_cs[..., -1:] - a_cs), -1, 2)
    states = jnp.einsum("bcsgn,bcsgrp->bcgrpn", B_c, xdt * decay_states[..., None])
    chunk_decay = jnp.exp(a_cs[..., -1])

    def step(h, inp):
        st, dec = inp
        return h * dec[..., None, None] + st, h

    h0 = jnp.zeros((Bsz, G, R, P, N), f32)
    _, prev = lax.scan(step, h0, (jnp.moveaxis(states, 1, 0), jnp.moveaxis(chunk_decay, 1, 0)))
    prev = jnp.moveaxis(prev, 0, 1)
    decay_out = jnp.moveaxis(jnp.exp(a_cs), -1, 2)
    y_off = jnp.einsum("bclgn,bcgrpn->bclgrp", C_c, prev) * decay_out[..., None]
    y = y_diag + y_off + x_c * d_skip.astype(f32).reshape(G, R)[..., None]
    gs = SSD_D_INNER // G
    yg = y.reshape(Bsz, S, G, gs) * jax.nn.silu(z.astype(f32).reshape(Bsz, S, G, gs))
    yg = yg * lax.rsqrt(jnp.mean(yg * yg, -1, keepdims=True) + RMS_EPS) * norm_w.astype(f32).reshape(G, gs)
    return yg.reshape(Bsz, S, SSD_D_INNER).astype(u.dtype) @ out_w

def _mla_mixer(u, positions, in_w, q_norm_w, q_up_w, kv_norm_w, kv_up_w, out_w):
    f32 = jnp.float32
    Bsz, S, _ = u.shape
    H, QB = MLA_N_HEADS, MLA_Q_BLOCK
    nb = S // QB
    proj = u @ in_w
    q_c, kv_c, k_rope, z = jnp.split(
        proj, [MLA_Q_RANK, MLA_Q_RANK + MLA_KV_RANK, MLA_Q_RANK + MLA_KV_RANK + MLA_ROPE], axis=-1)
    q = (_rmsnorm(q_c, q_norm_w) @ q_up_w).astype(f32).reshape(Bsz, S, H, MLA_NOPE + MLA_ROPE)
    kv = (_rmsnorm(kv_c, kv_norm_w) @ kv_up_w).astype(f32).reshape(Bsz, S, H, MLA_NOPE + MLA_V)
    q_nope, q_rope = q[..., :MLA_NOPE], q[..., MLA_NOPE:]
    k_nope, v = kv[..., :MLA_NOPE], kv[..., MLA_NOPE:]
    inv_freq = ROPE_THETA ** (-jnp.arange(0, MLA_ROPE, 2, dtype=f32) / MLA_ROPE)
    ang = positions.astype(f32)[..., None] * inv_freq
    cos, sin = jnp.cos(ang), jnp.sin(ang)
    q_rope = _rope(q_rope, cos[:, :, None], sin[:, :, None])
    k_rope = _rope(k_rope.astype(f32), cos, sin)
    scale = (MLA_NOPE + MLA_ROPE) ** -0.5
    qn_b = q_nope.reshape(Bsz, nb, QB, H, MLA_NOPE).transpose(1, 0, 3, 2, 4)
    qr_b = q_rope.reshape(Bsz, nb, QB, H, MLA_ROPE).transpose(1, 0, 3, 2, 4)
    kpos = jnp.arange(S)

    def attend(args):
        qn, qr, blk = args
        s = (jnp.einsum("bhqd,bkhd->bhqk", qn, k_nope)
             + jnp.einsum("bhqr,bkr->bhqk", qr, k_rope)) * scale
        qpos = blk * QB + jnp.arange(QB)
        s = jnp.where(kpos[None, :] <= qpos[:, None], s, -jnp.inf)
        p = jax.nn.softmax(s, axis=-1)
        return jnp.einsum("bhqk,bkhd->bqhd", p, v)

    o = lax.map(attend, (qn_b, qr_b, jnp.arange(nb)))
    o = o.transpose(1, 0, 2, 3, 4).reshape(Bsz, S, H * MLA_V)
    o = o * jax.nn.silu(z.astype(f32))
    return o.astype(u.dtype) @ out_w

def _chunk_gated_delta(q, k, v, g, beta):
    Bsz, S, H, DK = q.shape
    DV = v.shape[-1]
    L = GDN_CHUNK
    nc = S // L

    def chunks(t):
        return jnp.swapaxes(t.reshape(Bsz, nc, L, H, *t.shape[3:]), 2, 3)

    q, k, v, g, beta = chunks(q), chunks(k), chunks(v), chunks(g), chunks(beta)
    g_cs = jnp.cumsum(g, axis=-1)
    incl = jnp.tril(jnp.ones((L, L), dtype=bool))
    strict = jnp.tril(jnp.ones((L, L), dtype=bool), -1)
    decay = jnp.exp(jnp.where(incl, g_cs[..., :, None] - g_cs[..., None, :], -jnp.inf))
    k_beta = k * beta[..., None]
    v_beta = v * beta[..., None]
    a_mat = jnp.where(strict, jnp.einsum("bchld,bchsd->bchls", k_beta, k) * decay, 0.0)
    eye = jnp.eye(L, dtype=q.dtype)
    rhs = jnp.concatenate([v_beta, k_beta * jnp.exp(g_cs)[..., None]], axis=-1)
    sol = lax.linalg.triangular_solve(eye + a_mat, rhs, left_side=True, lower=True, unit_diagonal=True)
    u_val, w_dec = sol[..., :DV], sol[..., DV:]
    qk = jnp.where(incl, jnp.einsum("bchld,bchsd->bchls", q, k) * decay, 0.0)
    q_dec = q * jnp.exp(g_cs)[..., None]
    g_last = g_cs[..., -1]
    k_dec = k * jnp.exp(g_last[..., None] - g_cs)[..., None]

    def step(state, inp):
        qk_c, q_dec_c, u_c, w_c, k_dec_c, gl_c = inp
        v_new = u_c - jnp.einsum("bhld,bhdv->bhlv", w_c, state)
        o_c = jnp.einsum("bhld,bhdv->bhlv", q_dec_c, state) + jnp.einsum("bhls,bhsv->bhlv", qk_c, v_new)
        state = state * jnp.exp(gl_c)[..., None, None] + jnp.einsum("bhld,bhlv->bhdv", k_dec_c, v_new)
        return state, o_c

    xs = tuple(jnp.moveaxis(t, 1, 0) for t in (qk, q_dec, u_val, w_dec, k_dec, g_last))
    _, o = lax.scan(step, jnp.zeros((Bsz, H, DK, DV), q.dtype), xs)
    o = jnp.swapaxes(jnp.moveaxis(o, 0, 1), 2, 3)
    return o.reshape(Bsz, S, H, DV)

def _gdn_mixer(u, in_w, conv_w, a_log, dt_bias, norm_w, out_w):
    f32 = jnp.float32
    Bsz, S, _ = u.shape
    HK, HV, DK, DV = GDN_N_QK_HEADS, GDN_N_V_HEADS, GDN_DK, GDN_DV
    proj = u @ in_w
    qkv, z, b, a = jnp.split(
        proj, [GDN_CONV_DIM, GDN_CONV_DIM + GDN_VAL_DIM, GDN_CONV_DIM + GDN_VAL_DIM + HV], axis=-1)
    qkv = jax.nn.silu(_causal_dwconv(qkv, conv_w))
    q, k, v = jnp.split(qkv, [GDN_KEY_DIM, 2 * GDN_KEY_DIM], axis=-1)
    rep = HV // HK
    q = jnp.repeat(_l2norm(q.reshape(Bsz, S, HK, DK)), rep, axis=2) * (DK ** -0.5)
    k = jnp.repeat(_l2norm(k.reshape(Bsz, S, HK, DK)), rep, axis=2)
    v = v.astype(f32).reshape(Bsz, S, HV, DV)
    beta = jax.nn.sigmoid(b.astype(f32))
    g = -jnp.exp(a_log.astype(f32)) * jax.nn.softplus(a.astype(f32) + dt_bias.astype(f32))
    o = _chunk_gated_delta(q, k, v, g, beta)
    o = _rmsnorm(o, norm_w) * jax.nn.silu(z.astype(f32).reshape(Bsz, S, HV, DV))
    return o.reshape(Bsz, S, GDN_VAL_DIM).astype(u.dtype) @ out_w

def _dt_bias(key, shape):
    dt = jnp.exp(jax.random.uniform(key, shape, jnp.float32, math.log(1e-3), math.log(1e-1)))
    return dt + jnp.log(-jnp.expm1(-dt))

def setup_inputs(seed: int = 0) -> dict:
    key = jax.random.key(seed)
    ks = jax.random.split(key, 32)
    f32 = jnp.float32

    def nrm(k, shape, scale):
        return jax.random.normal(k, shape, f32) * scale

    def gain(k, shape):
        return 1.0 + 0.02 * jax.random.normal(k, shape, f32)

    nA, nB, nC = N_SSD_LAYERS, N_MLA_LAYERS, N_GDN_LAYERS
    x = jax.random.normal(ks[0], (BATCH, SEQ, D_MODEL), f32)
    offset = jax.random.randint(ks[1], (BATCH, 1), 0, 1024, dtype=jnp.int32)
    positions = offset + jnp.arange(SEQ, dtype=jnp.int32)[None, :]
    return {
        "x": x,
        "positions": positions,
        "ssd_in_w": nrm(ks[2], (nA, D_MODEL, SSD_PROJ), D_MODEL ** -0.5),
        "ssd_conv_w": nrm(ks[3], (nA, SSD_CONV, SSD_CONV_DIM), SSD_CONV ** -0.5),
        "ssd_conv_b": nrm(ks[4], (nA, SSD_CONV_DIM), 0.02),
        "ssd_dt_bias": _dt_bias(ks[5], (nA, SSD_N_HEADS)),
        "ssd_a_log": jnp.log(jax.random.uniform(ks[6], (nA, SSD_N_HEADS), f32, 1.0, 16.0)),
        "ssd_d": gain(ks[7], (nA, SSD_N_HEADS)),
        "ssd_norm_w": gain(ks[8], (nA, SSD_D_INNER)),
        "ssd_out_w": nrm(ks[9], (nA, SSD_D_INNER, D_MODEL), SSD_D_INNER ** -0.5 * DEEPNORM_BETA),
        "mla_in_w": nrm(ks[10], (nB, D_MODEL, MLA_PROJ), D_MODEL ** -0.5),
        "mla_q_norm_w": gain(ks[11], (nB, MLA_Q_RANK)),
        "mla_q_up_w": nrm(ks[12], (nB, MLA_Q_RANK, MLA_N_HEADS * (MLA_NOPE + MLA_ROPE)), MLA_Q_RANK ** -0.5),
        "mla_kv_norm_w": gain(ks[13], (nB, MLA_KV_RANK)),
        "mla_kv_up_w": nrm(ks[14], (nB, MLA_KV_RANK, MLA_N_HEADS * (MLA_NOPE + MLA_V)), MLA_KV_RANK ** -0.5),
        "mla_out_w": nrm(ks[15], (nB, MLA_N_HEADS * MLA_V, D_MODEL), (MLA_N_HEADS * MLA_V) ** -0.5 * DEEPNORM_BETA),
        "gdn_in_w": nrm(ks[16], (nC, D_MODEL, GDN_PROJ), D_MODEL ** -0.5),
        "gdn_conv_w": nrm(ks[17], (nC, GDN_CONV, GDN_CONV_DIM), GDN_CONV ** -0.5),
        "gdn_a_log": jnp.log(jax.random.uniform(ks[18], (nC, GDN_N_V_HEADS), f32, 1.0, 16.0)),
        "gdn_dt_bias": _dt_bias(ks[19], (nC, GDN_N_V_HEADS)),
        "gdn_norm_w": gain(ks[20], (nC, GDN_DV)),
        "gdn_out_w": nrm(ks[21], (nC, GDN_VAL_DIM, D_MODEL), GDN_VAL_DIM ** -0.5 * DEEPNORM_BETA),
        "ln_g": gain(ks[22], (DEPTH, D_MODEL)),
        "ln_b": nrm(ks[23], (DEPTH, D_MODEL), 0.02),
    }

def reference(x, positions, ssd_in_w, ssd_conv_w, ssd_conv_b, ssd_dt_bias, ssd_a_log, ssd_d,
              ssd_norm_w, ssd_out_w, mla_in_w, mla_q_norm_w, mla_q_up_w, mla_kv_norm_w, mla_kv_up_w,
              mla_out_w, gdn_in_w, gdn_conv_w, gdn_a_log, gdn_dt_bias, gdn_norm_w, gdn_out_w, ln_g, ln_b):
    h = x
    for i in range(DEPTH):
        kind, j = i % N_MIXERS, i // N_MIXERS
        if kind == 0:
            y = _ssd_mixer(h, ssd_in_w[j], ssd_conv_w[j], ssd_conv_b[j], ssd_dt_bias[j], ssd_a_log[j],
                           ssd_d[j], ssd_norm_w[j], ssd_out_w[j])
        elif kind == 1:
            y = _mla_mixer(h, positions, mla_in_w[j], mla_q_norm_w[j], mla_q_up_w[j], mla_kv_norm_w[j],
                           mla_kv_up_w[j], mla_out_w[j])
        else:
            y = _gdn_mixer(h, gdn_in_w[j], gdn_conv_w[j], gdn_a_log[j], gdn_dt_bias[j], gdn_norm_w[j],
                           gdn_out_w[j])
        h = _layernorm(DEEPNORM_ALPHA * h + y.astype(h.dtype), ln_g[i], ln_b[i])
    return h


_drawn_inputs = setup_inputs


def setup_inputs(seed=0):
    import zlib

    import numpy as np

    out = dict(_drawn_inputs(seed))
    spreads = {}
    factors = {'ssd_conv_b': 5.835,
     'ssd_d': 8.0,
     'ssd_norm_w': 8.0,
     'mla_q_norm_w': 8.0,
     'mla_kv_norm_w': 8.0,
     'gdn_norm_w': 22.788}
    for name, (base, spread) in spreads.items():
        noise = np.random.default_rng([zlib.crc32(name.encode()), seed]).standard_normal(out[name].shape)
        drawn = base * np.exp(spread * noise) if base else spread * noise
        out[name] = __import__('jax').numpy.asarray(drawn.astype(out[name].dtype))
    for name, factor in factors.items():
        out[name] = (out[name] * factor).astype(out[name].dtype)
    return out
```

```python
from contextlib import contextmanager, ExitStack

import numpy as np
import concourse.bass as bass
from concourse import mybir

F32 = mybir.dt.float32
I32 = mybir.dt.int32
ALU = mybir.AluOpType
ACT = mybir.ActivationFunctionType
AX = mybir.AxisListType
ds = bass.ds

P = 128
T = 256
D = 2048
KD = D // P
DEPTH = 4
ALPHA = (2.0 * DEPTH) ** 0.25
LN_EPS, RMS_EPS = 1e-5, 1e-6
KINDS = ["ssd", "mla", "gdn", "ssd"]

SSD_IN, SSD_HEADS, SSD_GROUPS = 4096, 64, 8
SSD_R = SSD_HEADS // SSD_GROUPS
SSD_CONV_DIM = SSD_IN + 2 * SSD_GROUPS * P
SSD_COL_X = SSD_IN
SSD_COL_B = SSD_COL_X + SSD_IN
SSD_COL_C = SSD_COL_B + SSD_GROUPS * P
SSD_COL_DT = SSD_COL_C + SSD_GROUPS * P
SSD_XT = SSD_IN // P
SSD_TILES = 10

MLA_H, MLA_QR, MLA_KVR, MLA_ROPE = 16, 768, 512, 64
MLA_QT, MLA_KVT = MLA_QR // P, MLA_KVR // P
MLA_COL_KR = MLA_QR + MLA_KVR
MLA_COL_Z = MLA_COL_KR + MLA_ROPE
MLA_SCALE = (128 + MLA_ROPE) ** -0.5

GDN_HK, GDN_HV = 16, 32
GDN_COL_K, GDN_COL_V, GDN_COL_Z = 2048, 4096, 8192
GDN_COL_B = 12288
GDN_TILES = 6
LEVELS = (2, 4, 8, 16, 32)

SLOTS, SLOT = 10, 2048
NEG = -1.0e30
MAGIC = 1.5 * 2.0 ** 23
TWO_PI_A = 6.28125
TWO_PI_B = float(np.float32(np.round((2 * np.pi - TWO_PI_A) * 2 ** 21) / 2 ** 21))
TWO_PI_C = float(np.float32(2 * np.pi - TWO_PI_A - TWO_PI_B))

CONST = ["ident", "ones", "tri128", "tri64", "blk64", "neg128", "neg64", "negq", "rot",
         "lev1", "lev2", "lev4", "lev8", "lev16", "lev32"]


def constants():
    r, c = np.arange(P)[:, None], np.arange(P)[None, :]
    same64 = r // 64 == c // 64
    m = {
        "ident": r == c,
        "ones": np.ones((P, P)),
        "tri128": r <= c,
        "tri64": (r <= c) & same64,
        "blk64": same64,
        "neg128": np.where(r <= c, 0.0, NEG),
        "neg64": np.where((r <= c) & same64, 0.0, NEG),
        "negq": np.where(c <= r, 0.0, NEG),
        "rot": np.where((c % 64 < 32) & (r == c + 32), -1.0, 0.0) + np.where((c % 64 >= 32) & (r == c - 32), 1.0, 0.0),
    }
    for b in (1,) + LEVELS:
        m[f"lev{b}"] = (r // (2 * b) == c // (2 * b)) & (c // b % 2 == 1) & (r // b % 2 == 0)
    inv = (10000.0 ** (-np.arange(0, MLA_ROPE, 2, dtype=np.float64) / MLA_ROPE)).astype(np.float32)
    cols = [np.asarray(m[n], np.float32) for n in CONST] + [np.tile(inv, 4)[:, None]]
    return np.ascontiguousarray(np.concatenate(cols, axis=1).astype(np.float32))


class Count:

    def __init__(self):
        self.n, self.turn, self.step = 0, 0, 0

    def next(self, by=1):
        self.n += by
        return self.n + self.turn * self.step if self.step else self.n


@contextmanager
def rolled(eng, start, end, steps):
    with eng.Fori(start, end) as i:
        at = [(c, c.n) for c, _ in steps]
        for c, by in steps:
            c.turn, c.step = i - start, by
        yield i
    for (c, n0), (_, by) in zip(at, steps):
        assert c.n - n0 == by, (c.n - n0, by)
        c.n, c.turn, c.step = n0 + by * (end - start), 0, 0


def build(nc, a, layers=range(DEPTH)):
    layers = list(layers)
    with ExitStack() as ctx:
        _program(nc, a, layers, ctx)


def _program(nc, a, layers, ctx):
    def sb(name, shape, dt=F32):
        return ctx.enter_context(nc.sbuf_tensor(name, shape, dt))

    def sem(name):
        return ctx.enter_context(nc.semaphore(name))

    H = sb("H", [P, KD, T])
    Y = sb("Y", [P, 32, T])
    ring = sb("ring", [P, SLOTS, SLOT])
    cst = sb("cst", [P, len(CONST) * P + 1])
    arena = sb("arena", [P, 12400])
    params = sb("params", [P, 10, P])
    hd = sb("hd", [P, 16 + 2 * 32])
    posi = sb("posi", [P, T], I32)
    banks = [ctx.enter_context(nc.psum_tensor(f"bank{i}", [P, 512], F32)) for i in range(8)]
    C = {n: cst[:, P * i:P * (i + 1)] for i, n in enumerate(CONST)}
    inv_freq = cst[:, len(CONST) * P:len(CONST) * P + 1]
    ident = C["ident"]

    def carve(*shapes, base=0):
        at, out = base, []
        for s in shapes:
            n = int(np.prod(s))
            v = arena[:, at:at + n]
            if len(s) == 2:
                v = v.rearrange("p (a b) -> p a b", a=s[0])
            if len(s) == 3:
                v = v.rearrange("p (a b c) -> p a b c", a=s[0], b=s[1])
            out.append(v)
            at += n
        assert at <= 12400, at
        return out

    def slot(p, k=KD):
        return ring[:, p, :].rearrange("p (k c) -> p k c", k=k)

    bank = [b[:] for b in banks]
    pj = [bank[0][:, 0:T], bank[1][:, 0:T]]

    def as3(ap, a):
        return ap.rearrange("p (a b) -> p a b", a=a)

    landed = [sem(f"landed{p}") for p in range(SLOTS)]
    unit_done = sem("unit_done")
    dve_step, act_step = sem("dve_step"), sem("act_step")
    class Events(dict):

        def __missing__(self, name):
            self[name] = sem(name)
            return self[name]

    E = Events()

    first_unit, layer_no, nth_ssd = {}, {}, {}
    at = 0
    for n, l in enumerate(layers):
        kind = KINDS[l]
        layer_no[l] = n
        nth_ssd[l] = sum(KINDS[x] == "ssd" for x in layers[:n])
        first_unit[l] = at
        at += {"ssd": 1 + SSD_TILES * SSD_GROUPS, "mla": 11 + 16 + 3 * 8, "gdn": 1 + GDN_TILES * GDN_HK}[kind]
        first_unit[l, "out"] = at
        at += 16 if kind == "mla" else 32

    def w_tile(w, col, width=P, k0=0):
        return w.rearrange("(k p) n -> p k n", p=P)[:, k0:k0 + KD, ds(col, width)]

    ssd = {}
    (ssd["conv"], ssd["B"], ssd["C"], ssd["X"], ssd["Z"], ssd["xdt"], ssd["xds"], ssd["btok"], ssd["rows"],
     ssd["D"], ssd["E"], ssd["st"], ssd["YG"], ssd["rstd"], ssd["tok"], ssd["acol"], ssd["dst"]) = carve(
        (2, T), (T,), (T,), (4, T), (4, T), (2, 512), (512,), (P,), (SSD_R, T),
        (2, SSD_R, P), (SSD_R, P), (512,), (4, T), (T,), (4, 64), (2, 64), (64,))
    ssd["SQ"] = ssd["E"].rearrange("p r t -> p (r t)").rearrange("p (a b) -> p a b", a=4)
    dtv = [ssd["YG"][0:64, i, :] for i in range(4)] + [ssd["xdt"][0:64, 0, 0:T], ssd["xdt"][0:64, 0, T:2 * T],
                                                      ssd["xdt"][0:64, 1, 0:T], ssd["xdt"][0:64, 1, T:2 * T]]
    ln = {}
    ln["pre"], ln["sum"], ln["mean"], ln["rstd"], ln["sq"] = carve((KD, T), (T,), (T,), (T,), (2, T))
    xrows = arena[:, 0:2 * D].rearrange("p (c n) -> p c n", c=2)
    prows = Y[:, 0:5, :].rearrange("p a (b c) -> p (a b) c", b=2)
    dskip_rows = Y[:, 5, 0:P].rearrange("p (n h) -> p n h", n=2)

    y_base, yb = {}, 0
    for l in layers:
        y_base[l] = yb
        yb += 32 if KINDS[l] == "ssd" else 0

    PCOL = {}
    for n, l in enumerate((0, 3)):
        for tap in range(4):
            PCOL[l, f"tap{tap}"] = (3 * n + tap // 2) * P + 48 * (tap % 2)
        PCOL[l, "g"], PCOL[l, "b"] = 3 * n * P + 96, 3 * n * P + 112
        PCOL[l, "norm"], PCOL[l, "cb"] = (3 * n + 1) * P + 96, (3 * n + 2) * P
    for tap in range(4):
        PCOL[2, f"tap{tap}"] = (6 + tap // 2) * P + 64 * (tap % 2)
    PCOL[2, "g"], PCOL[2, "b"], PCOL[2, "norm"] = 8 * P, 8 * P + 16, 8 * P + 32
    PCOL[1, "qn"], PCOL[1, "kvn"], PCOL[1, "g"], PCOL[1, "b"] = 9 * P, 9 * P + 6, 9 * P + 10, 9 * P + 26
    PROWS = [128, 128, 48, 128, 128, 48, 128, 128, 33, 42]

    def pcol(l, name, idx):
        flat = params[:].rearrange("p a b -> p (a b)")
        return flat[:, ds(PCOL[l, name] + idx, 1)]


    def rows128(ap):
        return ap.rearrange("(r c) -> r c", c=P)

    PRM_DMAS = []
    for n, l in enumerate((0, 3)):
        for tap in range(4):
            r0 = 48 * (tap % 2)
            PRM_DMAS.append((prows[r0:r0 + 48, 3 * n + tap // 2, :], rows128(a["ssd_conv_w"][n, tap])))
        PRM_DMAS += [(prows[96:112, 3 * n, :], rows128(a["ln_g"][l])), (prows[112:128, 3 * n, :], rows128(a["ln_b"][l])),
                     (prows[96:128, 3 * n + 1, :], rows128(a["ssd_norm_w"][n])),
                     (prows[0:48, 3 * n + 2, :], rows128(a["ssd_conv_b"][n]))]
    for tap in range(4):
        r0 = 64 * (tap % 2)
        PRM_DMAS.append((prows[r0:r0 + 64, 6 + tap // 2, :], rows128(a["gdn_conv_w"][0, tap])))
    PRM_DMAS += [(prows[0:16, 8, :], rows128(a["ln_g"][2])), (prows[16:32, 8, :], rows128(a["ln_b"][2])),
                 (prows[32:33, 8, :], a["gdn_norm_w"]),
                 (prows[0:6, 9, :], rows128(a["mla_q_norm_w"][0])), (prows[6:10, 9, :], rows128(a["mla_kv_norm_w"][0])),
                 (prows[10:26, 9, :], rows128(a["ln_g"][1])), (prows[26:42, 9, :], rows128(a["ln_b"][1]))]
    N_PRM_DMA = len(PRM_DMAS)

    def column(ap):
        return ap.rearrange("(h o) -> h o", o=1)

    HEAD_DMAS = []
    for n in range(2):
        HEAD_DMAS += [(hd[0:64, 4 * n:4 * n + 1], column(a["ssd_dt_bias"][n])),
                      (hd[0:64, 4 * n + 1:4 * n + 2], column(a["ssd_a_log"][n])),
                      (dskip_rows[:, n, :], a["ssd_d"][n].partition_broadcast(P))]
    HEAD_DMAS += [(hd[32:64, 8:9], column(a["gdn_dt_bias"][0])), (hd[32:64, 9:10], column(a["gdn_a_log"][0])),
                  (posi[:], a["positions"][0].partition_broadcast(P))]
    N_HEAD_DMA = len(HEAD_DMAS)

    def load_ssd(sp, l, load, single, turns_of):
        w, ns = a["ssd_in_w"][l // 3], nth_ssd[l]
        scr = a["scr_ssd"][ns]
        single(9, w_tile(w, SSD_COL_DT, 64))

        def rows_of(g):
            G = g + ns * SSD_GROUPS
            row = g * SSD_R if isinstance(g, int) else sp.snap(g * SSD_R)
            if not (isinstance(G, int) and G == 0):
                sp.wait_ge(unit_done, 1)
                sp.wait_ge(E["diff_ready"], G)
                sp.wait_ge(E["e_exp"], G)
            sp.dma_start(ssd["rows"], scr[ds(row, SSD_R), :].partition_broadcast(P)).then_inc(E["rows_in"], 16)

        def body(g, free):
            cols = [SSD_COL_B + g * P, SSD_COL_C + g * P] + [SSD_COL_X + g * 512 + t * P for t in range(4)] \
                + [g * 512 + t * P for t in range(4)]
            if not isinstance(g, int):
                free[5] = free[6] = sp.snap(free[6])
            for p in range(SSD_TILES):
                load(p, w_tile(w, cols[p] if isinstance(g, int) else sp.snap(cols[p])), free[p])
                if p == 6 and not isinstance(g, int):
                    rows_of(g)
            if isinstance(g, int):
                sp.wait_ge(E["acs_ready"], ns + 1)
                sp.dma_start(scr, dtv[7]).then_inc(E["scr_out"], 16)
                sp.wait_ge(E["scr_out"], 16 * (ns + 1))
                rows_of(0)
        turns_of(body, SSD_TILES, SSD_GROUPS)

    def y_ready_at(l, h):
        if KINDS[l] == "mla":
            return E["o_ready"], 16
        if KINDS[l] == "gdn":
            return E["gy_ready"], 8 * (h + 1) + 1
        return E["y_ready"], y_base[l] + 16 * (h + 1)

    def pe_ssd(pe, l, take, taken, tile, hidden, first_hidden):
        ns = nth_ssd[l]
        S = ssd

        def body(g):
            G = g + ns * SSD_GROUPS
            head = isinstance(g, int)

            def proj(p):
                take(p)
                if p in (0, 1):
                    if not head:
                        pe.wait_ge(E["z_ready"], G * 4)
                    if head and p == 1:
                        pe.wait_ge(E["dt_x"], ns + 1)
                elif p < 8:
                    pe.wait_ge(E["conv_ready"], G * 6 + p - 1)
                else:
                    pe.wait_ge(E["z_ready"], G * 4 + p - 7)
                tile(p, pj[p % 2], hidden)

            proj(0)
            if not head:
                for i in range(4):
                    pe.wait_ge(E["sq_ready"], (G - 1) * 4 + i + 1)
                    mm = nc.tensor.matmul(bank[7][:, 0:T], C["ones"], S["SQ"][:, i, :], start=i == 0, stop=i == 3)
                mm.then_inc(E["stat_done"], 1)
            proj(1)
            if head:
                pe.wait_ge(E["dt_a"], ns + 1)
                for j in range(4):
                    src = (dtv[5] if j < 2 else dtv[6])[:, j % 2 * P:(j % 2 + 1) * P]
                    mm = nc.tensor.transpose(bank[2][:, j * 64:(j + 1) * 64], src, ident[0:64, 0:64])
                mm.then_inc(E["dt_t"], 1)
            proj(2)
            if head:
                pe.wait_ge(E["dt_tok"], ns + 1)
                for c in range(2):
                    nc.tensor.matmul(bank[3][0:64, c * P:(c + 1) * P], S["tok"][:, 2 + c, :], C["tri128"],
                                     start=True, stop=True)
                nc.tensor.matmul(bank[4][:, 0:P], C["tri128"], S["tok"][:, 2:4, :], start=True, stop=True)
                nc.tensor.matmul(bank[4][:, P:P + 64], C["ones"], S["tok"][:, 2, :], start=True, stop=True
                                 ).then_inc(E["cum_done"], 1)
            proj(3)
            proj(4)
            pe.wait_ge(E["conv_silu"], G * 6 + 2)
            if head:
                pe.wait_ge(E["acs_ready"], ns + 1)
            for c in range(2):
                mm = nc.tensor.matmul(bank[6][:, c * P:(c + 1) * P], S["B"][:, c * P:(c + 1) * P],
                                      S["C"][:, c * P:(c + 1) * P], start=True, stop=True)
            mm.then_inc(E["cb_done"], 1)
            proj(5)
            proj(6)
            pe.wait_ge(E["conv_silu"], G * 6 + 6)
            for c in range(2):
                for t in range(4):
                    mm = nc.tensor.transpose(bank[2 + c][:, t * P:(t + 1) * P], S["X"][:, t, c * P:(c + 1) * P], ident)
                mm.then_inc(E["tx_done"], 1)
            if not head:
                pe.wait_ge(E["rstd_ready"], G)
            nc.tensor.transpose(bank[7][:, 0:P], S["B"][:, 0:P], ident).then_inc(E["bt_done"], 1)
            proj(7)
            pe.wait_ge(E["btok_ready"], G + 1)
            pe.wait_ge(E["xds_ready"], G + 1)
            nc.tensor.matmul(bank[7], S["btok"], S["xds"], start=True, stop=True).then_inc(E["st_done"], 1)
            pe.wait_ge(E["m_ready"], G * 2 + 1)
            for r in range(SSD_R):
                o = bank[4 + r // 4][64 * (r % 2):64 * (r % 2) + 64, r // 2 % 2 * T:r // 2 % 2 * T + P]
                nc.tensor.matmul(o, S["xdt"][:, 0, r * 64:(r + 1) * 64], S["D"][:, 0, r, :], start=True, stop=True)
            proj(8)
            pe.wait_ge(E["m_ready"], G * 2 + 2)
            pe.wait_ge(E["cdec_ready"], G + 1)
            pe.wait_ge(E["st_ready"], G + 1)
            for r in range(SSD_R):
                o = bank[4 + r // 4][64 * (r % 2):64 * (r % 2) + 64, r // 2 % 2 * T + P:r // 2 % 2 * T + 2 * P]
                nc.tensor.matmul(o, S["xdt"][:, 1, r * 64:(r + 1) * 64], S["D"][:, 1, r, :], start=True, stop=False)
                mm = nc.tensor.matmul(o, S["st"][:, r * 64:(r + 1) * 64], S["E"][:, r, :], start=False, stop=True)
            mm.then_inc(E["y_done"], 1)
            proj(9)

        take(9)
        fh = first_hidden(l)
        tile(9, pj[1][0:64], hidden, width=64, waits=fh)
        body(0)
        with rolled(pe, 1, SSD_GROUPS, [(taken[p], 16) for p in range(SSD_TILES)]) as g:
            body(g)
        G = ns * SSD_GROUPS + SSD_GROUPS
        for i in range(4):
            pe.wait_ge(E["sq_ready"], (G - 1) * 4 + i + 1)
            mm = nc.tensor.matmul(bank[7][:, 0:T], C["ones"], S["SQ"][:, i, :], start=i == 0, stop=i == 3)
        mm.then_inc(E["stat_done"], 1)

    def conv(dve, link, src, dst, l, tile_no):
        link(nc.vector.tensor_scalar(dst, src, pcol(l, "tap3", tile_no), None, ALU.mult))
        for s in (1, 2, 3):
            ins = nc.vector.scalar_tensor_tensor(out=dst[:, s:T], in0=src[:, 0:T - s],
                                                 scalar=pcol(l, f"tap{3 - s}", tile_no), in1=dst[:, s:T],
                                                 op0=ALU.mult, op1=ALU.add)
            if s < 3:
                link(ins)
        return ins

    def dve_ssd(dve, l, link, step):
        ns, S = nth_ssd[l], ssd
        U = first_unit[l]
        raw, absx, ex, w1, lnw, dt, da, arow = dtv
        hcol = hd[0:64, 4 * (l // 3):4 * (l // 3) + 3]
        dve.wait_ge(unit_done, U + 1)
        nc.vector.tensor_scalar(raw, pj[1][0:64], hcol[:, 0:1], None, ALU.add).then_inc(E["dt_x"], 1)
        dve.wait_ge(E["dt_exp"], ns + 1)
        nc.vector.tensor_scalar(w1, ex, 1.0, None, ALU.add).then_inc(E["dt_w"], 1)
        dve.wait_ge(E["dt_w"], ns + 1)
        link(nc.vector.tensor_scalar(dt, w1, 1.0, 0.0, ALU.subtract, ALU.is_equal))
        link(nc.vector.scalar_tensor_tensor(out=da, in0=w1, scalar=-1.0, in1=dt, op0=ALU.add, op1=ALU.add))
        link(nc.vector.reciprocal(da, da))
        link(nc.vector.tensor_tensor(da, da, ex, ALU.mult))
        dve.wait_ge(E["dt_ln"], ns + 1)
        link(nc.vector.tensor_tensor(dt, dt, lnw, ALU.add))
        link(nc.vector.tensor_tensor(da, da, dt, ALU.mult))
        link(nc.vector.scalar_tensor_tensor(out=dt, in0=raw, scalar=0.0, in1=da, op0=ALU.max, op1=ALU.add))
        nc.vector.tensor_scalar(da, dt, hcol[:, 2:3], -1.0, ALU.mult, ALU.mult).then_inc(E["dt_a"], 1)

        def body(g):
            G = g + ns * SSD_GROUPS
            head = isinstance(g, int)

            def conv_of(k, tile_no):
                dve.wait_ge(unit_done, U + 2 + g * SSD_TILES + k)
                if not (isinstance(G, int) and G == 0 and k < 2):
                    dve.wait_ge(E["conv_silu"], G * 6 + k - 1)
                conv(dve, link, pj[k % 2], S["conv"][:, k % 2, :], l, tile_no).then_inc(E["conv_ready"], 1)
            conv_of(0, SSD_XT + g)
            if head:
                dve.wait_ge(E["dt_t"], ns + 1)
                nc.vector.tensor_copy(S["tok"], as3(bank[2][:, 0:256], 4)).then_inc(E["dt_tok"], 1)
            conv_of(1, SSD_XT + SSD_GROUPS + g)
            if head:
                dve.wait_ge(E["cum_done"], ns + 1)
                link(nc.vector.tensor_copy(S["acol"], as3(bank[4][:, 0:P], 2)))
                nc.vector.tensor_tensor(S["dst"], bank[4][:, P:P + 64], S["acol"][:, 0, :], ALU.subtract
                                        ).then_inc(E["dst_pre"], 1)
                nc.vector.tensor_copy(arow, bank[3][0:64, 0:T]).then_inc(E["acs_ready"], 1)
                dve.wait_ge(E["acs_ready"], ns + 1)
            conv_of(2, g * 4)
            conv_of(3, g * 4 + 1)
            dve.wait_ge(E["rows_in"], (G + 1) * 16)
            for c in range(2):
                for r in range(SSD_R):
                    ins = nc.vector.scalar_tensor_tensor(
                        out=S["D"][:, c, r, :], in0=S["rows"][:, r, c * P:(c + 1) * P],
                        scalar=S["acol"][:, c, ds(g * SSD_R + r, 1)], in1=C["neg128"], op0=ALU.subtract, op1=ALU.min)
            ins.then_inc(E["diff_ready"], 1)
            if not head:
                ssd_norm(G, g)
            conv_of(4, g * 4 + 2)
            conv_of(5, g * 4 + 3)
            dve.wait_ge(E["cb_done"], G + 1)
            for c in range(2):
                dve.wait_ge(E["d_exp"], G * 2 + c + 1)
                cb = bank[6][:, c * P:(c + 1) * P].rearrange("p (o l) -> p o l", o=1).broadcast_to([P, SSD_R, P])
                nc.vector.tensor_tensor(S["D"][:, c], S["D"][:, c], cb, ALU.mult).then_inc(E["m_ready"], 1)
            for c in range(2):
                dve.wait_ge(E["tx_done"], G * 2 + c + 1)
                by = S["tok"][:, c, ds(g * SSD_R, SSD_R)].rearrange("p (r o) -> p r o", o=1).broadcast_to([P, SSD_R, 64])
                nc.vector.tensor_tensor(as3(S["xdt"][:, c, :], SSD_R), as3(bank[2 + c], SSD_R), by, ALU.mult
                                        ).then_inc(E["xdt_ready"], 1)
            dve.wait_ge(E["xdt_ready"], G * 2 + 2)
            if head:
                dve.wait_ge(E["dst_ready"], ns + 1)
            by = S["dst"][:, ds(g * SSD_R, SSD_R)].rearrange("p (r o) -> p r o", o=1).broadcast_to([P, SSD_R, 64])
            nc.vector.tensor_tensor(as3(S["xds"], SSD_R), as3(S["xdt"][:, 0, :], SSD_R), by, ALU.mult
                                    ).then_inc(E["xds_ready"], 1)
            dve.wait_ge(E["y_done"], G + 1)
            for i in range(4):
                link(nc.vector.scalar_tensor_tensor(
                    out=S["YG"][:, i, :], in0=S["X"][:, i, :], scalar=hd[:, ds(16 + 32 * (l // 3) + g * 4 + i, 1)],
                    in1=bank[4 + i // 2][:, i % 2 * T:(i % 2 + 1) * T], op0=ALU.mult, op1=ALU.add))
            for i in range(4):
                dve.wait_ge(E["z_ready"], G * 4 + i + 1)
                nc.vector.tensor_tensor(S["YG"][:, i, :], S["YG"][:, i, :], S["Z"][:, i, :], ALU.mult
                                        ).then_inc(E["yg_ready"], 1)

        def ssd_norm(G, g):
            dve.wait_ge(E["yg_ready"], G * 4)
            dve.wait_ge(E["rstd_ready"], G)
            for i in range(4):
                t = g * 4 - 4 + i
                nc.vector.scalar_tensor_tensor(out=Y[:, t, :], in0=S["YG"][:, i, :], scalar=pcol(l, "norm", t),
                                               in1=S["rstd"], op0=ALU.mult, op1=ALU.mult).then_inc(E["y_ready"], 1)
        body(0)
        with rolled(dve, 1, SSD_GROUPS, [(step, 6 * 3 + 4)]) as g:
            body(g)
        ssd_norm(ns * SSD_GROUPS + SSD_GROUPS, SSD_GROUPS)

    def dve_norm(dve, l, link, step):
        n = layer_no[l]
        U, per = first_unit[l, "out"], (1 if KINDS[l] == "mla" else 2)
        link(nc.vector.memset(ln["sum"], 0.0))

        def body(i):
            for t in range(4):
                dve.wait_ge(unit_done, U + (i * 4 + t + 1) * per)
                nc.vector.scalar_tensor_tensor(out=ln["pre"][:, ds(i * 4 + t, 1), :], in0=H[:, ds(i * 4 + t, 1), :],
                                               scalar=ALPHA, in1=pj[t % 2], op0=ALU.mult, op1=ALU.add
                                               ).then_inc(E["pre_ready"], 1)
                dve.wait_ge(E["pre_ready"], KD * n + i * 4 + t + 1)
                link(nc.vector.tensor_tensor(ln["sum"], ln["sum"], ln["pre"][:, ds(i * 4 + t, 1), :], ALU.add))
        with rolled(dve, 0, 4, [(step, 4)]) as i:
            body(i)
        nc.vector.tensor_scalar(ln["sum"], ln["sum"], 1.0 / D, None, ALU.mult).then_inc(E["sum_ready"], 1)
        dve.wait_ge(E["mean_done"], n + 1)
        for k in range(KD):
            nc.vector.tensor_tensor(ln["pre"][:, k, :], ln["pre"][:, k, :], bank[2][:, 0:T], ALU.subtract
                                    ).then_inc(E["cent_ready"], 1)
        dve.wait_ge(E["cent_ready"], KD * (n + 1))
        dve.wait_ge(E["lrstd_ready"], n + 1)
        for k in range(KD):
            nc.vector.scalar_tensor_tensor(out=ln["pre"][:, k, :], in0=ln["pre"][:, k, :], scalar=pcol(l, "g", k),
                                           in1=ln["rstd"], op0=ALU.mult, op1=ALU.mult).then_inc(E["ln_mul"], 1)

    def act_rstd(act, link, dst, src, scale, eps):
        link(nc.scalar.activation(dst, src, ACT.Ln, bias=eps, scale=scale))
        return nc.scalar.activation(dst, dst, ACT.Exp, scale=-0.5)

    def act_ssd(act, l, link, astep):
        ns, S = nth_ssd[l], ssd
        U = first_unit[l]
        raw, absx, ex, w1, lnw, dt, da, arow = dtv
        act.wait_ge(E["dt_x"], ns + 1)
        link(nc.scalar.activation(absx, raw, ACT.Abs))
        nc.scalar.activation(ex, absx, ACT.Exp, scale=-1.0).then_inc(E["dt_exp"], 1)
        act.wait_ge(E["dt_w"], ns + 1)
        nc.scalar.activation(lnw, w1, ACT.Ln).then_inc(E["dt_ln"], 1)

        def body(g):
            G = g + ns * SSD_GROUPS
            head = isinstance(g, int)

            def silu_of(k, dst, tile_no):
                act.wait_ge(E["conv_ready"], G * 6 + k + 1)
                nc.scalar.activation(dst, S["conv"][:, k % 2, :], ACT.Silu, bias=pcol(l, "cb", tile_no)
                                     ).then_inc(E["conv_silu"], 1)

            def z_of(i):
                act.wait_ge(unit_done, U + 2 + g * SSD_TILES + 6 + i)
                nc.scalar.activation(S["Z"][:, i, :], pj[i % 2], ACT.Silu).then_inc(E["z_ready"], 1)
            silu_of(0, S["B"], SSD_XT + g)
            if not head:
                act.wait_ge(E["cdec_ready"], G)
            silu_of(1, S["C"], SSD_XT + SSD_GROUPS + g)
            silu_of(2, S["X"][:, 0, :], g * 4)
            silu_of(3, S["X"][:, 1, :], g * 4 + 1)
            if head:
                act.wait_ge(E["dst_pre"], ns + 1)
                nc.scalar.activation(S["dst"], S["dst"], ACT.Exp).then_inc(E["dst_ready"], 1)
            else:
                act.wait_ge(E["stat_done"], G)
                act_rstd(act, link, S["rstd"], bank[7][:, 0:T], 1.0 / 512, RMS_EPS).then_inc(E["rstd_ready"], 1)
            act.wait_ge(E["diff_ready"], G + 1)
            for c in range(2):
                nc.scalar.activation(S["D"][:, c], S["D"][:, c], ACT.Exp).then_inc(E["d_exp"], 1)
            nc.scalar.activation(S["E"], S["rows"][:, :, P:T], ACT.Exp).then_inc(E["e_exp"], 1)
            silu_of(4, S["X"][:, 2, :], g * 4 + 2)
            silu_of(5, S["X"][:, 3, :], g * 4 + 3)
            z_of(0)
            act.wait_ge(E["bt_done"], G + 1)
            nc.scalar.activation(S["btok"], bank[7][:, 0:P], ACT.Copy).then_inc(E["btok_ready"], 1)
            z_of(1)
            act.wait_ge(E["st_done"], G + 1)
            nc.scalar.activation(S["st"], bank[7], ACT.Copy).then_inc(E["st_ready"], 1)
            z_of(2)
            z_of(3)
            for i in range(4):
                act.wait_ge(E["yg_ready"], G * 4 + i + 1)
                nc.scalar.activation(S["SQ"][:, i, :], S["YG"][:, i, :], ACT.Square).then_inc(E["sq_ready"], 1)
        body(0)
        with rolled(act, 1, SSD_GROUPS, [(astep, 1)]) as g:
            body(g)
        G = (ns + 1) * SSD_GROUPS
        act.wait_ge(E["stat_done"], G)
        act_rstd(act, link, S["rstd"], bank[7][:, 0:T], 1.0 / 512, RMS_EPS).then_inc(E["rstd_ready"], 1)

    def act_norm(act, l, link):
        n = layer_no[l]
        for k in range(KD):
            act.wait_ge(E["cent_ready"], KD * n + k + 1)
            if k >= 2:
                act.wait_ge(E["csq_used"], KD * n + k - 1)
            nc.scalar.activation(ln["sq"][:, k % 2, :], ln["pre"][:, k, :], ACT.Square).then_inc(E["csq_ready"], 1)
        act.wait_ge(E["csq_used"], KD * (n + 1))
        act_rstd(act, link, ln["rstd"], bank[3][:, 0:T], 1.0 / D, LN_EPS).then_inc(E["lrstd_ready"], 1)
        for k in range(KD):
            act.wait_ge(E["ln_mul"], KD * n + k + 1)
            nc.scalar.activation(H[:, k, :], ln["pre"][:, k, :], ACT.Identity, bias=pcol(l, "b", k)
                                 ).then_inc(E["h_ready"], 1)


    mla = {}
    (mla["qkv"], mla["sq"], mla["rs"], mla["kr0"], mla["kr"], mla["cos"], mla["sin"], mla["rt"], mla["kT"], mla["qn"],
     mla["qr0"], mla["qr"], mla["V"], mla["S"], mla["mask"], mla["pT"], mla["mx"], mla["acc"]) = carve(
        (10, T), (10, T), (2, T), (T,), (T,), (T,), (T,), (2, T), (2, T), (2, T),
        (T,), (T,), (2, T), (2, 384), (384,), (2, 384), (16,), (16,))

    def load_mla(sp, l, load, single, turns_of):
        w = a["mla_in_w"][0]
        for p in range(MLA_QT + MLA_KVT):
            single(p, w_tile(w, p * P))
        single(9, w_tile(w, MLA_COL_KR, 64))
        sp.dma_start(slot(9)[:, :, 64:128], w_tile(w, MLA_COL_KR, 64)).then_inc(E["kr_twice"], 16)
        turns_of(lambda i, free: [load(p, w_tile(w, MLA_COL_Z + p * P + i * 4 * P if isinstance(i, int) else
                                                 sp.snap(MLA_COL_Z + p * P + i * 4 * P)), free[p]) for p in range(4)], 4, 4)
        qw = a["mla_q_up_w"][0].rearrange("(k p) n -> p k n", p=P)
        kvw = a["mla_kv_up_w"][0].rearrange("(k p) n -> p k n", p=P)

        def body(i, free):
            for e in range(2):
                c = (2 * i + e) * 192
                load(4 + e, qw[:, :, ds(c if isinstance(i, int) else sp.snap(c), 192)], free[e],
                     dst=ring[:, 4 + e, 0:MLA_QT * 192].rearrange("p (k c) -> p k c", k=MLA_QT))
            c = i * 512
            load(6, kvw[:, :, ds(c if isinstance(i, int) else sp.snap(c), 512)], free[2],
                 dst=ring[:, 6, :].rearrange("p (k c) -> p k c", k=MLA_KVT))
        turns_of(body, 3, MLA_H // 2, base=4)

    def pe_mla(pe, l, take, taken, tile, hidden, first_hidden):
        M = mla
        fh = first_hidden(l)
        for p in range(10):
            take(p)
            if p >= 2:
                pe.wait_ge(E["qkv_raw"], p - 1)
            tile(p, pj[p % 2], hidden, waits=fh if p == 0 else None)
        take(9)
        pe.wait_ge(E["kr_twice"], 16)
        pe.wait_ge(E["qkv_raw"], 9)
        tile(9, pj[0], hidden)

        def z_body(i):
            for p in range(4):
                take(p)
                if isinstance(i, int) and p < 2:
                    pe.wait_ge(E["qkv_raw"], 10)
                    if p == 1:
                        pe.wait_ge(E["kr_raw"], 1)
                else:
                    pe.wait_ge(E["mz_ready"], i * 4 + p - 1)
                tile(p, pj[(p + 1) % 2], hidden)
        z_body(0)
        for j, (i0, i1) in enumerate(((0, MLA_QT), (MLA_QT, 10))):
            for i in range(i0, i1):
                pe.wait_ge(E["qkv_sq"], i + 1)
                mm = nc.tensor.matmul(bank[2 + j][:, 0:T], C["ones"], M["sq"][:, i, :], start=i == i0, stop=i == i1 - 1)
            mm.then_inc(E["qkv_stat"], 1)
        nc.tensor.matmul(bank[4][:, 0:T], C["rot"], M["kr0"], start=True, stop=True).then_inc(E["kr_rot"], 1)
        with rolled(pe, 1, 4, [(taken[p], 16) for p in range(4)]) as i:
            z_body(i)
        pe.wait_ge(E["qkv_ready"], 10)
        pe.wait_ge(E["kr_ready"], 1)
        pe.wait_ge(E["mz_ready"], 16)

        def attend(h):
            for e in range(2):
                pe.wait_ge(E["p_ready"], h * 2 + e + 1)
                for b in range(3):
                    mm = nc.tensor.transpose(bank[6 + e][:, b * P:(b + 1) * P], M["S"][:, e, b * P:(b + 1) * P], ident)
                mm.then_inc(E["pt_done"], 1)
            for e in range(2):
                pe.wait_ge(E["pt_ready"], h * 2 + e + 1)
                v0, v1 = M["V"][:, 0, e * P:(e + 1) * P], M["V"][:, 1, e * P:(e + 1) * P]
                nc.tensor.matmul(bank[6 + e][:, 0:P], v0, M["pT"][:, e, 0:P], start=True, stop=True)
                nc.tensor.matmul(bank[6 + e][:, P:T], v0, M["pT"][:, e, P:T], start=True, stop=False)
                nc.tensor.matmul(bank[6 + e][:, P:T], v1, M["pT"][:, e, T:T + P], start=False, stop=True
                                 ).then_inc(E["pv_done"], 1)

        def body(h):
            first = isinstance(h, int)
            for e in range(2):
                take(4 + e)
                w = ring[:, 4 + e, 0:MLA_QT * 192].rearrange("p (k c) -> p k c", k=MLA_QT)
                for k in range(MLA_QT):
                    nc.tensor.matmul(bank[2 + e][:, 0:T], w[:, k, 0:P], M["qkv"][:, k, :], start=k == 0, stop=k == MLA_QT - 1)
                for k in range(MLA_QT):
                    mm = nc.tensor.matmul(bank[4][64 * e:64 * e + 64, 0:T], w[:, k, P:P + 64], M["qkv"][:, k, :],
                                          start=k == 0, stop=k == MLA_QT - 1)
                mm.then_inc(unit_done, 1)
            take(6)
            w = ring[:, 6, :].rearrange("p (k c) -> p k c", k=MLA_KVT)
            for e in range(2):
                for k in range(MLA_KVT):
                    mm = nc.tensor.matmul(pj[e], w[:, k, e * T:e * T + P], M["qkv"][:, MLA_QT + k, :],
                                          start=k == 0, stop=k == MLA_KVT - 1)
                mm.then_inc(E["up_done"], 1)
            pe.wait_ge(E["qr_raw"], h + 1)
            nc.tensor.matmul(bank[4][:, T:2 * T], C["rot"], M["qr0"], start=True, stop=True).then_inc(E["rot_done"], 1)
            if not first:
                attend(h - 1)
            wv = w.rearrange("p k (e c) -> p k e c", e=2)
            for c in range(2):
                for k in range(MLA_KVT):
                    mm = nc.tensor.matmul(bank[5][:, c * T:(c + 1) * T], M["qkv"][:, MLA_QT + k, c * P:(c + 1) * P],
                                          wv[:, k, :, P:T], start=k == 0, stop=k == MLA_KVT - 1)
            mm.then_inc(unit_done, 1)
            pe.wait_ge(E["qr_ready"], h + 1)
            for e in range(2):
                pe.wait_ge(E["kt_ready"], h * 2 + e + 1)
                pe.wait_ge(E["qn_ready"], h * 2 + e + 1)
                if not first:
                    pe.wait_ge(E["o_ready"], h * 2 - 1 + e)
                r0 = 64 * e
                for qt, (c0, n) in enumerate(((0, P), (P, T))):
                    nc.tensor.matmul(bank[6 + e][:, c0:c0 + n], M["qn"][:, e, qt * P:(qt + 1) * P], M["kT"][:, e, 0:n],
                                     start=True, stop=False)
                    mm = nc.tensor.matmul(bank[6 + e][:, c0:c0 + n], M["qr"][r0:r0 + 64, qt * P:(qt + 1) * P],
                                          M["kr"][r0:r0 + 64, 0:n], start=False, stop=True)
                mm.then_inc(E["sc_done"], 1)
        body(0)
        with rolled(pe, 1, MLA_H // 2, [(taken[p], 16) for p in (4, 5, 6)]) as h:
            body(h)
        attend(MLA_H // 2 - 1)

    def dve_mla(dve, l, link, step):
        M = mla
        U = first_unit[l]
        U2 = U + 11 + 16
        if layer_no[l]:
            dve.wait_ge(E["h_ready"], KD * layer_no[l])
        ang, n1 = M["S"][:, 0, 0:T], M["S"][:, 1, 0:T]
        link(nc.vector.tensor_copy(n1, posi[:]))
        link(nc.vector.tensor_scalar(ang, n1, inv_freq, None, ALU.mult))
        for dst, quarter in ((M["sin"], 0.0), (M["cos"], 0.25)):
            link(nc.vector.tensor_scalar(n1, ang, 1.0 / (2 * np.pi), quarter, ALU.mult, ALU.add))
            link(nc.vector.tensor_scalar(n1, n1, MAGIC, -MAGIC, ALU.add, ALU.add))
            link(nc.vector.scalar_tensor_tensor(out=dst, in0=n1, scalar=-TWO_PI_A, in1=ang, op0=ALU.mult, op1=ALU.add))
            link(nc.vector.scalar_tensor_tensor(out=dst, in0=n1, scalar=-TWO_PI_B, in1=dst, op0=ALU.mult, op1=ALU.add))
            link(nc.vector.scalar_tensor_tensor(out=dst, in0=n1, scalar=-TWO_PI_C, in1=dst, op0=ALU.mult, op1=ALU.add))
            link(nc.vector.tensor_scalar(dst, dst, 2 * np.pi * quarter, 3.1415925, ALU.add, ALU.min))
            nc.vector.tensor_scalar(dst, dst, -3.1415925, None, ALU.max).then_inc(E["trig_arg"], 1)
        nc.vector.tensor_copy(M["mask"][:, 0:P], C["negq"]).then_inc(E["mask_ready"], 1)
        nc.vector.memset(M["mask"][:, P:T], 0.0).then_inc(E["mask_ready"], 1)
        nc.vector.tensor_copy(M["mask"][:, T:T + P], C["negq"]).then_inc(E["mask_ready"], 1)
        for p in range(10):
            dve.wait_ge(unit_done, U + p + 1)
            nc.vector.tensor_copy(M["qkv"][:, p, :], pj[p % 2]).then_inc(E["qkv_raw"], 1)
        dve.wait_ge(unit_done, U + 11)
        nc.vector.tensor_copy(M["kr0"], pj[0]).then_inc(E["kr_raw"], 1)

        def rotary(dst, x, rot):
            link(nc.vector.tensor_tensor(M["rt"][:, 0, :], rot, M["sin"], ALU.mult))
            link(nc.vector.tensor_tensor(M["rt"][:, 1, :], x, M["cos"], ALU.mult))
            return nc.vector.tensor_tensor(dst, M["rt"][:, 0, :], M["rt"][:, 1, :], ALU.add)
        dve.wait_ge(E["kr_rot"], 1)
        dve.wait_ge(E["trig"], 2)
        rotary(M["kr"], M["kr0"], bank[4][:, 0:T]).then_inc(E["kr_ready"], 1)
        for i in range(10):
            j = int(i >= MLA_QT)
            dve.wait_ge(E["qkv_rstd"], j + 1)
            nc.vector.scalar_tensor_tensor(out=M["qkv"][:, i, :], in0=M["qkv"][:, i, :],
                                           scalar=pcol(l, "kvn" if j else "qn", i - MLA_QT * j), in1=M["rs"][:, j, :],
                                           op0=ALU.mult, op1=ALU.mult).then_inc(E["qkv_ready"], 1)

        def gate(h):
            for e in range(2):
                dve.wait_ge(E["pv_done"], h * 2 + e + 1)
                nc.vector.tensor_tensor(Y[:, ds(h * 2 + e, 1), :], bank[6 + e][:, 0:T], Y[:, ds(h * 2 + e + 16, 1), :],
                                        ALU.mult).then_inc(E["o_ready"], 1)

        def body(h):
            for e in range(2):
                dve.wait_ge(E["up_done"], h * 2 + e + 1)
                nc.vector.tensor_copy(M["kT"][:, e, :], pj[e]).then_inc(E["kt_ready"], 1)
            dve.wait_ge(E["rot_done"], h + 1)
            rotary(M["qr"], M["qr0"], bank[4][:, T:2 * T]).then_inc(E["qr_ready"], 1)
            if not isinstance(h, int):
                gate(h - 1)
            for e in range(2):
                mx = M["mx"][:, 4 * e:4 * e + 2]
                dve.wait_ge(E["sc_done"], h * 2 + e + 1)
                link(nc.vector.tensor_tensor(M["S"][:, e, :], bank[6 + e][:, 0:384], M["mask"], ALU.add))
                link(nc.vector.tensor_reduce(mx[:, 0:1], M["S"][:, e, 0:P], AX.X, ALU.max))
                link(nc.vector.tensor_reduce(mx[:, 1:2], M["S"][:, e, P:384], AX.X, ALU.max))
                nc.vector.tensor_scalar(M["mx"][:, 4 * e + 2:4 * e + 4], mx, -MLA_SCALE, None, ALU.mult
                                        ).then_inc(E["sc_max"], 1)
            for e in range(2):
                dve.wait_ge(E["p_exp"], h * 2 + e + 1)
                link(nc.vector.reciprocal(M["acc"][:, 4 * e + 2:4 * e + 4], M["acc"][:, 4 * e:4 * e + 2]))
                link(nc.vector.tensor_scalar(M["S"][:, e, 0:P], M["S"][:, e, 0:P], M["acc"][:, 4 * e + 2:4 * e + 3], None,
                                             ALU.mult))
                nc.vector.tensor_scalar(M["S"][:, e, P:384], M["S"][:, e, P:384], M["acc"][:, 4 * e + 3:4 * e + 4], None,
                                        ALU.mult).then_inc(E["p_ready"], 1)
        body(0)
        with rolled(dve, 1, MLA_H // 2, [(step, 12)]) as h:
            body(h)
        gate(MLA_H // 2 - 1)

    def act_mla(act, l, link, astep):
        M = mla
        U = first_unit[l]
        U2 = U + 11 + 16
        for i, dst in enumerate((M["sin"], M["cos"])):
            act.wait_ge(E["trig_arg"], i + 1)
            nc.scalar.activation(dst, dst, ACT.Sin).then_inc(E["trig"], 1)
        for i in range(10):
            act.wait_ge(E["qkv_raw"], i + 1)
            nc.scalar.activation(M["sq"][:, i, :], M["qkv"][:, i, :], ACT.Square).then_inc(E["qkv_sq"], 1)

        def z_body(i):
            for p in range(4):
                act.wait_ge(unit_done, U + 11 + i * 4 + p + 1)
                nc.scalar.activation(Y[:, ds(i * 4 + (16 + p), 1), :], pj[(p + 1) % 2], ACT.Silu).then_inc(E["mz_ready"], 1)
        z_body(0)
        for j, n in enumerate((MLA_QR, MLA_KVR)):
            act.wait_ge(E["qkv_stat"], j + 1)
            act_rstd(act, link, M["rs"][:, j, :], bank[2 + j][:, 0:T], 1.0 / n, RMS_EPS).then_inc(E["qkv_rstd"], 1)
        with act.Fori(1, 4) as i:
            z_body(i)

        def probs_t(h):
            for e in range(2):
                act.wait_ge(E["pt_done"], h * 2 + e + 1)
                nc.scalar.activation(M["pT"][:, e, :], bank[6 + e][:, 0:384], ACT.Copy).then_inc(E["pt_ready"], 1)

        def body(h):
            for e in range(2):
                act.wait_ge(unit_done, U2 + h * 3 + e + 1)
                nc.scalar.activation(M["qn"][:, e, :], bank[2 + e][:, 0:T], ACT.Copy).then_inc(E["qn_ready"], 1)
            nc.scalar.activation(M["qr0"], bank[4][:, 0:T], ACT.Copy).then_inc(E["qr_raw"], 1)
            if not isinstance(h, int):
                probs_t(h - 1)
            act.wait_ge(unit_done, U2 + h * 3 + 3)
            nc.scalar.activation(M["V"], as3(bank[5], 2), ACT.Copy).then_inc(E["v_ready"], 1)
            for e in range(2):
                act.wait_ge(E["sc_max"], h * 2 + e + 1)
                link(nc.scalar.activation(M["S"][:, e, 0:P], M["S"][:, e, 0:P], ACT.Exp, scale=MLA_SCALE,
                                          bias=M["mx"][:, 4 * e + 2:4 * e + 3], accum_out=M["acc"][:, 4 * e:4 * e + 1]))
                nc.scalar.activation(M["S"][:, e, P:384], M["S"][:, e, P:384], ACT.Exp, scale=MLA_SCALE,
                                     bias=M["mx"][:, 4 * e + 3:4 * e + 4], accum_out=M["acc"][:, 4 * e + 1:4 * e + 2]
                                     ).then_inc(E["p_exp"], 1)
        body(0)
        with rolled(act, 1, MLA_H // 2, [(astep, 2)]) as h:
            body(h)
        probs_t(MLA_H // 2 - 1)

    gdn = {}
    (gdn["conv"], gdn["qk"], gdn["v"], gdn["sqk"], gdn["rs"], gdn["qkn"], gdn["rows"], gdn["D"], gdn["A"], gdn["kbe"],
     gdn["kdec"], gdn["vb"], gdn["wT"], gdn["u"], gdn["vn"], gdn["S"], gdn["eg"], gdn["qdec"], gdn["osq"], gdn["ors"],
     gdn["sc"], gdn["tok"], gdn["gcol"]) = carve(
        (2, T), (2, T), (2, T), (2, T), (2, T), (2, T), (4, T), (4, P), (4, P), (4, P),
        (4, P), (4, P), (4, P), (4, P), (2, P), (2, P), (2, T), (2, T), (2, T), (2, T),
        (3, 2, 32), (2, 64), (2, 32))
    lent = ring[:, 8:10, :].rearrange("p a b -> p (a b)")
    gdn["lev"] = lent[:, 0:2560].rearrange("p (n x l) -> p n x l", n=5, x=4)
    gdn["U"], gdn["T"], gdn["PM"] = (lent[:, a0:a0 + 512].rearrange("p (x l) -> p x l", x=4) for a0 in (2560, 3072, 3584))
    gba = [gdn[n][0:64].rearrange("p x l -> p (x l)")[:, 0:T] for n in ("kbe", "kdec", "vb", "wT", "u", "A")]

    GDN_PLAN = {0: "grams", 1: "turns", 4: "inv0", 15: "wu", 16: "out0", 23: "norm"}
    for n in range(5):
        GDN_PLAN[5 + 2 * n], GDN_PLAN[6 + 2 * n] = f"left{n}", f"right{n}"
    for c in (1, 2, 3):
        GDN_PLAN[15 + 2 * c], GDN_PLAN[16 + 2 * c] = f"new{c}", f"out{c}"
    STATS_AT = 10

    def load_gdn(sp, l, load, single, turns_of):
        w, scr = a["gdn_in_w"][0], a["scr_gdn"]
        single(7, w_tile(w, GDN_COL_B, 64))

        def rows_of(j):
            row = 2 * j if isinstance(j, int) else sp.snap(2 * j)
            if not (isinstance(j, int) and j == 0):
                sp.wait_ge(unit_done, 1)
                sp.wait_ge(E["rows_used"], j)
                sp.wait_ge(E["eg_ready"], j)
            for half in range(2):
                r = row + half * GDN_HV
                sp.dma_start(gdn["rows"][:, 2 * half:2 * half + 2, :], scr[ds(r, 2), :].partition_broadcast(P)
                             ).then_inc(E["grows_in"], 16)

        def body(j, free):
            cols = [j * P, GDN_COL_K + j * P, GDN_COL_V + j * T, GDN_COL_V + P + j * T, GDN_COL_Z + j * T,
                    GDN_COL_Z + P + j * T]
            for p in range(GDN_TILES):
                load(p, w_tile(w, cols[p] if isinstance(j, int) else sp.snap(cols[p])), free[p])
            if isinstance(j, int):
                sp.wait_ge(E["gscr_ready"], 1)
                sp.dma_start(scr[0:32, :], gba[4][0:32]).then_inc(E["gscr_out"], 16)
                sp.dma_start(scr[32:64, :], gba[5][0:32]).then_inc(E["gscr_out"], 16)
                sp.wait_ge(E["gscr_out"], 32)
            rows_of(j)
        turns_of(body, GDN_TILES, GDN_HK)

    def pe_gdn(pe, l, take, taken, tile, hidden, first_hidden):
        S = gdn

        def halves(c):
            return c // 2, slice(64 * (c % 2), 64 * (c % 2) + 64)

        def chain(name, j):
            n = int(name[-1]) if name[-1].isdigit() else 0
            step = name.rstrip("0123456789")
            b2, b3, b4, b5, b6, b7 = (as3(bank[i], 4) for i in range(2, 8))
            if step == "grams":
                pe.wait_ge(E["nrm_ready"], 2 * (j + 1))
                for c in range(2):
                    cc = slice(c * P, (c + 1) * P)
                    nc.tensor.matmul(b2[:, c, :], S["qkn"][:, 1, cc], S["qkn"][:, 1, cc], start=True, stop=True)
                    mm = nc.tensor.matmul(b2[:, 2 + c, :], S["qkn"][:, 1, cc], S["qkn"][:, 0, cc], start=True, stop=True)
                mm.then_inc(E["kk_done"], 1)
            if step == "turns":
                pe.wait_ge(E["gy_ready"], j + 1)
                for c in range(2):
                    mm = nc.tensor.transpose(b3[:, c, :], S["qkn"][:, 1, c * P:(c + 1) * P], ident)
                mm.then_inc(E["kt_done"], 1)
                pe.wait_ge(E["gconv_silu"], 4 * (j + 1))
                for e in range(2):
                    for c in range(2):
                        mm = nc.tensor.transpose(b4[:, 2 * e + c, :], S["v"][:, e, c * P:(c + 1) * P], ident)
                mm.then_inc(E["vt_done"], 1)
            if step == "inv":
                pe.wait_ge(E["u_ready"], 6 * j + 1)
                for x in range(4):
                    mm = nc.tensor.transpose(b5[:, x, :], S["U"][:, x, :], ident)
                mm.then_inc(E["t0_done"], 1)
            if step == "left":
                pe.wait_ge(E["t_ready"], 5 * j + n + 1)
                pe.wait_ge(E["lev_ready"], 5 * j + n + 1)
                for x in range(4):
                    mm = nc.tensor.matmul(b5[:, x, :], S["lev"][:, n, x, :], S["T"][:, x, :], start=True, stop=True)
                mm.then_inc(E["left_done"], 1)
            if step == "right":
                pe.wait_ge(E["pm_ready"], 5 * j + n + 1)
                for x in range(4):
                    mm = nc.tensor.matmul(b7[:, x, :], S["PM"][:, x, :], S["U"][:, x, :], start=True, stop=True)
                mm.then_inc(E["ru_done"], 1)
                if n < 4:
                    for x in range(4):
                        mm = nc.tensor.matmul(b6[:, x, :], S["U"][:, x, :], S["PM"][:, x, :], start=True, stop=True)
                    mm.then_inc(E["rt_done"], 1)
            if step == "wu":
                pe.wait_ge(E["u_ready"], 6 * j + 6)
                pe.wait_ge(E["kbe_ready"], j + 1)
                for x in range(4):
                    mm = nc.tensor.matmul(b5[:, x, :], S["kbe"][:, x, :], S["U"][:, x, :], start=True, stop=True)
                mm.then_inc(E["w_done"], 1)
                pe.wait_ge(E["vb_ready"], j + 1)
                for x in range(4):
                    mm = nc.tensor.matmul(b6[:, x, :], S["U"][:, x, :], S["vb"][:, x, :], start=True, stop=True)
                mm.then_inc(E["uv_done"], 1)
            if step == "new":
                c, h = halves(n)
                pe.wait_ge(E["s_ready"], 6 * j + 2 * n)
                for e in range(2):
                    mm = nc.tensor.matmul(b7[h, e, :], S["wT"][:, 2 * e + c, h], S["S"][:, e, :], start=True, stop=True)
                mm.then_inc(E["ws_done"], 1)
            if step == "out":
                c, h = halves(n)
                pe.wait_ge(E["vn_ready"], 4 * j + n + 1)
                if n == 0:
                    pe.wait_ge(E["qdec_ready"], 2 * (j + 1))
                    pe.wait_ge(E["kdec_ready"], j + 1)
                if n < 3:
                    for e in range(2):
                        mm = nc.tensor.matmul(b4[:, e, :], S["kdec"][h, 2 * e + c, :], S["vn"][h, e, :], start=True, stop=True)
                    mm.then_inc(E["ds_done"], 1)
                for e in range(2):
                    o = bank[3][:, e * T + n * 64:e * T + n * 64 + 64]
                    if n:
                        nc.tensor.matmul(o, S["S"][:, e, :], S["qdec"][:, e, n * 64:n * 64 + 64], start=True, stop=False)
                    mm = nc.tensor.matmul(o, S["vn"][h, e, :], S["D"][h, 2 * e + c, h], start=n == 0, stop=True)
                mm.then_inc(E["os_done"], 1)
            if step == "norm":
                pe.wait_ge(E["osq_ready"], j + 1)
                nc.tensor.matmul(bank[7], C["ones"], S["osq"].rearrange("p e t -> p (e t)"), start=True, stop=True
                                 ).then_inc(E["ostat_done"], 1)

        def body(j):
            first = isinstance(j, int)
            for q in range(4 * GDN_TILES):
                p = q // 4
                if not first and q in GDN_PLAN:
                    chain(GDN_PLAN[q], j - 1)
                if q == STATS_AT:
                    pe.wait_ge(E["sqk_ready"], 2 * (j + 1))
                    nc.tensor.matmul(bank[2], C["ones"], S["sqk"].rearrange("p e t -> p (e t)"), start=True, stop=True
                                     ).then_inc(E["nstat_done"], 1)
                if q % 4 == 0:
                    take(p)
                    if p < 2:
                        if first:
                            if p == 1:
                                pe.wait_ge(E["ba_raw"], 1)
                        else:
                            pe.wait_ge(E["gz_ready"], 2 * j - 1 + p)
                    elif p < 6:
                        pe.wait_ge(E["gconv_ready"], 4 * j + p - 1)
                for k in range(4 * (q % 4), 4 * (q % 4) + 4):
                    mm = nc.tensor.matmul(pj[p % 2], slot(p)[:, k, :], hidden(k), start=k == 0, stop=k == KD - 1)
                if q % 4 == 3:
                    mm.then_inc(unit_done, 1)
                if first and q == 7:
                    pe.wait_ge(E["ba_ready"], 1)
                    for c in range(2):
                        mm = nc.tensor.transpose(bank[2][:, c * 64:(c + 1) * 64], gba[5][:, c * P:(c + 1) * P],
                                                 ident[0:64, 0:64])
                    mm.then_inc(E["ba_t"], 1)
                if first and q == 13:
                    pe.wait_ge(E["ba_tok"], 1)
                    for c in range(2):
                        nc.tensor.matmul(bank[5][0:32, c * P:(c + 1) * P], S["tok"][:, c, 32:64], C["tri64"],
                                         start=True, stop=True)
                    nc.tensor.matmul(bank[6][:, 0:64], C["tri64"], S["tok"][:, :, 32:64], start=True, stop=True)
                    nc.tensor.matmul(bank[6][:, 64:128], C["blk64"], S["tok"][:, :, 32:64], start=True, stop=True
                                     ).then_inc(E["gc_done"], 1)

        take(7)
        tile(7, pj[1][0:64], hidden, width=64, waits=first_hidden(l))
        body(0)
        with rolled(pe, 1, GDN_HK, [(taken[p], 16) for p in range(GDN_TILES)]) as j:
            body(j)
        for q in sorted(GDN_PLAN):
            chain(GDN_PLAN[q], GDN_HK - 1)

    def per_token(ap):
        return ap.broadcast_to([P, 2, P])

    def dve_gdn(dve, l, link, step):
        S = gdn
        U = first_unit[l]
        flat = lambda ap: ap.rearrange("p x l -> p (x l)")
        if layer_no[l]:
            dve.wait_ge(E["h_ready"], KD * layer_no[l])
        raw, ab, ex, w1, sig, bg = gba
        lnw = S["osq"][0:64, 0, :]
        da, dt = S["ors"][0:64, 0, :], S["ors"][0:64, 1, :]
        sg = S["osq"][0:32, 1, :]
        nc.vector.memset(hd[:, 15:16], 0.0).then_inc(E["gy_ready"], 1)
        dve.wait_ge(unit_done, U + 1)
        nc.vector.tensor_scalar(raw, pj[1][0:64], hd[0:64, 8:9], None, ALU.add).then_inc(E["ba_raw"], 1)
        dve.wait_ge(E["ba_exp"], 1)
        nc.vector.tensor_scalar(w1, ex, 1.0, None, ALU.add).then_inc(E["ba_w"], 1)
        dve.wait_ge(E["ba_w"], 1)
        link(nc.vector.tensor_scalar(dt, w1, 1.0, 0.0, ALU.subtract, ALU.is_equal))
        link(nc.vector.scalar_tensor_tensor(out=da, in0=w1, scalar=-1.0, in1=dt, op0=ALU.add, op1=ALU.add))
        link(nc.vector.reciprocal(da, da))
        link(nc.vector.tensor_tensor(da, da, ex, ALU.mult))
        dve.wait_ge(E["ba_ln"], 1)
        link(nc.vector.tensor_tensor(dt, dt, lnw, ALU.add))
        link(nc.vector.tensor_tensor(da, da, dt, ALU.mult))
        link(nc.vector.scalar_tensor_tensor(out=dt, in0=raw, scalar=0.0, in1=da, op0=ALU.max, op1=ALU.add))
        link(nc.vector.tensor_scalar(bg[32:64], dt[32:64], hd[32:64, 10:11], -1.0, ALU.mult, ALU.mult))
        dve.wait_ge(E["ba_sig"], 1)
        link(nc.vector.tensor_scalar(sg, sg, 1.0, None, ALU.add))
        nc.vector.reciprocal(bg[0:32], sg).then_inc(E["ba_ready"], 1)

        def respond(name, j):
            n = int(name[-1]) if name[-1].isdigit() else 0
            kind = name.rstrip("0123456789")
            b2, b3, b4, b5, b6, b7 = (as3(bank[i], 4) for i in range(2, 8))
            if kind == "grams":
                dve.wait_ge(E["grows_in"], 32 * (j + 1))
                for e in range(2):
                    for c in range(2):
                        ins = nc.vector.scalar_tensor_tensor(
                            out=S["D"][:, 2 * e + c, :], in0=S["rows"][:, e, c * P:(c + 1) * P],
                            scalar=S["gcol"][:, c, ds(2 * j + e, 1)], in1=C["neg64"], op0=ALU.subtract, op1=ALU.min)
                ins.then_inc(E["gdiff_ready"], 1)
                dve.wait_ge(E["kk_done"], j + 1)
                dve.wait_ge(E["gdecay"], j + 1)
                D4 = S["D"].rearrange("p (e c) l -> p e c l", e=2)
                A4 = S["A"].rearrange("p (e c) l -> p e c l", e=2)
                for e in range(2):
                    ins = nc.vector.tensor_tensor(A4[:, e], D4[:, e], b2[:, 0:2, :], ALU.mult)
                link(ins)
                for e in range(2):
                    ins = nc.vector.tensor_tensor(D4[:, e], D4[:, e], b2[:, 2:4, :], ALU.mult)
                link(nc.vector.tensor_tensor(flat(S["A"]), flat(S["A"]), S["rows"][:, 2:4, :].rearrange("p e t -> p (e t)"),
                                             ALU.mult))
                nc.vector.tensor_copy(S["vn"][:, 0, 0:1], S["A"][:, 0, 0:1]).then_inc(E["rows_used"], 1)
                lev1 = C["lev1"].rearrange("p (o l) -> p o l", o=1).broadcast_to([P, 4, P])
                idb = ident.rearrange("p (o l) -> p o l", o=1).broadcast_to([P, 4, P])
                link(nc.vector.tensor_tensor(S["U"], S["A"], lev1, ALU.mult))
                nc.vector.tensor_tensor(S["U"], idb, S["U"], ALU.subtract).then_inc(E["u_ready"], 1)
            if kind == "turns":
                dve.wait_ge(E["kt_done"], j + 1)
                for e in range(2):
                    for c in range(2):
                        ins = nc.vector.tensor_scalar(S["kbe"][:, 2 * e + c, :], b3[:, c, :],
                                                      S["sc"][:, 0, c, ds(2 * j + e, 1)], None, ALU.mult)
                ins.then_inc(E["kbe_ready"], 1)
                for e in range(2):
                    for c in range(2):
                        ins = nc.vector.tensor_scalar(S["kdec"][:, 2 * e + c, :], b3[:, c, :],
                                                      S["sc"][:, 1, c, ds(2 * j + e, 1)], None, ALU.mult)
                ins.then_inc(E["kdec_ready"], 1)
                dve.wait_ge(E["vt_done"], j + 1)
                for e in range(2):
                    for c in range(2):
                        ins = nc.vector.tensor_scalar(S["vb"][:, 2 * e + c, :], b4[:, 2 * e + c, :],
                                                      S["tok"][:, c, ds(2 * j + e, 1)], None, ALU.mult)
                ins.then_inc(E["vb_ready"], 1)
                dve.wait_ge(E["eg_ready"], j + 1)
                for e in range(2):
                    nc.vector.tensor_tensor(S["qdec"][:, e, :], S["qkn"][:, 0, :], S["eg"][:, e, :], ALU.mult
                                            ).then_inc(E["qdec_ready"], 1)
            if kind == "inv":
                dve.wait_ge(E["t0_done"], j + 1)
                nc.vector.tensor_copy(flat(S["T"]), bank[5]).then_inc(E["t_ready"], 1)
            if kind == "left":
                dve.wait_ge(E["left_done"], 5 * j + n + 1)
                nc.vector.tensor_copy(flat(S["PM"]), bank[5]).then_inc(E["pm_ready"], 1)
            if kind == "right":
                dve.wait_ge(E["ru_done"], 5 * j + n + 1)
                if n < 4:
                    dve.wait_ge(E["rt_done"], 4 * j + n + 1)
                    nc.vector.tensor_tensor(flat(S["T"]), flat(S["T"]), bank[6], ALU.subtract).then_inc(E["t_ready"], 1)
                nc.vector.tensor_tensor(flat(S["U"]), flat(S["U"]), bank[7], ALU.subtract).then_inc(E["u_ready"], 1)
            if kind == "wu":
                dve.wait_ge(E["w_done"], j + 1)
                link(nc.vector.tensor_copy(flat(S["wT"]), bank[5]))
                dve.wait_ge(E["uv_done"], j + 1)
                nc.vector.tensor_copy(flat(S["u"]), bank[6]).then_inc(E["u2_ready"], 1)
                dve.wait_ge(E["u2_ready"], j + 1)
                us = S["u"].rearrange("p (e c) l -> p e c l", e=2)
                nc.vector.tensor_copy(S["vn"][0:64], us[0:64, :, 0, :]).then_inc(E["vn_ready"], 1)
            if kind == "new":
                c, h = n // 2, slice(64 * (n % 2), 64 * (n % 2) + 64)
                us = S["u"].rearrange("p (e c) l -> p e c l", e=2)
                dve.wait_ge(E["ws_done"], 3 * j + n)
                nc.vector.tensor_tensor(S["vn"][h], us[h, :, c, :], b7[h, 0:2, :], ALU.subtract).then_inc(E["vn_ready"], 1)
            if kind == "out" and n < 3:
                dve.wait_ge(E["ds_done"], 3 * j + n + 1)
                dve.wait_ge(E["os_done"], 4 * j + n + 1)
                for e in range(2):
                    last = n * 64 + 63
                    if n == 0:
                        nc.vector.tensor_copy(S["S"][:, e, :], b4[:, e, :]).then_inc(E["s_ready"], 1)
                    else:
                        nc.vector.scalar_tensor_tensor(out=S["S"][:, e, :], in0=S["S"][:, e, :],
                                                       scalar=S["eg"][:, e, last:last + 1], in1=b4[:, e, :],
                                                       op0=ALU.mult, op1=ALU.add).then_inc(E["s_ready"], 1)
            if kind == "norm":
                dve.wait_ge(E["ors_ready"], j + 1)
                link(nc.vector.scalar_tensor_tensor(out=flat(S["osq"]), in0=bank[3], scalar=pcol(l, "norm", 0),
                                                    in1=flat(S["ors"]), op0=ALU.mult, op1=ALU.mult))
                dve.wait_ge(E["gz_ready"], 2 * (j + 1))
                yy = Y[:, ds(2 * j, 2), :]
                nc.vector.tensor_tensor(yy, S["osq"], yy, ALU.mult).then_inc(E["gy_ready"], 1)

        def body(j):
            first = isinstance(j, int)
            for q in range(4 * GDN_TILES):
                if not first and q in GDN_PLAN:
                    respond(GDN_PLAN[q], j - 1)
                if q == STATS_AT:
                    dve.wait_ge(E["rs_ready"], j + 1)
                    nc.vector.scalar_tensor_tensor(out=S["qkn"][:, 0, :], in0=S["qk"][:, 0, :], scalar=P ** -0.5,
                                                   in1=S["rs"][:, 0, :], op0=ALU.mult, op1=ALU.mult
                                                   ).then_inc(E["nrm_ready"], 1)
                    nc.vector.tensor_tensor(S["qkn"][:, 1, :], S["qk"][:, 1, :], S["rs"][:, 1, :], ALU.mult
                                            ).then_inc(E["nrm_ready"], 1)
                if first and q == 7:
                    dve.wait_ge(E["ba_t"], 1)
                    nc.vector.tensor_copy(S["tok"], as3(bank[2][:, 0:P], 2)).then_inc(E["ba_tok"], 1)
                if first and q == 13:
                    dve.wait_ge(E["gc_done"], 1)
                    link(nc.vector.tensor_copy(S["gcol"], as3(bank[6][:, 0:64], 2)))
                    nc.vector.tensor_tensor(S["sc"][:, 1], as3(bank[6][:, 64:128], 2), S["gcol"], ALU.subtract
                                            ).then_inc(E["gsc_pre"], 1)
                    nc.vector.tensor_copy(gba[4][0:32], bank[5][0:32, 0:T]).then_inc(E["gscr_ready"], 1)
                    dve.wait_ge(E["gsc_exp"], 2)
                    link(nc.vector.tensor_tensor(S["sc"][:, 0], S["sc"][:, 0], S["tok"][:, :, 0:32], ALU.mult))
                if q % 4 == 0 and 4 <= q <= 16:
                    p = q // 4 - 1
                    dve.wait_ge(unit_done, U + 2 + j * GDN_TILES + p)
                    if not (first and p < 2):
                        dve.wait_ge(E["gconv_silu"], 4 * j + p - 1)
                    tile_no = [j, GDN_HK + j, 2 * GDN_HK + 2 * j, 2 * GDN_HK + 2 * j + 1][p]
                    conv(dve, link, pj[p % 2], S["conv"][:, p % 2, :], l, tile_no).then_inc(E["gconv_ready"], 1)
        body(0)
        with rolled(dve, 1, GDN_HK, [(step, 17)]) as j:
            body(j)
        for q in sorted(GDN_PLAN):
            respond(GDN_PLAN[q], GDN_HK - 1)

    def act_gdn(act, l, link, astep):
        S = gdn
        U = first_unit[l]
        flat = lambda ap: ap.rearrange("p x l -> p (x l)")
        raw, ab, ex, w1, sig, bg = gba
        lnw, sg = S["osq"][0:64, 0, :], S["osq"][0:32, 1, :]
        act.wait_ge(E["ba_raw"], 1)
        link(nc.scalar.activation(ab, raw, ACT.Abs))
        nc.scalar.activation(ex, ab, ACT.Exp, scale=-1.0).then_inc(E["ba_exp"], 1)
        nc.scalar.activation(sg, raw[0:32], ACT.Exp, scale=-1.0).then_inc(E["ba_sig"], 1)
        act.wait_ge(E["ba_w"], 1)
        nc.scalar.activation(lnw, w1, ACT.Ln).then_inc(E["ba_ln"], 1)

        def respond(name, j):
            if name == "grams":
                act.wait_ge(E["gdiff_ready"], j + 1)
                nc.scalar.activation(flat(S["D"]), flat(S["D"]), ACT.Exp).then_inc(E["gdecay"], 1)
                nc.scalar.activation(flat(S["eg"]), S["rows"][:, 0:2, :].rearrange("p e t -> p (e t)"), ACT.Exp
                                     ).then_inc(E["eg_ready"], 1)
            if name == "norm":
                act.wait_ge(E["os_done"], 4 * (j + 1))
                nc.scalar.activation(flat(S["osq"]), bank[3], ACT.Square).then_inc(E["osq_ready"], 1)
                act.wait_ge(E["ostat_done"], j + 1)
                act_rstd(act, link, flat(S["ors"]), bank[7], 1.0 / P, RMS_EPS).then_inc(E["ors_ready"], 1)

        def body(j):
            first = isinstance(j, int)
            for q in range(4 * GDN_TILES + 1):
                if not first and q in GDN_PLAN:
                    respond(GDN_PLAN[q], j - 1)
                if q == STATS_AT:
                    act.wait_ge(E["nstat_done"], j + 1)
                    act_rstd(act, link, flat(S["rs"]), bank[2], 1.0, RMS_EPS).then_inc(E["rs_ready"], 1)
                if first and q == 14:
                    act.wait_ge(E["gsc_pre"], 1)
                    nc.scalar.activation(S["sc"][:, 0], S["gcol"], ACT.Exp).then_inc(E["gsc_exp"], 1)
                    nc.scalar.activation(S["sc"][:, 1], S["sc"][:, 1], ACT.Exp).then_inc(E["gsc_exp"], 1)
                if q % 4 == 0 and 4 <= q <= 16:
                    p = q // 4 - 1
                    act.wait_ge(E["gconv_ready"], 4 * j + p + 1)
                    if p == 2 and not first:
                        act.wait_ge(E["vt_done"], j)
                    dst = S["qk"][:, p, :] if p < 2 else S["v"][:, p - 2, :]
                    nc.scalar.activation(dst, S["conv"][:, p % 2, :], ACT.Silu).then_inc(E["gconv_silu"], 1)
                    if p < 2:
                        act.wait_ge(E["gconv_silu"], 4 * j + p + 1)
                        nc.scalar.activation(S["sqk"][:, p, :], dst, ACT.Square).then_inc(E["sqk_ready"], 1)
                if q in (20, 24):
                    e = (q - 20) // 4
                    act.wait_ge(unit_done, U + 2 + j * GDN_TILES + 4 + e)
                    nc.scalar.activation(Y[:, ds(2 * j + e, 1), :], pj[e], ACT.Silu).then_inc(E["gz_ready"], 1)
        body(0)
        with rolled(act, 1, GDN_HK, [(astep, 2)]) as j:
            body(j)
        respond("grams", GDN_HK - 1)
        respond("norm", GDN_HK - 1)

    def pool_gdn(pool, l):
        with pool.Fori(0, GDN_HK) as j:
            for n, b in enumerate(LEVELS):
                if n == 0:
                    pool.wait_ge(E["u_ready"], 6 * j + 1)
                by = C[f"lev{b}"].rearrange("p (o l) -> p o l", o=1).broadcast_to([P, 4, P])
                nc.gpsimd.tensor_tensor(gdn["lev"][:, n], gdn["A"], by, ALU.mult).then_inc(E["lev_ready"], 1)

    block = ctx.enter_context(nc.Block())

    @block.sync
    def _(sp):
        last = [0] * SLOTS
        units = [0]

        def load(p, src, free, dst=None):
            if not (isinstance(free, int) and free == 0):
                if not isinstance(free, int):
                    sp.wait_ge(unit_done, 1)
                sp.wait_ge(unit_done, free)
            sp.dma_start(slot(p)[:, :, 0:src.shape[2]] if dst is None else dst, src).then_inc(landed[p], 16)

        def single(p, src, dst=None):
            load(p, src, last[p], dst)
            units[0] += 1
            last[p] = units[0]

        def turns_of(body, n, turns, base=0):
            u0 = units[0]
            body(0, list(last[base:base + n]))
            with sp.Fori(1, turns) as i:
                body(i, [(i - 1) * n + (u0 + p + 1) for p in range(n)])
            for p in range(n):
                last[base + p] = u0 + (turns - 1) * n + p + 1
            units[0] += n * turns

        def load_out(w, kt):
            per = kt // KD

            def body(i, free):
                for t in range(4):
                    col = i * 512 + t * P
                    for h in range(per):
                        col = col if isinstance(i, int) else sp.snap(i * 512 + t * P)
                        load(t * per + h, w_tile(w, col, k0=h * KD), free[t * per + h])
            turns_of(body, 4 * per, 4)

        sp.dma_start(cst[:], a["consts"]).then_inc(E["consts_in"], 16)
        for c in range(2):
            sp.dma_start(xrows[:, c, :], a["x"][0, c * P:(c + 1) * P, :]).then_inc(E["x_in"], 16)
        for l in layers:
            if KINDS[l] == "ssd":
                load_ssd(sp, l, load, single, turns_of)
                load_out(a["ssd_out_w"][l // 3], 32)
            if KINDS[l] == "mla":
                load_mla(sp, l, load, single, turns_of)
                load_out(a["mla_out_w"][0], 16)
            if KINDS[l] == "gdn":
                load_gdn(sp, l, load, single, turns_of)
                last[8] = last[9] = units[0] + 2
                load_out(a["gdn_out_w"][0], 32)
        sp.wait_ge(E["out_rows"], 8)
        for c in range(2):
            sp.dma_start(a["out"][0, c * P:(c + 1) * P, :], xrows[:, c, :]).then_inc(E["out_done"], 16)
        sp.wait_ge(E["out_done"], 32)

    @block.tensor
    def _(pe):
        taken = [Count() for _ in range(SLOTS)]

        def take(p):
            pe.wait_ge(landed[p], taken[p].next(16))

        def tile(p, dst, rhs, width=P, start=True, stop=True, waits=None, out_of=None):
            for k in range(KD):
                if waits is not None:
                    waits(k)
                mm = nc.tensor.matmul(dst, slot(p)[:, k, 0:width], rhs(k), start=start and k == 0,
                                      stop=stop and k == KD - 1)
            mm.then_inc(unit_done, 1)

        def hidden(k):
            return H[:, k, :]

        def first_hidden(l):
            n = layer_no[l]
            return (lambda k: pe.wait_ge(E["h_ready"], KD * (n - 1) + k + 1)) if n else None

        def out_and_norm(l, kt):
            per = kt // KD
            n = layer_no[l]

            def body(i):
                for t in range(4):
                    if t >= 2 or not isinstance(i, int):
                        pe.wait_ge(E["pre_ready"], KD * n + i * 4 + t - 1)
                    for h in range(per):
                        take(t * per + h)
                        if isinstance(i, int) and t == 0:
                            pe.wait_ge(*y_ready_at(l, h))
                        tile(t * per + h, pj[t % 2], lambda k: Y[:, h * KD + k, :], start=h == 0, stop=h == per - 1)
            body(0)
            with rolled(pe, 1, 4, [(taken[p], 16) for p in range(4 * per)]) as i:
                body(i)
            pe.wait_ge(E["sum_ready"], n + 1)
            nc.tensor.matmul(bank[2][:, 0:T], C["ones"], ln["sum"], start=True, stop=True).then_inc(E["mean_done"], 1)
            for k in range(KD):
                pe.wait_ge(E["csq_ready"], KD * n + k + 1)
                mm = nc.tensor.matmul(bank[3][:, 0:T], C["ones"], ln["sq"][:, k % 2, :], start=k == 0, stop=k == KD - 1)
                mm.then_inc(E["csq_used"], 1)

        pe.wait_ge(E["consts_in"], 16)
        pe.wait_ge(E["prm_in"], 16 * N_PRM_DMA)
        for i, rows in enumerate(PROWS):
            if i >= 2:
                pe.wait_ge(E["prm_ready"], i - 1)
            nc.tensor.transpose(bank[2 + i % 2][:, 0:rows], prows[0:rows, i, :], ident[0:rows, 0:rows]
                                ).then_inc(E["prm_t"], 1)
        pe.wait_ge(E["x_in"], 32)
        for i in range(8):
            if i >= 4:
                pe.wait_ge(E["h_in"], i - 3)
            for j in range(4):
                c, k = i // 4, i % 4 * 4 + j
                mm = nc.tensor.transpose(bank[4 + i % 4][:, j * P:(j + 1) * P], xrows[:, c, k * P:(k + 1) * P], ident)
            mm.then_inc(E["x_t"], 1)
        pe.wait_ge(E["h_in"], 8)

        for l in layers:
            if KINDS[l] == "ssd":
                pe_ssd(pe, l, take, taken, tile, hidden, first_hidden)
                out_and_norm(l, 32)
            if KINDS[l] == "mla":
                pe_mla(pe, l, take, taken, tile, hidden, first_hidden)
                out_and_norm(l, 16)
            if KINDS[l] == "gdn":
                pe_gdn(pe, l, take, taken, tile, hidden, first_hidden)
                out_and_norm(l, 32)
        for i in range(8):
            if i >= 4:
                pe.wait_ge(E["out_rows"], i - 3)
            if i < 4:
                pe.wait_ge(E["h_ready"], KD * (len(layers) - 1) + 4 * (i + 1))
            for j in range(4):
                c, k = i // 4, i % 4 * 4 + j
                mm = nc.tensor.transpose(bank[4 + i % 4][:, j * P:(j + 1) * P], H[:, k, c * P:(c + 1) * P], ident)
            mm.then_inc(E["out_t"], 1)

    @block.vector
    def _(dve):
        step = Count()

        def link(ins):
            ins.then_inc(dve_step, 1)
            dve.wait_ge(dve_step, step.next())

        nc.vector.memset(hd[0:32, 8:9], 0.0).then_inc(E["zero_ready"], 1)
        dve.wait_ge(E["heads_in"], 16 * N_HEAD_DMA)
        for n in range(2):
            for e in range(2):
                nc.vector.tensor_copy(hd[64 * e:64 * e + 64, 16 + 32 * n:48 + 32 * n],
                                      dskip_rows[64 * e:64 * e + 64, n, e::2]).then_inc(E["dskip_ready"], 1)
        for i, rows in enumerate(PROWS):
            dve.wait_ge(E["prm_t"], i + 1)
            nc.vector.tensor_copy(params[:, i, 0:rows], bank[2 + i % 2][:, 0:rows]).then_inc(E["prm_ready"], 1)
        for i in range(8):
            dve.wait_ge(E["x_t"], i + 1)
            nc.vector.tensor_copy(H[:, i % 4 * 4:i % 4 * 4 + 4, i // 4 * P:(i // 4 + 1) * P], as3(bank[4 + i % 4], 4)
                                  ).then_inc(E["h_in"], 1)
        dve.wait_ge(E["h_in"], 8)

        for l in layers:
            if KINDS[l] == "ssd":
                dve_ssd(dve, l, link, step)
            if KINDS[l] == "mla":
                dve_mla(dve, l, link, step)
            if KINDS[l] == "gdn":
                dve_gdn(dve, l, link, step)
            dve_norm(dve, l, link, step)
        for i in range(8):
            dve.wait_ge(E["out_t"], i + 1)
            nc.vector.tensor_copy(xrows[:, i // 4, i % 4 * 512:(i % 4 + 1) * 512], bank[4 + i % 4]
                                  ).then_inc(E["out_rows"], 1)

    @block.scalar
    def _(act):
        astep = Count()

        def link(ins):
            ins.then_inc(act_step, 1)
            act.wait_ge(act_step, astep.next())
        for dst, src in PRM_DMAS:
            act.dma_start(dst, src).then_inc(E["prm_in"], 16)
        for dst, src in HEAD_DMAS:
            act.dma_start(dst, src).then_inc(E["heads_in"], 16)
        act.wait_ge(E["heads_in"], 16 * N_HEAD_DMA)
        for n in range(2):
            link(nc.scalar.activation(hd[0:64, 4 * n + 2:4 * n + 3], hd[0:64, 4 * n + 1:4 * n + 2], ACT.Exp))
        link(nc.scalar.activation(hd[32:64, 10:11], hd[32:64, 9:10], ACT.Exp))
        act.wait_ge(E["prm_ready"], len(PROWS))

        for l in layers:
            if KINDS[l] == "ssd":
                act_ssd(act, l, link, astep)
            if KINDS[l] == "mla":
                act_mla(act, l, link, astep)
            if KINDS[l] == "gdn":
                act_gdn(act, l, link, astep)
            act_norm(act, l, link)

    @block.gpsimd
    def _(pool):
        for l in layers:
            if KINDS[l] == "ssd":
                ns = nth_ssd[l]
                with pool.Fori(0, SSD_GROUPS) as g:
                    G = g + ns * SSD_GROUPS
                    pool.wait_ge(E["e_exp"], G + 1)
                    pool.wait_ge(E["conv_silu"], G * 6 + 2)
                    by = ssd["C"][:, P:T].rearrange("p (o l) -> p o l", o=1).broadcast_to([P, SSD_R, P])
                    nc.gpsimd.tensor_tensor(ssd["E"], ssd["E"], by, ALU.mult).then_inc(E["cdec_ready"], 1)
            if KINDS[l] == "gdn":
                pool_gdn(pool, l)


_INS = ["x", "positions", "ssd_in_w", "ssd_conv_w", "ssd_conv_b", "ssd_dt_bias", "ssd_a_log", "ssd_d", "ssd_norm_w",
        "ssd_out_w", "mla_in_w", "mla_q_norm_w", "mla_q_up_w", "mla_kv_norm_w", "mla_kv_up_w", "mla_out_w",
        "gdn_in_w", "gdn_conv_w", "gdn_a_log", "gdn_dt_bias", "gdn_norm_w", "gdn_out_w", "ln_g", "ln_b"]


def scratch(nc):
    return {"scr_ssd": nc.dram_tensor("scr_ssd", (2, SSD_HEADS, T), F32).ap(),
            "scr_gdn": nc.dram_tensor("scr_gdn", (2 * GDN_HV, T), F32).ap()}


def kernel(**inputs):
    import concourse.bacc as bacc
    from concourse.bass_utils import run_bass_kernel_spmd

    nc = bacc.Bacc("TRN2", target_bir_lowering=False, num_devices=1)
    arrays, args = {}, {}
    for name in _INS + ["consts"]:
        array = constants() if name == "consts" else np.ascontiguousarray(inputs[name])
        arrays[f"in_{name}"] = array
        args[name] = nc.dram_tensor(f"in_{name}", array.shape, mybir.dt.from_np(array.dtype), kind="ExternalInput").ap()
    args["out"] = nc.dram_tensor("out", (1, T, D), F32, kind="ExternalOutput").ap()
    args.update(scratch(nc))
    build(nc, args)
    r = run_bass_kernel_spmd(nc, [arrays], core_ids=[0])
    return r.results[0]["out"]
```

```python
from contextlib import contextmanager, ExitStack

import numpy as np
import concourse.bass as bass
from concourse import mybir

F32 = mybir.dt.float32
F32R = mybir.dt.float32r
I32 = mybir.dt.int32
ALU = mybir.AluOpType
ACT = mybir.ActivationFunctionType
AX = mybir.AxisListType
ds = bass.ds

P = 128
T = 256
D = 2048
KD = D // P
DEPTH = 4
ALPHA = (2.0 * DEPTH) ** 0.25
LN_EPS, RMS_EPS = 1e-5, 1e-6
KINDS = ["ssd", "mla", "gdn", "ssd"]

SSD_IN, SSD_HEADS, SSD_GROUPS = 4096, 64, 8
SSD_R = SSD_HEADS // SSD_GROUPS
SSD_CONV_DIM = SSD_IN + 2 * SSD_GROUPS * P
SSD_COL_X = SSD_IN
SSD_COL_B = SSD_COL_X + SSD_IN
SSD_COL_C = SSD_COL_B + SSD_GROUPS * P
SSD_COL_DT = SSD_COL_C + SSD_GROUPS * P
SSD_XT = SSD_IN // P
SSD_TILES = 10

MLA_H, MLA_QR, MLA_KVR, MLA_ROPE = 16, 768, 512, 64
MLA_QT, MLA_KVT = MLA_QR // P, MLA_KVR // P
MLA_COL_KR = MLA_QR + MLA_KVR
MLA_COL_Z = MLA_COL_KR + MLA_ROPE
MLA_SCALE = (128 + MLA_ROPE) ** -0.5

GDN_HK, GDN_HV = 16, 32
GDN_COL_K, GDN_COL_V, GDN_COL_Z = 2048, 4096, 8192
GDN_COL_B = 12288
GDN_TILES = 6
LEVELS = (2, 4, 8, 16, 32)

SLOTS, SLOT = 6, 2048
SSD_SLOTS, SSD_SLOTS_1 = [0, 1, 2, 3, 4, 0, 1, 2, 3, 4], [2, 3, 4, 5, 0, 1, 2, 3, 4, 5]
GDN_SLOTS, GDN_SLOTS_1 = [0, 1, 2, 3, 4, 5], [2, 3, 4, 5, 4, 5]
OUT_SLOTS = {32: [0, 1, 2, 3, 4, 5, 2, 3], 16: [0, 1, 2, 3]}
MLA_SLOTS = [p % SLOTS for p in range(12)]
Z_SLOTS = [0, 1, 2, 3]
UP_SLOT = 2
NEG = -1.0e30
MAGIC = 1.5 * 2.0 ** 23
TWO_PI_A = 6.28125
TWO_PI_B = float(np.float32(np.round((2 * np.pi - TWO_PI_A) * 2 ** 21) / 2 ** 21))
TWO_PI_C = float(np.float32(2 * np.pi - TWO_PI_A - TWO_PI_B))

CONST = ["ident", "ones", "tri128", "tri64", "blk64", "neg128", "neg64", "negq", "rot",
         "lev1", "lev2", "lev4", "lev8", "lev16", "lev32"]


def constants():
    r, c = np.arange(P)[:, None], np.arange(P)[None, :]
    same64 = r // 64 == c // 64
    m = {
        "ident": r == c,
        "ones": np.ones((P, P)),
        "tri128": r <= c,
        "tri64": (r <= c) & same64,
        "blk64": same64,
        "neg128": np.where(r <= c, 0.0, NEG),
        "neg64": np.where((r <= c) & same64, 0.0, NEG),
        "negq": np.where(c <= r, 0.0, NEG),
        "rot": np.where((c % 64 < 32) & (r == c + 32), -1.0, 0.0) + np.where((c % 64 >= 32) & (r == c - 32), 1.0, 0.0),
    }
    for b in (1,) + LEVELS:
        m[f"lev{b}"] = (r // (2 * b) == c // (2 * b)) & (c // b % 2 == 1) & (r // b % 2 == 0)
    inv = (10000.0 ** (-np.arange(0, MLA_ROPE, 2, dtype=np.float64) / MLA_ROPE)).astype(np.float32)
    cols = [np.asarray(m[n], np.float32) for n in CONST] + [np.tile(inv, 4)[:, None]]
    return np.ascontiguousarray(np.concatenate(cols, axis=1).astype(np.float32))


class Count:

    def __init__(self):
        self.n, self.turn, self.step = 0, 0, 0

    def next(self, by=1):
        self.n += by
        return self.n + self.turn * self.step if self.step else self.n


@contextmanager
def rolled(eng, start, end, steps):
    with eng.Fori(start, end) as i:
        at = [(c, c.n) for c, _ in steps]
        for c, by in steps:
            c.turn, c.step = i - start, by
        yield i
    for (c, n0), (_, by) in zip(at, steps):
        assert c.n - n0 == by, (c.n - n0, by)
        c.n, c.turn, c.step = n0 + by * (end - start), 0, 0


def build(nc, a, layers=range(DEPTH)):
    layers = list(layers)
    with ExitStack() as ctx:
        _program(nc, a, layers, ctx)


def _program(nc, a, layers, ctx):
    def sb(name, shape, dt=F32):
        return ctx.enter_context(nc.sbuf_tensor(name, shape, dt))

    def sem(name):
        return ctx.enter_context(nc.semaphore(name))

    def twins(name, shape):
        with nc.sbuf_tensor(name, shape, F32) as plain:
            pass
        return plain, sb(name + "_r", shape, F32R)

    H_hi = sb("H_hi", [P, KD, T], F32R)
    pre, H_lo = twins("pre", [P, KD, T])
    Y, Y_lo = twins("Y", [P, 32, T])
    ring, ring_lo = twins("ring", [P, SLOTS, SLOT])
    W_hi = sb("W_hi", [P, 2, SLOT], F32R)
    cst = sb("cst", [P, len(CONST) * P + 1])
    ARENA = 12100
    arena, arena_r = twins("arena", [P, ARENA])
    Y_hi = arena_r[:, ARENA - 32 * T:ARENA].rearrange("p (k t) -> p k t", t=T)
    params = sb("params", [P, 10, P])
    hd = sb("hd", [P, 16 + 2 * 32])
    posi = sb("posi", [P, T], I32)
    banks = [ctx.enter_context(nc.psum_tensor(f"bank{i}", [P, 512], F32)) for i in range(8)]
    C = {n: cst[:, P * i:P * (i + 1)] for i, n in enumerate(CONST)}
    inv_freq = cst[:, len(CONST) * P:len(CONST) * P + 1]
    ident = C["ident"]

    def carve(*shapes, base=0):
        at, out = base, []
        for s in shapes:
            n = int(np.prod(s))
            v = arena[:, at:at + n]
            if len(s) == 2:
                v = v.rearrange("p (a b) -> p a b", a=s[0])
            if len(s) == 3:
                v = v.rearrange("p (a b c) -> p a b c", a=s[0], b=s[1])
            out.append(v)
            at += n
        assert at <= ARENA, at
        return out

    def slot(p, k=KD):
        return ring[:, p, :].rearrange("p (k c) -> p k c", k=k)

    bank = [b[:] for b in banks]
    pj = [bank[0][:, 0:T], bank[1][:, 0:T]]

    def as3(ap, a):
        return ap.rearrange("p (a b) -> p a b", a=a)

    landed = [sem(f"landed{p}") for p in range(SLOTS)]
    up_landed = [sem(f"up_landed{p}") for p in range(3)]
    half_done = sem("half_done")
    hi_ready = sem("hi_ready")
    lo0_ready, lo1_ready = sem("lo0_ready"), sem("lo1_ready")
    unit_done = sem("unit_done")
    dve_step, act_step = sem("dve_step"), sem("act_step")
    class Events(dict):

        def __missing__(self, name):
            self[name] = sem(name)
            return self[name]

    E = Events()

    first_unit, first_split, layer_no, nth_ssd = {}, {}, {}, {}
    at = up = 0
    for n, l in enumerate(layers):
        kind = KINDS[l]
        layer_no[l] = n
        nth_ssd[l] = sum(KINDS[x] == "ssd" for x in layers[:n])
        first_unit[l], first_split[l] = at, at - up
        at += {"ssd": 2 + SSD_TILES * SSD_GROUPS, "mla": 12 + 16 + 3 * 8, "gdn": 2 + GDN_TILES * GDN_HK}[kind]
        up += 24 if kind == "mla" else 0
        first_unit[l, "out"], first_split[l, "out"] = at, at - up
        at += 16 if kind == "mla" else 32
    last_layer = layers[-1]

    def w_tile(w, col, width=P, k0=0, kn=KD):
        return w.rearrange("(k p) n -> p k n", p=P)[:, k0:k0 + kn, ds(col, width)]

    class Splitter:

        def __init__(self, eng, part):
            self.eng, self.part = eng, part
            self.taken = [Count() for _ in range(SLOTS)]

        def split(self, p, par, s, freed=None):
            eng, h = self.eng, SLOT // 2
            if self.part == "act":
                eng.wait_ge(landed[p], self.taken[p].next(16))
                for half, at in ((0, slice(0, h)), (1, slice(h, 2 * h))):
                    if freed is not None:
                        eng.wait_ge((half_done, unit_done)[half], freed[half])
                    nc.scalar.activation(W_hi[:, par, at], ring[:, p, at], ACT.Copy).then_inc(hi_ready, 1)
            if self.part == "dve":
                eng.wait_ge(hi_ready, s * 2 + 1)
                nc.vector.tensor_tensor(ring_lo[:, p, 0:h], ring[:, p, 0:h], W_hi[:, par, 0:h].bitcast(F32),
                                        ALU.subtract).then_inc(lo0_ready, 1)
            if self.part == "pool":
                eng.wait_ge(hi_ready, s * 2 + 2)
                nc.gpsimd.tensor_tensor(ring_lo[:, p, h:SLOT], ring[:, p, h:SLOT], W_hi[:, par, h:SLOT].bitcast(F32),
                                        ALU.subtract).then_inc(lo1_ready, 1)

        def ahead(self, slots, p, s, u):
            self.split((slots + [0, 1])[p + 2], p % 2, s + 2, freed=(s + 1, u + 1))

        def steps(self, slots):
            return [(self.taken[p], 16 * slots.count(p)) for p in range(SLOTS) if p in slots]

    ssd = {}
    (ssd["conv"], ssd["B"], ssd["C"], ssd["X"], ssd["Z"], ssd["xdt"], ssd["xds"], ssd["btok"], ssd["rows"],
     ssd["D"], ssd["E"], ssd["st"], ssd["YG"], ssd["rstd"], ssd["tok"], ssd["acol"], ssd["dst"]) = carve(
        (2, T), (T,), (T,), (4, T), (4, T), (2, 512), (512,), (P,), (SSD_R, T),
        (2, SSD_R, P), (SSD_R, P), (512,), (4, T), (T,), (4, 64), (2, 64), (64,))
    ssd["SQ"] = ssd["E"].rearrange("p r t -> p (r t)").rearrange("p (a b) -> p a b", a=4)
    dtv = [ssd["YG"][0:64, i, :] for i in range(4)] + [ssd["xdt"][0:64, 0, 0:T], ssd["xdt"][0:64, 0, T:2 * T],
                                                      ssd["xdt"][0:64, 1, 0:T], ssd["xdt"][0:64, 1, T:2 * T]]
    ln = {}
    ln["sum"], ln["rstd"], ln["sq"] = carve((T,), (T,), (2, T))
    xrows = arena[:, 0:2 * D].rearrange("p (c n) -> p c n", c=2)
    prows = Y[:, 0:5, :].rearrange("p a (b c) -> p (a b) c", b=2)
    dskip_rows = Y[:, 5, 0:P].rearrange("p (n h) -> p n h", n=2)

    y_base, y_split_base, yb, yc = {}, {}, 0, 0
    for l in layers:
        y_base[l], y_split_base[l] = yb, yc
        yb += 32 if KINDS[l] == "ssd" else 0
        yc += 4 if KINDS[l] == "mla" else 8

    PCOL = {}
    for n, l in enumerate((0, 3)):
        for tap in range(4):
            PCOL[l, f"tap{tap}"] = (3 * n + tap // 2) * P + 48 * (tap % 2)
        PCOL[l, "g"], PCOL[l, "b"] = 3 * n * P + 96, 3 * n * P + 112
        PCOL[l, "norm"], PCOL[l, "cb"] = (3 * n + 1) * P + 96, (3 * n + 2) * P
    for tap in range(4):
        PCOL[2, f"tap{tap}"] = (6 + tap // 2) * P + 64 * (tap % 2)
    PCOL[2, "g"], PCOL[2, "b"], PCOL[2, "norm"] = 8 * P, 8 * P + 16, 8 * P + 32
    PCOL[1, "qn"], PCOL[1, "kvn"], PCOL[1, "g"], PCOL[1, "b"] = 9 * P, 9 * P + 6, 9 * P + 10, 9 * P + 26
    PROWS = [128, 128, 48, 128, 128, 48, 128, 128, 33, 42]

    def pcol(l, name, idx):
        flat = params[:].rearrange("p a b -> p (a b)")
        return flat[:, ds(PCOL[l, name] + idx, 1)]


    def rows128(ap):
        return ap.rearrange("(r c) -> r c", c=P)

    PRM_DMAS = []
    for n, l in enumerate((0, 3)):
        for tap in range(4):
            r0 = 48 * (tap % 2)
            PRM_DMAS.append((prows[r0:r0 + 48, 3 * n + tap // 2, :], rows128(a["ssd_conv_w"][n, tap])))
        PRM_DMAS += [(prows[96:112, 3 * n, :], rows128(a["ln_g"][l])), (prows[112:128, 3 * n, :], rows128(a["ln_b"][l])),
                     (prows[96:128, 3 * n + 1, :], rows128(a["ssd_norm_w"][n])),
                     (prows[0:48, 3 * n + 2, :], rows128(a["ssd_conv_b"][n]))]
    for tap in range(4):
        r0 = 64 * (tap % 2)
        PRM_DMAS.append((prows[r0:r0 + 64, 6 + tap // 2, :], rows128(a["gdn_conv_w"][0, tap])))
    PRM_DMAS += [(prows[0:16, 8, :], rows128(a["ln_g"][2])), (prows[16:32, 8, :], rows128(a["ln_b"][2])),
                 (prows[32:33, 8, :], a["gdn_norm_w"]),
                 (prows[0:6, 9, :], rows128(a["mla_q_norm_w"][0])), (prows[6:10, 9, :], rows128(a["mla_kv_norm_w"][0])),
                 (prows[10:26, 9, :], rows128(a["ln_g"][1])), (prows[26:42, 9, :], rows128(a["ln_b"][1]))]
    N_PRM_DMA = len(PRM_DMAS)

    def column(ap):
        return ap.rearrange("(h o) -> h o", o=1)

    HEAD_DMAS = []
    for n in range(2):
        HEAD_DMAS += [(hd[0:64, 4 * n:4 * n + 1], column(a["ssd_dt_bias"][n])),
                      (hd[0:64, 4 * n + 1:4 * n + 2], column(a["ssd_a_log"][n])),
                      (dskip_rows[:, n, :], a["ssd_d"][n].partition_broadcast(P))]
    HEAD_DMAS += [(hd[32:64, 8:9], column(a["gdn_dt_bias"][0])), (hd[32:64, 9:10], column(a["gdn_a_log"][0])),
                  (posi[:], a["positions"][0].partition_broadcast(P))]
    N_HEAD_DMA = len(HEAD_DMAS)

    def load_ssd(sp, l, load, turns_of):
        w, ns = a["ssd_in_w"][l // 3], nth_ssd[l]
        scr = a["scr_ssd"][ns]
        for p in range(2):
            load(p, w_tile(w, SSD_COL_DT, 64), first_unit[l] + p)

        def rows_of(g):
            G = g + ns * SSD_GROUPS
            row = g * SSD_R if isinstance(g, int) else sp.snap(g * SSD_R)
            if not (isinstance(G, int) and G == 0):
                sp.wait_ge(unit_done, 1)
                sp.wait_ge(E["diff_ready"], G)
                sp.wait_ge(E["e_exp"], G)
            sp.dma_start(ssd["rows"], scr[ds(row, SSD_R), :].partition_broadcast(P)).then_inc(E["rows_in"], 16)

        def source(g, p):
            return w_tile(w, [SSD_COL_B + g * P, SSD_COL_C + g * P, SSD_COL_X + g * 512, SSD_COL_X + P + g * 512,
                              SSD_COL_X + 2 * P + g * 512, SSD_COL_X + 3 * P + g * 512,
                              g * 512, g * 512 + P, g * 512 + 2 * P, g * 512 + 3 * P][p])

        def beside(g, p):
            if p == 6 and not isinstance(g, int):
                rows_of(g)
            if p == 7 and isinstance(g, int):
                sp.wait_ge(E["acs_ready"], ns + 1)
                sp.dma_start(scr, dtv[7]).then_inc(E["scr_out"], 16)
                sp.wait_ge(E["scr_out"], 16 * (ns + 1))
                rows_of(0)
        turns_of(source, first_unit[l] + 2, SSD_SLOTS_1, SSD_SLOTS, SSD_GROUPS, beside)

    def pe_ssd(pe, l, tile, contract, head_tile, hidden, first_hidden):
        ns = nth_ssd[l]
        S = ssd

        def body(g):
            G = g + ns * SSD_GROUPS
            head = isinstance(g, int)

            def proj(p):
                if p in (0, 1):
                    if not head:
                        pe.wait_ge(E["z_ready"], G * 4)
                    if head and p == 1:
                        pe.wait_ge(E["dt_x"], ns + 1)
                elif p < 8:
                    pe.wait_ge(E["conv_ready"], G * 6 + p - 1)
                else:
                    pe.wait_ge(E["z_ready"], G * 4 + p - 7)
                tile(slots[p], p, pj[p % 2], hidden, first_split[l] + 2 + g * SSD_TILES + p)

            slots = SSD_SLOTS_1 if head else SSD_SLOTS
            proj(0)
            if not head:
                for i in range(4):
                    pe.wait_ge(E["sq_ready"], (G - 1) * 4 + i + 1)
                    mm = nc.tensor.matmul(bank[7][:, 0:T], C["ones"], S["SQ"][:, i, :], start=i == 0, stop=i == 3)
                mm.then_inc(E["stat_done"], 1)
            proj(1)
            if head:
                pe.wait_ge(E["dt_a"], ns + 1)
                for j in range(4):
                    src = (dtv[5] if j < 2 else dtv[6])[:, j % 2 * P:(j % 2 + 1) * P]
                    mm = nc.tensor.transpose(bank[2][:, j * 64:(j + 1) * 64], src, ident[0:64, 0:64])
                mm.then_inc(E["dt_t"], 1)
            proj(2)
            if head:
                pe.wait_ge(E["dt_tok"], ns + 1)
                for c in range(2):
                    nc.tensor.matmul(bank[3][0:64, c * P:(c + 1) * P], S["tok"][:, 2 + c, :], C["tri128"],
                                     start=True, stop=True)
                nc.tensor.matmul(bank[4][:, 0:P], C["tri128"], S["tok"][:, 2:4, :], start=True, stop=True)
                nc.tensor.matmul(bank[4][:, P:P + 64], C["ones"], S["tok"][:, 2, :], start=True, stop=True
                                 ).then_inc(E["cum_done"], 1)
            proj(3)
            proj(4)
            pe.wait_ge(E["conv_silu"], G * 6 + 2)
            if head:
                pe.wait_ge(E["acs_ready"], ns + 1)
            for c in range(2):
                mm = nc.tensor.matmul(bank[6][:, c * P:(c + 1) * P], S["B"][:, c * P:(c + 1) * P],
                                      S["C"][:, c * P:(c + 1) * P], start=True, stop=True)
            mm.then_inc(E["cb_done"], 1)
            proj(5)
            proj(6)
            pe.wait_ge(E["conv_silu"], G * 6 + 6)
            for c in range(2):
                for t in range(4):
                    mm = nc.tensor.transpose(bank[2 + c][:, t * P:(t + 1) * P], S["X"][:, t, c * P:(c + 1) * P], ident)
                mm.then_inc(E["tx_done"], 1)
            if not head:
                pe.wait_ge(E["rstd_ready"], G)
            nc.tensor.transpose(bank[7][:, 0:P], S["B"][:, 0:P], ident).then_inc(E["bt_done"], 1)
            proj(7)
            pe.wait_ge(E["btok_ready"], G + 1)
            pe.wait_ge(E["xds_ready"], G + 1)
            nc.tensor.matmul(bank[7], S["btok"], S["xds"], start=True, stop=True).then_inc(E["st_done"], 1)
            pe.wait_ge(E["m_ready"], G * 2 + 1)
            for r in range(SSD_R):
                o = bank[4 + r // 4][64 * (r % 2):64 * (r % 2) + 64, r // 2 % 2 * T:r // 2 % 2 * T + P]
                nc.tensor.matmul(o, S["xdt"][:, 0, r * 64:(r + 1) * 64], S["D"][:, 0, r, :], start=True, stop=True)
            proj(8)
            pe.wait_ge(E["m_ready"], G * 2 + 2)
            pe.wait_ge(E["cdec_ready"], G + 1)
            pe.wait_ge(E["st_ready"], G + 1)
            for r in range(SSD_R):
                o = bank[4 + r // 4][64 * (r % 2):64 * (r % 2) + 64, r // 2 % 2 * T + P:r // 2 % 2 * T + 2 * P]
                nc.tensor.matmul(o, S["xdt"][:, 1, r * 64:(r + 1) * 64], S["D"][:, 1, r, :], start=True, stop=False)
                mm = nc.tensor.matmul(o, S["st"][:, r * 64:(r + 1) * 64], S["E"][:, r, :], start=False, stop=True)
            mm.then_inc(E["y_done"], 1)
            proj(9)

        head_tile(0, pj[1], first_split[l], first_hidden(l))
        body(0)
        with pe.Fori(1, SSD_GROUPS) as g:
            body(g)
        G = ns * SSD_GROUPS + SSD_GROUPS
        for i in range(4):
            pe.wait_ge(E["sq_ready"], (G - 1) * 4 + i + 1)
            mm = nc.tensor.matmul(bank[7][:, 0:T], C["ones"], S["SQ"][:, i, :], start=i == 0, stop=i == 3)
        mm.then_inc(E["stat_done"], 1)

    def conv(dve, link, src, dst, l, tile_no):
        link(nc.vector.tensor_scalar(dst, src, pcol(l, "tap3", tile_no), None, ALU.mult))
        for s in (1, 2, 3):
            ins = nc.vector.scalar_tensor_tensor(out=dst[:, s:T], in0=src[:, 0:T - s],
                                                 scalar=pcol(l, f"tap{3 - s}", tile_no), in1=dst[:, s:T],
                                                 op0=ALU.mult, op1=ALU.add)
            if s < 3:
                link(ins)
        return ins

    def dve_ssd(dve, l, link, step, splitter):
        ns, S = nth_ssd[l], ssd
        U, S0 = first_unit[l], first_split[l]
        for e in range(2):
            splitter.ahead([0, 1] + SSD_SLOTS_1, e, S0 + e, U + e)
        raw, absx, ex, w1, lnw, dt, da, arow = dtv
        hcol = hd[0:64, 4 * (l // 3):4 * (l // 3) + 3]
        dve.wait_ge(unit_done, U + 2)
        nc.vector.tensor_scalar(raw, pj[1][0:64], hcol[:, 0:1], None, ALU.add).then_inc(E["dt_x"], 1)
        dve.wait_ge(E["dt_exp"], ns + 1)
        nc.vector.tensor_scalar(w1, ex, 1.0, None, ALU.add).then_inc(E["dt_w"], 1)
        dve.wait_ge(E["dt_w"], ns + 1)
        link(nc.vector.tensor_scalar(dt, w1, 1.0, 0.0, ALU.subtract, ALU.is_equal))
        link(nc.vector.scalar_tensor_tensor(out=da, in0=w1, scalar=-1.0, in1=dt, op0=ALU.add, op1=ALU.add))
        link(nc.vector.reciprocal(da, da))
        link(nc.vector.tensor_tensor(da, da, ex, ALU.mult))
        dve.wait_ge(E["dt_ln"], ns + 1)
        link(nc.vector.tensor_tensor(dt, dt, lnw, ALU.add))
        link(nc.vector.tensor_tensor(da, da, dt, ALU.mult))
        link(nc.vector.scalar_tensor_tensor(out=dt, in0=raw, scalar=0.0, in1=da, op0=ALU.max, op1=ALU.add))
        nc.vector.tensor_scalar(da, dt, hcol[:, 2:3], -1.0, ALU.mult, ALU.mult).then_inc(E["dt_a"], 1)

        def body(g):
            G = g + ns * SSD_GROUPS
            head = isinstance(g, int)

            def ahead(p):
                splitter.ahead(SSD_SLOTS_1 if head else SSD_SLOTS, p, S0 + 2 + g * SSD_TILES + p, U + 2 + g * SSD_TILES + p)

            def conv_of(k, tile_no):
                ahead(k)
                dve.wait_ge(unit_done, U + 3 + g * SSD_TILES + k)
                if not (isinstance(G, int) and G == 0 and k < 2):
                    dve.wait_ge(E["conv_silu"], G * 6 + k - 1)
                conv(dve, link, pj[k % 2], S["conv"][:, k % 2, :], l, tile_no).then_inc(E["conv_ready"], 1)
            conv_of(0, SSD_XT + g)
            if head:
                dve.wait_ge(E["dt_t"], ns + 1)
                nc.vector.tensor_copy(S["tok"], as3(bank[2][:, 0:256], 4)).then_inc(E["dt_tok"], 1)
            conv_of(1, SSD_XT + SSD_GROUPS + g)
            if head:
                dve.wait_ge(E["cum_done"], ns + 1)
                link(nc.vector.tensor_copy(S["acol"], as3(bank[4][:, 0:P], 2)))
                nc.vector.tensor_tensor(S["dst"], bank[4][:, P:P + 64], S["acol"][:, 0, :], ALU.subtract
                                        ).then_inc(E["dst_pre"], 1)
                nc.vector.tensor_copy(arow, bank[3][0:64, 0:T]).then_inc(E["acs_ready"], 1)
                dve.wait_ge(E["acs_ready"], ns + 1)
            conv_of(2, g * 4)
            conv_of(3, g * 4 + 1)
            dve.wait_ge(E["rows_in"], (G + 1) * 16)
            for c in range(2):
                for r in range(SSD_R):
                    ins = nc.vector.scalar_tensor_tensor(
                        out=S["D"][:, c, r, :], in0=S["rows"][:, r, c * P:(c + 1) * P],
                        scalar=S["acol"][:, c, ds(g * SSD_R + r, 1)], in1=C["neg128"], op0=ALU.subtract, op1=ALU.min)
            ins.then_inc(E["diff_ready"], 1)
            if not head:
                ssd_norm(G, g)
            conv_of(4, g * 4 + 2)
            conv_of(5, g * 4 + 3)
            dve.wait_ge(E["cb_done"], G + 1)
            for c in range(2):
                dve.wait_ge(E["d_exp"], G * 2 + c + 1)
                cb = bank[6][:, c * P:(c + 1) * P].rearrange("p (o l) -> p o l", o=1).broadcast_to([P, SSD_R, P])
                nc.vector.tensor_tensor(S["D"][:, c], S["D"][:, c], cb, ALU.mult).then_inc(E["m_ready"], 1)
            ahead(6)
            for c in range(2):
                dve.wait_ge(E["tx_done"], G * 2 + c + 1)
                by = S["tok"][:, c, ds(g * SSD_R, SSD_R)].rearrange("p (r o) -> p r o", o=1).broadcast_to([P, SSD_R, 64])
                nc.vector.tensor_tensor(as3(S["xdt"][:, c, :], SSD_R), as3(bank[2 + c], SSD_R), by, ALU.mult
                                        ).then_inc(E["xdt_ready"], 1)
            dve.wait_ge(E["xdt_ready"], G * 2 + 2)
            if head:
                dve.wait_ge(E["dst_ready"], ns + 1)
            by = S["dst"][:, ds(g * SSD_R, SSD_R)].rearrange("p (r o) -> p r o", o=1).broadcast_to([P, SSD_R, 64])
            nc.vector.tensor_tensor(as3(S["xds"], SSD_R), as3(S["xdt"][:, 0, :], SSD_R), by, ALU.mult
                                    ).then_inc(E["xds_ready"], 1)
            ahead(7)
            ahead(8)
            dve.wait_ge(E["y_done"], G + 1)
            for i in range(4):
                link(nc.vector.scalar_tensor_tensor(
                    out=S["YG"][:, i, :], in0=S["X"][:, i, :], scalar=hd[:, ds(16 + 32 * (l // 3) + g * 4 + i, 1)],
                    in1=bank[4 + i // 2][:, i % 2 * T:(i % 2 + 1) * T], op0=ALU.mult, op1=ALU.add))
            ahead(9)
            for i in range(4):
                dve.wait_ge(E["z_ready"], G * 4 + i + 1)
                nc.vector.tensor_tensor(S["YG"][:, i, :], S["YG"][:, i, :], S["Z"][:, i, :], ALU.mult
                                        ).then_inc(E["yg_ready"], 1)

        def ssd_norm(G, g):
            dve.wait_ge(E["yg_ready"], G * 4)
            dve.wait_ge(E["rstd_ready"], G)
            for i in range(4):
                t = g * 4 - 4 + i
                nc.vector.scalar_tensor_tensor(out=Y[:, t, :], in0=S["YG"][:, i, :], scalar=pcol(l, "norm", t),
                                               in1=S["rstd"], op0=ALU.mult, op1=ALU.mult).then_inc(E["y_ready"], 1)
        body(0)
        with rolled(dve, 1, SSD_GROUPS, [(step, 6 * 3 + 4)]) as g:
            body(g)
        ssd_norm(ns * SSD_GROUPS + SSD_GROUPS, SSD_GROUPS)

    def look_ahead(splitter, l, i, p):
        per = 1 if KINDS[l] == "mla" else 2
        slots = OUT_SLOTS[per * KD]
        if not (l == last_layer and isinstance(i, int) and i == 3 and p >= 4 * per - 2):
            done = i * 4 * per + p
            splitter.ahead(slots, p, first_split[l, "out"] + done, first_unit[l, "out"] + done)

    def gated_ready(eng, l):
        if KINDS[l] == "ssd":
            eng.wait_ge(E["y_ready"], y_base[l] + 32)
        if KINDS[l] == "mla":
            eng.wait_ge(E["o_ready"], 16)
        if KINDS[l] == "gdn":
            eng.wait_ge(E["gy_ready"], 17)

    def act_gated_hi(act, l):
        gated_ready(act, l)
        for c in range(4 if KINDS[l] == "mla" else 8):
            nc.scalar.activation(Y_hi[:, 4 * c:4 * c + 4, :], Y[:, 4 * c:4 * c + 4, :], ACT.Copy).then_inc(E["yhi_ready"], 1)

    def dve_gated_lo(dve, l):
        for c in range(4 if KINDS[l] == "mla" else 8):
            dve.wait_ge(E["yhi_ready"], y_split_base[l] + c + 1)
            nc.vector.tensor_tensor(Y_lo[:, 4 * c:4 * c + 4, :], Y[:, 4 * c:4 * c + 4, :],
                                    Y_hi[:, 4 * c:4 * c + 4, :].bitcast(F32), ALU.subtract).then_inc(E["ysplit"], 1)

    def dve_norm(dve, l, link, step, splitter):
        n = layer_no[l]
        U, per = first_unit[l, "out"], (1 if KINDS[l] == "mla" else 2)
        link(nc.vector.memset(ln["sum"], 0.0))

        def body(i):
            for t in range(4):
                d = ds(i * 4 + t, 1)
                for p in range(t * per, (t + 1) * per):
                    look_ahead(splitter, l, i, p)
                dve.wait_ge(unit_done, U + (i * 4 + t + 1) * per)
                link(nc.vector.scalar_tensor_tensor(out=pre[:, d, :], in0=H_lo[:, d, :].bitcast(F32), scalar=ALPHA,
                                                    in1=pj[t % 2], op0=ALU.mult, op1=ALU.add))
                nc.vector.scalar_tensor_tensor(out=pre[:, d, :], in0=H_hi[:, d, :].bitcast(F32), scalar=ALPHA,
                                               in1=pre[:, d, :], op0=ALU.mult, op1=ALU.add).then_inc(E["pre_ready"], 1)
                dve.wait_ge(E["pre_ready"], KD * n + i * 4 + t + 1)
                link(nc.vector.tensor_tensor(ln["sum"], ln["sum"], pre[:, d, :], ALU.add))
        turns = 4 if l != last_layer else 3
        with rolled(dve, 0, turns, [(step, 8)]) as i:
            body(i)
        if l == last_layer:
            body(3)
        nc.vector.tensor_scalar(ln["sum"], ln["sum"], 1.0 / D, None, ALU.mult).then_inc(E["sum_ready"], 1)
        dve.wait_ge(E["mean_done"], n + 1)
        for k in range(KD):
            nc.vector.tensor_tensor(pre[:, k, :], pre[:, k, :], bank[2][:, 0:T], ALU.subtract
                                    ).then_inc(E["cent_ready"], 1)
        dve.wait_ge(E["cent_ready"], KD * (n + 1))
        dve.wait_ge(E["lrstd_ready"], n + 1)
        for k in range(KD + 2):
            if k < KD:
                nc.vector.scalar_tensor_tensor(out=pre[:, k, :], in0=pre[:, k, :], scalar=pcol(l, "g", k),
                                               in1=ln["rstd"], op0=ALU.mult, op1=ALU.mult).then_inc(E["ln_mul"], 1)
            if k >= 2 and l != last_layer:
                dve.wait_ge(E["hhi_ready"], KD * n + k - 1)
                nc.vector.scalar_tensor_tensor(out=H_lo[:, k - 2, :], in0=pre[:, k - 2, :], scalar=pcol(l, "b", k - 2),
                                               in1=H_hi[:, k - 2, :].bitcast(F32), op0=ALU.add, op1=ALU.subtract
                                               ).then_inc(E["h_ready"], 1)

    def act_rstd(act, link, dst, src, scale, eps):
        link(nc.scalar.activation(dst, src, ACT.Ln, bias=eps, scale=scale))
        return nc.scalar.activation(dst, dst, ACT.Exp, scale=-0.5)

    def act_ssd(act, l, link, astep, splitter):
        ns, S = nth_ssd[l], ssd
        U, S0 = first_unit[l], first_split[l]
        for e in range(2):
            splitter.ahead([0, 1] + SSD_SLOTS_1, e, S0 + e, U + e)
        raw, absx, ex, w1, lnw, dt, da, arow = dtv
        act.wait_ge(E["dt_x"], ns + 1)
        link(nc.scalar.activation(absx, raw, ACT.Abs))
        nc.scalar.activation(ex, absx, ACT.Exp, scale=-1.0).then_inc(E["dt_exp"], 1)
        act.wait_ge(E["dt_w"], ns + 1)
        nc.scalar.activation(lnw, w1, ACT.Ln).then_inc(E["dt_ln"], 1)

        def body(g):
            G = g + ns * SSD_GROUPS
            head = isinstance(g, int)

            def ahead(p):
                splitter.ahead(SSD_SLOTS_1 if head else SSD_SLOTS, p, S0 + 2 + g * SSD_TILES + p, U + 2 + g * SSD_TILES + p)

            def silu_of(k, dst, tile_no):
                ahead(k)
                act.wait_ge(E["conv_ready"], G * 6 + k + 1)
                nc.scalar.activation(dst, S["conv"][:, k % 2, :], ACT.Silu, bias=pcol(l, "cb", tile_no)
                                     ).then_inc(E["conv_silu"], 1)

            def z_of(i):
                ahead(6 + i)
                act.wait_ge(unit_done, U + 3 + g * SSD_TILES + 6 + i)
                nc.scalar.activation(S["Z"][:, i, :], pj[i % 2], ACT.Silu).then_inc(E["z_ready"], 1)
            silu_of(0, S["B"], SSD_XT + g)
            if not head:
                act.wait_ge(E["cdec_ready"], G)
            silu_of(1, S["C"], SSD_XT + SSD_GROUPS + g)
            silu_of(2, S["X"][:, 0, :], g * 4)
            silu_of(3, S["X"][:, 1, :], g * 4 + 1)
            if head:
                act.wait_ge(E["dst_pre"], ns + 1)
                nc.scalar.activation(S["dst"], S["dst"], ACT.Exp).then_inc(E["dst_ready"], 1)
            else:
                act.wait_ge(E["stat_done"], G)
                act_rstd(act, link, S["rstd"], bank[7][:, 0:T], 1.0 / 512, RMS_EPS).then_inc(E["rstd_ready"], 1)
            act.wait_ge(E["diff_ready"], G + 1)
            for c in range(2):
                nc.scalar.activation(S["D"][:, c], S["D"][:, c], ACT.Exp).then_inc(E["d_exp"], 1)
            nc.scalar.activation(S["E"], S["rows"][:, :, P:T], ACT.Exp).then_inc(E["e_exp"], 1)
            silu_of(4, S["X"][:, 2, :], g * 4 + 2)
            silu_of(5, S["X"][:, 3, :], g * 4 + 3)
            z_of(0)
            act.wait_ge(E["bt_done"], G + 1)
            nc.scalar.activation(S["btok"], bank[7][:, 0:P], ACT.Copy).then_inc(E["btok_ready"], 1)
            z_of(1)
            act.wait_ge(E["st_done"], G + 1)
            nc.scalar.activation(S["st"], bank[7], ACT.Copy).then_inc(E["st_ready"], 1)
            z_of(2)
            z_of(3)
            for i in range(4):
                act.wait_ge(E["yg_ready"], G * 4 + i + 1)
                nc.scalar.activation(S["SQ"][:, i, :], S["YG"][:, i, :], ACT.Square).then_inc(E["sq_ready"], 1)
        body(0)
        with rolled(act, 1, SSD_GROUPS, [(astep, 1)] + splitter.steps(SSD_SLOTS)) as g:
            body(g)
        G = (ns + 1) * SSD_GROUPS
        act.wait_ge(E["stat_done"], G)
        act_rstd(act, link, S["rstd"], bank[7][:, 0:T], 1.0 / 512, RMS_EPS).then_inc(E["rstd_ready"], 1)

    def act_norm(act, l, link, astep, splitter):
        n = layer_no[l]
        per = 1 if KINDS[l] == "mla" else 2
        slots = OUT_SLOTS[per * KD]
        turns = 4 if l != last_layer else 3
        with rolled(act, 0, turns, splitter.steps(slots)) as i:
            for p in range(4 * per):
                look_ahead(splitter, l, i, p)
        if l == last_layer:
            for p in range(4 * per):
                look_ahead(splitter, l, 3, p)
        for k in range(KD):
            act.wait_ge(E["cent_ready"], KD * n + k + 1)
            if k >= 2:
                act.wait_ge(E["csq_used"], KD * n + k - 1)
            nc.scalar.activation(ln["sq"][:, k % 2, :], pre[:, k, :], ACT.Square).then_inc(E["csq_ready"], 1)
        act.wait_ge(E["csq_used"], KD * (n + 1))
        act_rstd(act, link, ln["rstd"], bank[3][:, 0:T], 1.0 / D, LN_EPS).then_inc(E["lrstd_ready"], 1)
        for k in range(KD):
            act.wait_ge(E["ln_mul"], KD * n + k + 1)
            dst, done = (H_hi, E["hhi_ready"]) if l != last_layer else (pre, E["last_ready"])
            nc.scalar.activation(dst[:, k, :], pre[:, k, :], ACT.Identity, bias=pcol(l, "b", k)).then_inc(done, 1)


    mla = {}
    (mla["qkv"], mla["sq"], mla["rs"], mla["kr0"], mla["kr"], mla["cos"], mla["sin"], mla["rt"], mla["kT"], mla["qn"],
     mla["qr0"], mla["qr"], mla["V"], mla["S"], mla["mask"], mla["pT"], mla["mx"], mla["acc"]) = carve(
        (10, T), (10, T), (2, T), (T,), (T,), (T,), (T,), (2, T), (2, T), (2, T),
        (T,), (T,), (2, T), (2, 384), (384,), (2, 384), (16,), (16,))

    def load_mla(sp, l, load, turns_of):
        w = a["mla_in_w"][0]
        U = first_unit[l]
        for p in range(MLA_QT + MLA_KVT):
            load(p % SLOTS, w_tile(w, p * P), U + p)
        for p in (10, 11):
            load(p % SLOTS, w_tile(w, MLA_COL_KR, 64), U + p)
        turns_of(lambda i, p: w_tile(w, MLA_COL_Z + p * P + i * 4 * P), U + 12, Z_SLOTS, Z_SLOTS, 4)
        for p in range(2):
            load(p, w_tile(a["mla_out_w"][0], p * P), first_unit[l, "out"] + p)
        qw = a["mla_q_up_w"][0].rearrange("(k p) n -> p k n", p=P)
        kvw = a["mla_kv_up_w"][0].rearrange("(k p) n -> p k n", p=P)
        dsts = [ring[:, UP_SLOT + e, 0:MLA_QT * 192].rearrange("p (k c) -> p k c", k=MLA_QT) for e in range(2)] \
            + [ring[:, UP_SLOT + 2, :].rearrange("p (k c) -> p k c", k=MLA_KVT)]

        def source(i, p):
            return kvw[:, :, ds(i * 512, 512)] if p == 2 else qw[:, :, ds((2 * i + p) * 192, 192)]
        turns_of(source, U + 28, [2, 3, 4], [2, 3, 4], MLA_H // 2, dst=lambda p: dsts[p], sems=up_landed)

    def pe_mla(pe, l, tile, contract, head_tile, hidden, first_hidden):
        M = mla
        S0 = first_split[l]
        for p in range(10):
            if p >= 2:
                pe.wait_ge(E["qkv_raw"], p - 1)
            tile(p % SLOTS, p, pj[p % 2], hidden, S0 + p, waits=first_hidden(l) if p == 0 else None)
        pe.wait_ge(E["qkv_raw"], 9)
        head_tile(4, pj[0], S0 + 10)

        def z_body(i):
            for p in range(4):
                if isinstance(i, int) and p < 2:
                    pe.wait_ge(E["qkv_raw"], 10)
                    if p == 1:
                        pe.wait_ge(E["kr_raw"], 1)
                else:
                    pe.wait_ge(E["mz_ready"], i * 4 + p - 1)
                tile(Z_SLOTS[p], p, pj[(p + 1) % 2], hidden, S0 + 12 + i * 4 + p)
        z_body(0)
        for j, (i0, i1) in enumerate(((0, MLA_QT), (MLA_QT, 10))):
            for i in range(i0, i1):
                pe.wait_ge(E["qkv_sq"], i + 1)
                mm = nc.tensor.matmul(bank[2 + j][:, 0:T], C["ones"], M["sq"][:, i, :], start=i == i0, stop=i == i1 - 1)
            mm.then_inc(E["qkv_stat"], 1)
        nc.tensor.matmul(bank[4][:, 0:T], C["rot"], M["kr0"], start=True, stop=True).then_inc(E["kr_rot"], 1)
        with pe.Fori(1, 4) as i:
            z_body(i)
        pe.wait_ge(E["qkv_ready"], 10)
        pe.wait_ge(E["kr_ready"], 1)
        pe.wait_ge(E["mz_ready"], 16)

        def attend(h):
            for e in range(2):
                pe.wait_ge(E["p_ready"], h * 2 + e + 1)
                for b in range(3):
                    mm = nc.tensor.transpose(bank[6 + e][:, b * P:(b + 1) * P], M["S"][:, e, b * P:(b + 1) * P], ident)
                mm.then_inc(E["pt_done"], 1)
            for e in range(2):
                pe.wait_ge(E["pt_ready"], h * 2 + e + 1)
                v0, v1 = M["V"][:, 0, e * P:(e + 1) * P], M["V"][:, 1, e * P:(e + 1) * P]
                nc.tensor.matmul(bank[6 + e][:, 0:P], v0, M["pT"][:, e, 0:P], start=True, stop=True)
                nc.tensor.matmul(bank[6 + e][:, P:T], v0, M["pT"][:, e, P:T], start=True, stop=False)
                nc.tensor.matmul(bank[6 + e][:, P:T], v1, M["pT"][:, e, T:T + P], start=False, stop=True
                                 ).then_inc(E["pv_done"], 1)

        def body(h):
            first = isinstance(h, int)
            for e in range(2):
                pe.wait_ge(up_landed[e], (h + 1) * 16)
                w = ring[:, UP_SLOT + e, 0:MLA_QT * 192].rearrange("p (k c) -> p k c", k=MLA_QT)
                for k in range(MLA_QT):
                    nc.tensor.matmul(bank[2 + e][:, 0:T], w[:, k, 0:P], M["qkv"][:, k, :], start=k == 0, stop=k == MLA_QT - 1)
                for k in range(MLA_QT):
                    mm = nc.tensor.matmul(bank[4][64 * e:64 * e + 64, 0:T], w[:, k, P:P + 64], M["qkv"][:, k, :],
                                          start=k == 0, stop=k == MLA_QT - 1)
                mm.then_inc(unit_done, 1)
            pe.wait_ge(up_landed[2], (h + 1) * 16)
            w = ring[:, UP_SLOT + 2, :].rearrange("p (k c) -> p k c", k=MLA_KVT)
            for e in range(2):
                for k in range(MLA_KVT):
                    mm = nc.tensor.matmul(pj[e], w[:, k, e * T:e * T + P], M["qkv"][:, MLA_QT + k, :],
                                          start=k == 0, stop=k == MLA_KVT - 1)
                mm.then_inc(E["up_done"], 1)
            pe.wait_ge(E["qr_raw"], h + 1)
            nc.tensor.matmul(bank[4][:, T:2 * T], C["rot"], M["qr0"], start=True, stop=True).then_inc(E["rot_done"], 1)
            if not first:
                attend(h - 1)
            wv = w.rearrange("p k (e c) -> p k e c", e=2)
            for c in range(2):
                for k in range(MLA_KVT):
                    mm = nc.tensor.matmul(bank[5][:, c * T:(c + 1) * T], M["qkv"][:, MLA_QT + k, c * P:(c + 1) * P],
                                          wv[:, k, :, P:T], start=k == 0, stop=k == MLA_KVT - 1)
            mm.then_inc(unit_done, 1)
            pe.wait_ge(E["qr_ready"], h + 1)
            for e in range(2):
                pe.wait_ge(E["kt_ready"], h * 2 + e + 1)
                pe.wait_ge(E["qn_ready"], h * 2 + e + 1)
                if not first:
                    pe.wait_ge(E["o_ready"], h * 2 - 1 + e)
                r0 = 64 * e
                for qt, (c0, n) in enumerate(((0, P), (P, T))):
                    nc.tensor.matmul(bank[6 + e][:, c0:c0 + n], M["qn"][:, e, qt * P:(qt + 1) * P], M["kT"][:, e, 0:n],
                                     start=True, stop=False)
                    mm = nc.tensor.matmul(bank[6 + e][:, c0:c0 + n], M["qr"][r0:r0 + 64, qt * P:(qt + 1) * P],
                                          M["kr"][r0:r0 + 64, 0:n], start=False, stop=True)
                mm.then_inc(E["sc_done"], 1)
        body(0)
        with pe.Fori(1, MLA_H // 2) as h:
            body(h)
        attend(MLA_H // 2 - 1)

    def dve_mla(dve, l, link, step, splitter):
        M = mla
        U, S0 = first_unit[l], first_split[l]
        if layer_no[l]:
            dve.wait_ge(E["h_ready"], KD * layer_no[l])
        ang, n1 = M["S"][:, 0, 0:T], M["S"][:, 1, 0:T]
        link(nc.vector.tensor_copy(n1, posi[:]))
        link(nc.vector.tensor_scalar(ang, n1, inv_freq, None, ALU.mult))
        for dst, quarter in ((M["sin"], 0.0), (M["cos"], 0.25)):
            link(nc.vector.tensor_scalar(n1, ang, 1.0 / (2 * np.pi), quarter, ALU.mult, ALU.add))
            link(nc.vector.tensor_scalar(n1, n1, MAGIC, -MAGIC, ALU.add, ALU.add))
            link(nc.vector.scalar_tensor_tensor(out=dst, in0=n1, scalar=-TWO_PI_A, in1=ang, op0=ALU.mult, op1=ALU.add))
            link(nc.vector.scalar_tensor_tensor(out=dst, in0=n1, scalar=-TWO_PI_B, in1=dst, op0=ALU.mult, op1=ALU.add))
            link(nc.vector.scalar_tensor_tensor(out=dst, in0=n1, scalar=-TWO_PI_C, in1=dst, op0=ALU.mult, op1=ALU.add))
            link(nc.vector.tensor_scalar(dst, dst, 2 * np.pi * quarter, 3.1415925, ALU.add, ALU.min))
            nc.vector.tensor_scalar(dst, dst, -3.1415925, None, ALU.max).then_inc(E["trig_arg"], 1)
        nc.vector.tensor_copy(M["mask"][:, 0:P], C["negq"]).then_inc(E["mask_ready"], 1)
        nc.vector.memset(M["mask"][:, P:T], 0.0).then_inc(E["mask_ready"], 1)
        nc.vector.tensor_copy(M["mask"][:, T:T + P], C["negq"]).then_inc(E["mask_ready"], 1)
        for p in range(10):
            splitter.ahead(MLA_SLOTS, p, S0 + p, U + p)
            dve.wait_ge(unit_done, U + p + 1)
            nc.vector.tensor_copy(M["qkv"][:, p, :], pj[p % 2]).then_inc(E["qkv_raw"], 1)
        for p in (10, 11):
            splitter.ahead(MLA_SLOTS, p, S0 + p, U + p)
        dve.wait_ge(unit_done, U + 12)
        nc.vector.tensor_copy(M["kr0"], pj[0]).then_inc(E["kr_raw"], 1)
        for p in range(4):
            splitter.ahead(Z_SLOTS, p, S0 + 12 + p, U + 12 + p)

        def rotary(dst, x, rot):
            link(nc.vector.tensor_tensor(M["rt"][:, 0, :], rot, M["sin"], ALU.mult))
            link(nc.vector.tensor_tensor(M["rt"][:, 1, :], x, M["cos"], ALU.mult))
            return nc.vector.tensor_tensor(dst, M["rt"][:, 0, :], M["rt"][:, 1, :], ALU.add)
        dve.wait_ge(E["kr_rot"], 1)
        dve.wait_ge(E["trig"], 2)
        rotary(M["kr"], M["kr0"], bank[4][:, 0:T]).then_inc(E["kr_ready"], 1)
        for i in range(10):
            j = int(i >= MLA_QT)
            dve.wait_ge(E["qkv_rstd"], j + 1)
            nc.vector.scalar_tensor_tensor(out=M["qkv"][:, i, :], in0=M["qkv"][:, i, :],
                                           scalar=pcol(l, "kvn" if j else "qn", i - MLA_QT * j), in1=M["rs"][:, j, :],
                                           op0=ALU.mult, op1=ALU.mult).then_inc(E["qkv_ready"], 1)
        with dve.Fori(1, 4) as i:
            for p in range(4):
                splitter.ahead(Z_SLOTS, p, S0 + 12 + i * 4 + p, U + 12 + i * 4 + p)

        def gate(h):
            for e in range(2):
                dve.wait_ge(E["pv_done"], h * 2 + e + 1)
                nc.vector.tensor_tensor(Y[:, ds(h * 2 + e, 1), :], bank[6 + e][:, 0:T], Y[:, ds(h * 2 + e + 16, 1), :],
                                        ALU.mult).then_inc(E["o_ready"], 1)

        def body(h):
            for e in range(2):
                dve.wait_ge(E["up_done"], h * 2 + e + 1)
                nc.vector.tensor_copy(M["kT"][:, e, :], pj[e]).then_inc(E["kt_ready"], 1)
            dve.wait_ge(E["rot_done"], h + 1)
            rotary(M["qr"], M["qr0"], bank[4][:, T:2 * T]).then_inc(E["qr_ready"], 1)
            if not isinstance(h, int):
                gate(h - 1)
            for e in range(2):
                mx = M["mx"][:, 4 * e:4 * e + 2]
                dve.wait_ge(E["sc_done"], h * 2 + e + 1)
                link(nc.vector.tensor_tensor(M["S"][:, e, :], bank[6 + e][:, 0:384], M["mask"], ALU.add))
                link(nc.vector.tensor_reduce(mx[:, 0:1], M["S"][:, e, 0:P], AX.X, ALU.max))
                link(nc.vector.tensor_reduce(mx[:, 1:2], M["S"][:, e, P:384], AX.X, ALU.max))
                nc.vector.tensor_scalar(M["mx"][:, 4 * e + 2:4 * e + 4], mx, -MLA_SCALE, None, ALU.mult
                                        ).then_inc(E["sc_max"], 1)
            for e in range(2):
                dve.wait_ge(E["p_exp"], h * 2 + e + 1)
                link(nc.vector.reciprocal(M["acc"][:, 4 * e + 2:4 * e + 4], M["acc"][:, 4 * e:4 * e + 2]))
                link(nc.vector.tensor_scalar(M["S"][:, e, 0:P], M["S"][:, e, 0:P], M["acc"][:, 4 * e + 2:4 * e + 3], None,
                                             ALU.mult))
                nc.vector.tensor_scalar(M["S"][:, e, P:384], M["S"][:, e, P:384], M["acc"][:, 4 * e + 3:4 * e + 4], None,
                                        ALU.mult).then_inc(E["p_ready"], 1)
        body(0)
        with rolled(dve, 1, MLA_H // 2, [(step, 12)]) as h:
            body(h)
        gate(MLA_H // 2 - 1)

    def act_mla(act, l, link, astep, splitter):
        M = mla
        U, S0 = first_unit[l], first_split[l]
        U2 = U + 12 + 16
        for i, dst in enumerate((M["sin"], M["cos"])):
            act.wait_ge(E["trig_arg"], i + 1)
            nc.scalar.activation(dst, dst, ACT.Sin).then_inc(E["trig"], 1)
        for i in range(10):
            splitter.ahead(MLA_SLOTS, i, S0 + i, U + i)
            act.wait_ge(E["qkv_raw"], i + 1)
            nc.scalar.activation(M["sq"][:, i, :], M["qkv"][:, i, :], ACT.Square).then_inc(E["qkv_sq"], 1)
        for p in (10, 11):
            splitter.ahead(MLA_SLOTS, p, S0 + p, U + p)

        def z_body(i):
            for p in range(4):
                splitter.ahead(Z_SLOTS, p, S0 + 12 + i * 4 + p, U + 12 + i * 4 + p)
                act.wait_ge(unit_done, U + 12 + i * 4 + p + 1)
                nc.scalar.activation(Y[:, ds(i * 4 + (16 + p), 1), :], pj[(p + 1) % 2], ACT.Silu).then_inc(E["mz_ready"], 1)
        z_body(0)
        for j, n in enumerate((MLA_QR, MLA_KVR)):
            act.wait_ge(E["qkv_stat"], j + 1)
            act_rstd(act, link, M["rs"][:, j, :], bank[2 + j][:, 0:T], 1.0 / n, RMS_EPS).then_inc(E["qkv_rstd"], 1)
        with rolled(act, 1, 4, splitter.steps(Z_SLOTS)) as i:
            z_body(i)

        def probs_t(h):
            for e in range(2):
                act.wait_ge(E["pt_done"], h * 2 + e + 1)
                nc.scalar.activation(M["pT"][:, e, :], bank[6 + e][:, 0:384], ACT.Copy).then_inc(E["pt_ready"], 1)

        def body(h):
            for e in range(2):
                act.wait_ge(unit_done, U2 + h * 3 + e + 1)
                nc.scalar.activation(M["qn"][:, e, :], bank[2 + e][:, 0:T], ACT.Copy).then_inc(E["qn_ready"], 1)
            nc.scalar.activation(M["qr0"], bank[4][:, 0:T], ACT.Copy).then_inc(E["qr_raw"], 1)
            if not isinstance(h, int):
                probs_t(h - 1)
            act.wait_ge(unit_done, U2 + h * 3 + 3)
            nc.scalar.activation(M["V"], as3(bank[5], 2), ACT.Copy).then_inc(E["v_ready"], 1)
            for e in range(2):
                act.wait_ge(E["sc_max"], h * 2 + e + 1)
                link(nc.scalar.activation(M["S"][:, e, 0:P], M["S"][:, e, 0:P], ACT.Exp, scale=MLA_SCALE,
                                          bias=M["mx"][:, 4 * e + 2:4 * e + 3], accum_out=M["acc"][:, 4 * e:4 * e + 1]))
                nc.scalar.activation(M["S"][:, e, P:384], M["S"][:, e, P:384], ACT.Exp, scale=MLA_SCALE,
                                     bias=M["mx"][:, 4 * e + 3:4 * e + 4], accum_out=M["acc"][:, 4 * e + 1:4 * e + 2]
                                     ).then_inc(E["p_exp"], 1)
        body(0)
        with rolled(act, 1, MLA_H // 2, [(astep, 2)]) as h:
            body(h)
        probs_t(MLA_H // 2 - 1)

    gdn = {}
    (gdn["conv"], gdn["qk"], gdn["v"], gdn["sqk"], gdn["rs"], gdn["qkn"], gdn["rows"], gdn["D"], gdn["A"], gdn["kbe"],
     gdn["kdec"], gdn["vb"], gdn["vn"], gdn["S"], gdn["eg"], gdn["qdec"], gdn["sc"], gdn["tok"], gdn["gcol"],
     gdn["lev"], gdn["U"], gdn["T"], gdn["PM"], gdn["osq"]) = carve(
        (2, T), (2, T), (2, T), (2, T), (2, T), (2, T), (4, T), (4, P), (4, P), (4, P),
        (4, P), (4, P), (2, P), (2, P), (2, T), (2, T), (3, 2, 32), (2, 64), (2, 32),
        (2, 4 * P), (4, P), (4, P), (4, P), (2, T))
    gdn["lev"] = gdn["lev"].rearrange("p n (x l) -> p n x l", x=4)
    gdn["wT"], gdn["u"], gdn["ors"] = gdn["kbe"], gdn["vb"], gdn["rs"]
    gba = [gdn[n][0:64].rearrange("p x l -> p (x l)")[:, 0:T] for n in ("kbe", "kdec", "vb", "U", "PM", "A")]

    GDN_PLAN = {0: "grams", 1: "turns", 4: "inv0", 15: "wu", 16: "out0", 23: "norm"}
    for n in range(5):
        GDN_PLAN[5 + 2 * n], GDN_PLAN[6 + 2 * n] = f"left{n}", f"right{n}"
    for c in (1, 2, 3):
        GDN_PLAN[15 + 2 * c], GDN_PLAN[16 + 2 * c] = f"new{c}", f"out{c}"
    STATS_AT = 10

    def load_gdn(sp, l, load, turns_of):
        w, scr = a["gdn_in_w"][0], a["scr_gdn"]
        for p in range(2):
            load(p, w_tile(w, GDN_COL_B, 64), first_unit[l] + p)

        def rows_of(j):
            row = 2 * j if isinstance(j, int) else sp.snap(2 * j)
            if not isinstance(j, int):
                sp.wait_ge(unit_done, 1)
                sp.wait_ge(E["rows_used"], j)
                sp.wait_ge(E["eg_ready"], j)
            for half in range(2):
                sp.dma_start(gdn["rows"][:, 2 * half:2 * half + 2, :],
                             scr[ds(row + half * GDN_HV, 2), :].partition_broadcast(P)).then_inc(E["grows_in"], 16)

        def source(j, p):
            return w_tile(w, [j * P, GDN_COL_K + j * P, GDN_COL_V + j * T, GDN_COL_V + P + j * T, GDN_COL_Z + j * T,
                              GDN_COL_Z + P + j * T][p])

        def beside(j, p):
            if p < 5:
                return
            if isinstance(j, int):
                sp.wait_ge(E["gscr_ready"], 1)
                sp.dma_start(scr[0:32, :], gba[4][0:32]).then_inc(E["gscr_out"], 16)
                sp.dma_start(scr[32:64, :], gba[5][0:32]).then_inc(E["gscr_out"], 16)
                sp.wait_ge(E["gscr_out"], 32)
            rows_of(j)
        turns_of(source, first_unit[l] + 2, GDN_SLOTS_1, GDN_SLOTS, GDN_HK, beside)

    def pe_gdn(pe, l, tile, contract, head_tile, hidden, first_hidden):
        S = gdn

        def halves(c):
            return c // 2, slice(64 * (c % 2), 64 * (c % 2) + 64)

        def chain(name, j):
            n = int(name[-1]) if name[-1].isdigit() else 0
            step = name.rstrip("0123456789")
            b2, b3, b4, b5, b6, b7 = (as3(bank[i], 4) for i in range(2, 8))
            if step == "grams":
                pe.wait_ge(E["nrm_ready"], 2 * (j + 1))
                for c in range(2):
                    cc = slice(c * P, (c + 1) * P)
                    nc.tensor.matmul(b2[:, c, :], S["qkn"][:, 1, cc], S["qkn"][:, 1, cc], start=True, stop=True)
                    mm = nc.tensor.matmul(b2[:, 2 + c, :], S["qkn"][:, 1, cc], S["qkn"][:, 0, cc], start=True, stop=True)
                mm.then_inc(E["kk_done"], 1)
            if step == "turns":
                pe.wait_ge(E["gy_ready"], j + 1)
                for c in range(2):
                    mm = nc.tensor.transpose(b3[:, c, :], S["qkn"][:, 1, c * P:(c + 1) * P], ident)
                mm.then_inc(E["kt_done"], 1)
                pe.wait_ge(E["gconv_silu"], 4 * (j + 1))
                for e in range(2):
                    for c in range(2):
                        mm = nc.tensor.transpose(b4[:, 2 * e + c, :], S["v"][:, e, c * P:(c + 1) * P], ident)
                mm.then_inc(E["vt_done"], 1)
            if step == "inv":
                pe.wait_ge(E["u_ready"], 6 * j + 1)
                for x in range(4):
                    mm = nc.tensor.transpose(b5[:, x, :], S["U"][:, x, :], ident)
                mm.then_inc(E["t0_done"], 1)
            if step == "left":
                pe.wait_ge(E["t_ready"], 5 * j + n + 1)
                pe.wait_ge(E["lev_ready"], 5 * j + n + 1)
                for x in range(4):
                    mm = nc.tensor.matmul(b5[:, x, :], S["lev"][:, n % 2, x, :], S["T"][:, x, :], start=True, stop=True)
                mm.then_inc(E["left_done"], 1)
            if step == "right":
                pe.wait_ge(E["pm_ready"], 5 * j + n + 1)
                for x in range(4):
                    mm = nc.tensor.matmul(b7[:, x, :], S["PM"][:, x, :], S["U"][:, x, :], start=True, stop=True)
                mm.then_inc(E["ru_done"], 1)
                if n < 4:
                    for x in range(4):
                        mm = nc.tensor.matmul(b6[:, x, :], S["U"][:, x, :], S["PM"][:, x, :], start=True, stop=True)
                    mm.then_inc(E["rt_done"], 1)
            if step == "wu":
                pe.wait_ge(E["u_ready"], 6 * j + 6)
                pe.wait_ge(E["kbe_ready"], j + 1)
                for x in range(4):
                    mm = nc.tensor.matmul(b5[:, x, :], S["kbe"][:, x, :], S["U"][:, x, :], start=True, stop=True)
                mm.then_inc(E["w_done"], 1)
                pe.wait_ge(E["vb_ready"], j + 1)
                for x in range(4):
                    mm = nc.tensor.matmul(b6[:, x, :], S["U"][:, x, :], S["vb"][:, x, :], start=True, stop=True)
                mm.then_inc(E["uv_done"], 1)
            if step == "new":
                c, h = halves(n)
                pe.wait_ge(E["s_ready"], 6 * j + 2 * n)
                for e in range(2):
                    mm = nc.tensor.matmul(b7[h, e, :], S["wT"][:, 2 * e + c, h], S["S"][:, e, :], start=True, stop=True)
                mm.then_inc(E["ws_done"], 1)
            if step == "out":
                c, h = halves(n)
                pe.wait_ge(E["vn_ready"], 4 * j + n + 1)
                if n == 0:
                    pe.wait_ge(E["qdec_ready"], 2 * (j + 1))
                    pe.wait_ge(E["kdec_ready"], j + 1)
                if n < 3:
                    for e in range(2):
                        mm = nc.tensor.matmul(b4[:, e, :], S["kdec"][h, 2 * e + c, :], S["vn"][h, e, :], start=True, stop=True)
                    mm.then_inc(E["ds_done"], 1)
                for e in range(2):
                    o = bank[3][:, e * T + n * 64:e * T + n * 64 + 64]
                    if n:
                        nc.tensor.matmul(o, S["S"][:, e, :], S["qdec"][:, e, n * 64:n * 64 + 64], start=True, stop=False)
                    mm = nc.tensor.matmul(o, S["vn"][h, e, :], S["D"][h, 2 * e + c, h], start=n == 0, stop=True)
                mm.then_inc(E["os_done"], 1)
            if step == "norm":
                pe.wait_ge(E["osq_ready"], j + 1)
                nc.tensor.matmul(bank[7], C["ones"], S["osq"].rearrange("p e t -> p (e t)"), start=True, stop=True
                                 ).then_inc(E["ostat_done"], 1)

        def body(j):
            first = isinstance(j, int)
            slots = GDN_SLOTS_1 if first else GDN_SLOTS
            for q in range(4 * GDN_TILES):
                p = q // 4
                if not first and q in GDN_PLAN:
                    chain(GDN_PLAN[q], j - 1)
                if q == STATS_AT:
                    pe.wait_ge(E["sqk_ready"], 2 * (j + 1))
                    nc.tensor.matmul(bank[2], C["ones"], S["sqk"].rearrange("p e t -> p (e t)"), start=True, stop=True
                                     ).then_inc(E["nstat_done"], 1)
                if q % 4 == 0:
                    if p < 2:
                        if first:
                            if p == 1:
                                pe.wait_ge(E["ba_raw"], 1)
                        else:
                            pe.wait_ge(E["gz_ready"], 2 * j - 1 + p)
                    elif p < 6:
                        pe.wait_ge(E["gconv_ready"], 4 * j + p - 1)
                mm = contract(slots[p], p, pj[p % 2], hidden, range(4 * (q % 4), 4 * (q % 4) + 4),
                              s=first_split[l] + 2 + j * GDN_TILES + p)
                if q % 4 == 3:
                    mm.then_inc(unit_done, 1)
                if first and q == 7:
                    pe.wait_ge(E["ba_ready"], 1)
                    for c in range(2):
                        mm = nc.tensor.transpose(bank[2][:, c * 64:(c + 1) * 64], gba[5][:, c * P:(c + 1) * P],
                                                 ident[0:64, 0:64])
                    mm.then_inc(E["ba_t"], 1)
                if first and q == 13:
                    pe.wait_ge(E["ba_tok"], 1)
                    for c in range(2):
                        nc.tensor.matmul(bank[5][0:32, c * P:(c + 1) * P], S["tok"][:, c, 32:64], C["tri64"],
                                         start=True, stop=True)
                    nc.tensor.matmul(bank[6][:, 0:64], C["tri64"], S["tok"][:, :, 32:64], start=True, stop=True)
                    nc.tensor.matmul(bank[6][:, 64:128], C["blk64"], S["tok"][:, :, 32:64], start=True, stop=True
                                     ).then_inc(E["gc_done"], 1)

        head_tile(0, pj[1], first_split[l], first_hidden(l))
        body(0)
        with pe.Fori(1, GDN_HK) as j:
            body(j)
        for q in sorted(GDN_PLAN):
            chain(GDN_PLAN[q], GDN_HK - 1)

    def gdn_ahead(splitter, l, j, p):
        splitter.ahead(GDN_SLOTS_1 if isinstance(j, int) else GDN_SLOTS, p, first_split[l] + 2 + j * GDN_TILES + p,
                       first_unit[l] + 2 + j * GDN_TILES + p)

    def dve_gdn(dve, l, link, step, splitter):
        S = gdn
        U, S0 = first_unit[l], first_split[l]
        flat = lambda ap: ap.rearrange("p x l -> p (x l)")
        if layer_no[l]:
            dve.wait_ge(E["h_ready"], KD * layer_no[l])
        raw, ab, ex, w1, sig, bg = gba
        lnw = S["osq"][0:64, 0, :]
        da, dt = S["ors"][0:64, 0, :], S["ors"][0:64, 1, :]
        sg = S["osq"][0:32, 1, :]
        nc.vector.memset(hd[:, 15:16], 0.0).then_inc(E["gy_ready"], 1)
        for e in range(2):
            splitter.ahead([0, 1] + GDN_SLOTS_1, e, S0 + e, U + e)
        dve.wait_ge(unit_done, U + 2)
        nc.vector.tensor_scalar(raw, pj[1][0:64], hd[0:64, 8:9], None, ALU.add).then_inc(E["ba_raw"], 1)
        dve.wait_ge(E["ba_exp"], 1)
        nc.vector.tensor_scalar(w1, ex, 1.0, None, ALU.add).then_inc(E["ba_w"], 1)
        dve.wait_ge(E["ba_w"], 1)
        link(nc.vector.tensor_scalar(dt, w1, 1.0, 0.0, ALU.subtract, ALU.is_equal))
        link(nc.vector.scalar_tensor_tensor(out=da, in0=w1, scalar=-1.0, in1=dt, op0=ALU.add, op1=ALU.add))
        link(nc.vector.reciprocal(da, da))
        link(nc.vector.tensor_tensor(da, da, ex, ALU.mult))
        dve.wait_ge(E["ba_ln"], 1)
        link(nc.vector.tensor_tensor(dt, dt, lnw, ALU.add))
        link(nc.vector.tensor_tensor(da, da, dt, ALU.mult))
        link(nc.vector.scalar_tensor_tensor(out=dt, in0=raw, scalar=0.0, in1=da, op0=ALU.max, op1=ALU.add))
        link(nc.vector.tensor_scalar(bg[32:64], dt[32:64], hd[32:64, 10:11], -1.0, ALU.mult, ALU.mult))
        dve.wait_ge(E["ba_sig"], 1)
        link(nc.vector.tensor_scalar(sg, sg, 1.0, None, ALU.add))
        nc.vector.reciprocal(bg[0:32], sg).then_inc(E["ba_ready"], 1)

        def respond(name, j):
            n = int(name[-1]) if name[-1].isdigit() else 0
            kind = name.rstrip("0123456789")
            b2, b3, b4, b5, b6, b7 = (as3(bank[i], 4) for i in range(2, 8))
            if kind == "grams":
                dve.wait_ge(E["grows_in"], 32 * (j + 1))
                for e in range(2):
                    for c in range(2):
                        ins = nc.vector.scalar_tensor_tensor(
                            out=S["D"][:, 2 * e + c, :], in0=S["rows"][:, e, c * P:(c + 1) * P],
                            scalar=S["gcol"][:, c, ds(2 * j + e, 1)], in1=C["neg64"], op0=ALU.subtract, op1=ALU.min)
                ins.then_inc(E["gdiff_ready"], 1)
                dve.wait_ge(E["kk_done"], j + 1)
                dve.wait_ge(E["gdecay"], j + 1)
                D4 = S["D"].rearrange("p (e c) l -> p e c l", e=2)
                A4 = S["A"].rearrange("p (e c) l -> p e c l", e=2)
                for e in range(2):
                    ins = nc.vector.tensor_tensor(A4[:, e], D4[:, e], b2[:, 0:2, :], ALU.mult)
                link(ins)
                for e in range(2):
                    ins = nc.vector.tensor_tensor(D4[:, e], D4[:, e], b2[:, 2:4, :], ALU.mult)
                link(nc.vector.tensor_tensor(flat(S["A"]), flat(S["A"]), S["rows"][:, 2:4, :].rearrange("p e t -> p (e t)"),
                                             ALU.mult))
                nc.vector.tensor_copy(S["vn"][:, 0, 0:1], S["A"][:, 0, 0:1]).then_inc(E["rows_used"], 1)
                lev1 = C["lev1"].rearrange("p (o l) -> p o l", o=1).broadcast_to([P, 4, P])
                idb = ident.rearrange("p (o l) -> p o l", o=1).broadcast_to([P, 4, P])
                link(nc.vector.tensor_tensor(S["U"], S["A"], lev1, ALU.mult))
                nc.vector.tensor_tensor(S["U"], idb, S["U"], ALU.subtract).then_inc(E["u_ready"], 1)
            if kind == "turns":
                dve.wait_ge(E["kt_done"], j + 1)
                for e in range(2):
                    for c in range(2):
                        ins = nc.vector.tensor_scalar(S["kbe"][:, 2 * e + c, :], b3[:, c, :],
                                                      S["sc"][:, 0, c, ds(2 * j + e, 1)], None, ALU.mult)
                ins.then_inc(E["kbe_ready"], 1)
                for e in range(2):
                    for c in range(2):
                        ins = nc.vector.tensor_scalar(S["kdec"][:, 2 * e + c, :], b3[:, c, :],
                                                      S["sc"][:, 1, c, ds(2 * j + e, 1)], None, ALU.mult)
                ins.then_inc(E["kdec_ready"], 1)
                dve.wait_ge(E["vt_done"], j + 1)
                for e in range(2):
                    for c in range(2):
                        ins = nc.vector.tensor_scalar(S["vb"][:, 2 * e + c, :], b4[:, 2 * e + c, :],
                                                      S["tok"][:, c, ds(2 * j + e, 1)], None, ALU.mult)
                ins.then_inc(E["vb_ready"], 1)
                dve.wait_ge(E["eg_ready"], j + 1)
                for e in range(2):
                    nc.vector.tensor_tensor(S["qdec"][:, e, :], S["qkn"][:, 0, :], S["eg"][:, e, :], ALU.mult
                                            ).then_inc(E["qdec_ready"], 1)
            if kind == "inv":
                dve.wait_ge(E["t0_done"], j + 1)
                nc.vector.tensor_copy(flat(S["T"]), bank[5]).then_inc(E["t_ready"], 1)
            if kind == "left":
                dve.wait_ge(E["left_done"], 5 * j + n + 1)
                nc.vector.tensor_copy(flat(S["PM"]), bank[5]).then_inc(E["pm_ready"], 1)
            if kind == "right":
                dve.wait_ge(E["ru_done"], 5 * j + n + 1)
                if n < 4:
                    dve.wait_ge(E["rt_done"], 4 * j + n + 1)
                    nc.vector.tensor_tensor(flat(S["T"]), flat(S["T"]), bank[6], ALU.subtract).then_inc(E["t_ready"], 1)
                nc.vector.tensor_tensor(flat(S["U"]), flat(S["U"]), bank[7], ALU.subtract).then_inc(E["u_ready"], 1)
            if kind == "wu":
                dve.wait_ge(E["w_done"], j + 1)
                link(nc.vector.tensor_copy(flat(S["wT"]), bank[5]))
                dve.wait_ge(E["uv_done"], j + 1)
                nc.vector.tensor_copy(flat(S["u"]), bank[6]).then_inc(E["u2_ready"], 1)
                dve.wait_ge(E["u2_ready"], j + 1)
                us = S["u"].rearrange("p (e c) l -> p e c l", e=2)
                nc.vector.tensor_copy(S["vn"][0:64], us[0:64, :, 0, :]).then_inc(E["vn_ready"], 1)
            if kind == "new":
                c, h = n // 2, slice(64 * (n % 2), 64 * (n % 2) + 64)
                us = S["u"].rearrange("p (e c) l -> p e c l", e=2)
                dve.wait_ge(E["ws_done"], 3 * j + n)
                nc.vector.tensor_tensor(S["vn"][h], us[h, :, c, :], b7[h, 0:2, :], ALU.subtract).then_inc(E["vn_ready"], 1)
            if kind == "out" and n < 3:
                dve.wait_ge(E["ds_done"], 3 * j + n + 1)
                dve.wait_ge(E["os_done"], 4 * j + n + 1)
                for e in range(2):
                    last = n * 64 + 63
                    if n == 0:
                        nc.vector.tensor_copy(S["S"][:, e, :], b4[:, e, :]).then_inc(E["s_ready"], 1)
                    else:
                        nc.vector.scalar_tensor_tensor(out=S["S"][:, e, :], in0=S["S"][:, e, :],
                                                       scalar=S["eg"][:, e, last:last + 1], in1=b4[:, e, :],
                                                       op0=ALU.mult, op1=ALU.add).then_inc(E["s_ready"], 1)
            if kind == "norm":
                dve.wait_ge(E["ors_ready"], j + 1)
                link(nc.vector.scalar_tensor_tensor(out=flat(S["osq"]), in0=bank[3], scalar=pcol(l, "norm", 0),
                                                    in1=flat(S["ors"]), op0=ALU.mult, op1=ALU.mult))
                dve.wait_ge(E["gz_ready"], 2 * (j + 1))
                yy = Y[:, ds(2 * j, 2), :]
                nc.vector.tensor_tensor(yy, S["osq"], yy, ALU.mult).then_inc(E["gy_ready"], 1)

        def body(j):
            first = isinstance(j, int)
            for q in range(4 * GDN_TILES + 1):
                if q and q % 4 == 0:
                    gdn_ahead(splitter, l, j, q // 4 - 1)
                if not first and q in GDN_PLAN:
                    respond(GDN_PLAN[q], j - 1)
                if q == STATS_AT:
                    dve.wait_ge(E["rs_ready"], j + 1)
                    nc.vector.scalar_tensor_tensor(out=S["qkn"][:, 0, :], in0=S["qk"][:, 0, :], scalar=P ** -0.5,
                                                   in1=S["rs"][:, 0, :], op0=ALU.mult, op1=ALU.mult
                                                   ).then_inc(E["nrm_ready"], 1)
                    nc.vector.tensor_tensor(S["qkn"][:, 1, :], S["qk"][:, 1, :], S["rs"][:, 1, :], ALU.mult
                                            ).then_inc(E["nrm_ready"], 1)
                if first and q == 7:
                    dve.wait_ge(E["ba_t"], 1)
                    nc.vector.tensor_copy(S["tok"], as3(bank[2][:, 0:P], 2)).then_inc(E["ba_tok"], 1)
                if first and q == 13:
                    dve.wait_ge(E["gc_done"], 1)
                    link(nc.vector.tensor_copy(S["gcol"], as3(bank[6][:, 0:64], 2)))
                    nc.vector.tensor_tensor(S["sc"][:, 1], as3(bank[6][:, 64:128], 2), S["gcol"], ALU.subtract
                                            ).then_inc(E["gsc_pre"], 1)
                    nc.vector.tensor_copy(gba[4][0:32], bank[5][0:32, 0:T]).then_inc(E["gscr_ready"], 1)
                    dve.wait_ge(E["gsc_exp"], 2)
                    link(nc.vector.tensor_tensor(S["sc"][:, 0], S["sc"][:, 0], S["tok"][:, :, 0:32], ALU.mult))
                if q % 4 == 0 and 4 <= q <= 16:
                    p = q // 4 - 1
                    dve.wait_ge(unit_done, U + 3 + j * GDN_TILES + p)
                    if not (first and p < 2):
                        dve.wait_ge(E["gconv_silu"], 4 * j + p - 1)
                    tile_no = [j, GDN_HK + j, 2 * GDN_HK + 2 * j, 2 * GDN_HK + 2 * j + 1][p]
                    conv(dve, link, pj[p % 2], S["conv"][:, p % 2, :], l, tile_no).then_inc(E["gconv_ready"], 1)
        body(0)
        with rolled(dve, 1, GDN_HK, [(step, 17)]) as j:
            body(j)
        for q in sorted(GDN_PLAN):
            respond(GDN_PLAN[q], GDN_HK - 1)

    def act_gdn(act, l, link, astep, splitter):
        S = gdn
        U, S0 = first_unit[l], first_split[l]
        for e in range(2):
            splitter.ahead([0, 1] + GDN_SLOTS_1, e, S0 + e, U + e)
        flat = lambda ap: ap.rearrange("p x l -> p (x l)")
        raw, ab, ex, w1, sig, bg = gba
        lnw, sg = S["osq"][0:64, 0, :], S["osq"][0:32, 1, :]
        act.wait_ge(E["ba_raw"], 1)
        link(nc.scalar.activation(ab, raw, ACT.Abs))
        nc.scalar.activation(ex, ab, ACT.Exp, scale=-1.0).then_inc(E["ba_exp"], 1)
        nc.scalar.activation(sg, raw[0:32], ACT.Exp, scale=-1.0).then_inc(E["ba_sig"], 1)
        act.wait_ge(E["ba_w"], 1)
        nc.scalar.activation(lnw, w1, ACT.Ln).then_inc(E["ba_ln"], 1)

        def respond(name, j):
            if name == "grams":
                act.wait_ge(E["gdiff_ready"], j + 1)
                nc.scalar.activation(flat(S["D"]), flat(S["D"]), ACT.Exp).then_inc(E["gdecay"], 1)
                nc.scalar.activation(flat(S["eg"]), S["rows"][:, 0:2, :].rearrange("p e t -> p (e t)"), ACT.Exp
                                     ).then_inc(E["eg_ready"], 1)
            if name == "norm":
                act.wait_ge(E["os_done"], 4 * (j + 1))
                nc.scalar.activation(flat(S["osq"]), bank[3], ACT.Square).then_inc(E["osq_ready"], 1)
                act.wait_ge(E["ostat_done"], j + 1)
                act_rstd(act, link, flat(S["ors"]), bank[7], 1.0 / P, RMS_EPS).then_inc(E["ors_ready"], 1)

        def body(j):
            first = isinstance(j, int)
            for q in range(4 * GDN_TILES + 1):
                if q and q % 4 == 0:
                    gdn_ahead(splitter, l, j, q // 4 - 1)
                if not first and q in GDN_PLAN:
                    respond(GDN_PLAN[q], j - 1)
                if q == STATS_AT:
                    act.wait_ge(E["nstat_done"], j + 1)
                    act_rstd(act, link, flat(S["rs"]), bank[2], 1.0, RMS_EPS).then_inc(E["rs_ready"], 1)
                if first and q == 14:
                    act.wait_ge(E["gsc_pre"], 1)
                    nc.scalar.activation(S["sc"][:, 0], S["gcol"], ACT.Exp).then_inc(E["gsc_exp"], 1)
                    nc.scalar.activation(S["sc"][:, 1], S["sc"][:, 1], ACT.Exp).then_inc(E["gsc_exp"], 1)
                if q % 4 == 0 and 4 <= q <= 16:
                    p = q // 4 - 1
                    act.wait_ge(E["gconv_ready"], 4 * j + p + 1)
                    if p == 2 and not first:
                        act.wait_ge(E["vt_done"], j)
                    dst = S["qk"][:, p, :] if p < 2 else S["v"][:, p - 2, :]
                    nc.scalar.activation(dst, S["conv"][:, p % 2, :], ACT.Silu).then_inc(E["gconv_silu"], 1)
                    if p < 2:
                        act.wait_ge(E["gconv_silu"], 4 * j + p + 1)
                        nc.scalar.activation(S["sqk"][:, p, :], dst, ACT.Square).then_inc(E["sqk_ready"], 1)
                if q in (20, 24):
                    e = (q - 20) // 4
                    act.wait_ge(unit_done, U + 3 + j * GDN_TILES + 4 + e)
                    nc.scalar.activation(Y[:, ds(2 * j + e, 1), :], pj[e], ACT.Silu).then_inc(E["gz_ready"], 1)
        body(0)
        with rolled(act, 1, GDN_HK, [(astep, 2)] + splitter.steps(GDN_SLOTS)) as j:
            body(j)
        respond("grams", GDN_HK - 1)
        respond("norm", GDN_HK - 1)

    def pool_gdn(pool, l, splitter):
        U, S0 = first_unit[l], first_split[l]

        def level(j, n):
            if n == 0:
                pool.wait_ge(E["u_ready"], 6 * j + 1)
            if n >= 2:
                pool.wait_ge(E["left_done"], 5 * j + n - 1)
            by = C[f"lev{LEVELS[n]}"].rearrange("p (o l) -> p o l", o=1).broadcast_to([P, 4, P])
            nc.gpsimd.tensor_tensor(gdn["lev"][:, n % 2], gdn["A"], by, ALU.mult).then_inc(E["lev_ready"], 1)
        for e in range(2):
            splitter.ahead([0, 1] + GDN_SLOTS_1, e, S0 + e, U + e)
        for p in range(GDN_TILES):
            gdn_ahead(splitter, l, 0, p)
        with pool.Fori(1, GDN_HK) as j:
            for p, levels in enumerate(((0, 1), (2, 3), (4,), (), (), ())):
                for n in levels:
                    level(j - 1, n)
                gdn_ahead(splitter, l, j, p)
        for n in range(5):
            level(GDN_HK - 1, n)

    def pool_ssd(pool, l, splitter):
        U, S0, ns = first_unit[l], first_split[l], nth_ssd[l]
        for e in range(2):
            splitter.ahead([0, 1] + SSD_SLOTS_1, e, S0 + e, U + e)

        def body(g):
            G = g + ns * SSD_GROUPS
            for p in range(SSD_TILES):
                splitter.ahead(SSD_SLOTS_1 if isinstance(g, int) else SSD_SLOTS, p, S0 + 2 + g * SSD_TILES + p,
                               U + 2 + g * SSD_TILES + p)
                if p == 4:
                    pool.wait_ge(E["e_exp"], G + 1)
                    pool.wait_ge(E["conv_silu"], G * 6 + 2)
                    by = ssd["C"][:, P:T].rearrange("p (o l) -> p o l", o=1).broadcast_to([P, SSD_R, P])
                    nc.gpsimd.tensor_tensor(ssd["E"], ssd["E"], by, ALU.mult).then_inc(E["cdec_ready"], 1)
        body(0)
        with pool.Fori(1, SSD_GROUPS) as g:
            body(g)

    def pool_mla(pool, l, splitter):
        U, S0 = first_unit[l], first_split[l]
        for p in range(12):
            splitter.ahead(MLA_SLOTS, p, S0 + p, U + p)
        with pool.Fori(0, 4) as i:
            for p in range(4):
                splitter.ahead(Z_SLOTS, p, S0 + 12 + i * 4 + p, U + 12 + i * 4 + p)

    block = ctx.enter_context(nc.Block())

    @block.sync
    def _(sp):
        last = [0] * SLOTS
        copies = [0]

        def load(p, src, u, free=None, dst=None, landed_as=None):
            free = last[p] if free is None else free
            if not isinstance(free, int):
                sp.wait_ge(unit_done, 1)
            if not (isinstance(free, int) and free == 0):
                sp.wait_ge(unit_done, free)
            dst = slot(p) if dst is None else dst
            if src.shape[-1] == 64:
                sp.dma_start(dst[:, :, 64:P], src).then_inc(E["copy_in"], 16)
                copies[0] += 16
                sp.wait_ge(E["copy_in"], copies[0])
                dst = dst[:, :, 0:64]
            sp.dma_start(dst, src).then_inc(landed[p] if landed_as is None else landed_as, 16)
            if isinstance(u, int):
                last[p] = u + 1

        def turns_of(source, u0, slots_1, slots, turns, beside=None, dst=None, sems=None, skip=0):
            n = len(slots)
            for p, q in enumerate(slots_1):
                if p >= skip:
                    load(q, source(0, p), u0 + p, dst=dst and dst(p), landed_as=sems and sems[p])
                if beside:
                    beside(0, p)
            with sp.Fori(1, turns) as i:
                free = []
                for p, q in enumerate(slots):
                    same = [r for r in range(p) if slots[r] == q]
                    before = [r for r in range(n) if slots[r] == q]
                    assert same or all(r <= before[-1] for r in range(n) if slots_1[r] == q)
                    free.append(i * n + (u0 + same[-1] + 1) if same else (i - 1) * n + (u0 + before[-1] + 1))
                if n == SSD_TILES:
                    free[5] = free[6] = sp.snap(free[6])
                for p, q in enumerate(slots):
                    load(q, source(i, p), None, free[p], dst=dst and dst(p), landed_as=sems and sems[p])
                    if beside:
                        beside(i, p)
            for p, q in enumerate(slots):
                last[q] = u0 + (turns - 1) * n + p + 1

        def load_out(l, w, kt):
            per = kt // KD
            slots = OUT_SLOTS[kt]

            def source(i, p):
                return w_tile(w, i * 512 + p // per * P, k0=p % per * KD)
            turns_of(source, first_unit[l, "out"], slots, slots, 4, skip=2 if KINDS[l] == "mla" else 0)

        sp.dma_start(cst[:], a["consts"]).then_inc(E["consts_in"], 16)
        for c in range(2):
            sp.dma_start(xrows[:, c, :], a["x"][0, c * P:(c + 1) * P, :]).then_inc(E["x_in"], 16)
        for l in layers:
            if KINDS[l] == "ssd":
                load_ssd(sp, l, load, turns_of)
                load_out(l, a["ssd_out_w"][l // 3], 32)
            if KINDS[l] == "mla":
                load_mla(sp, l, load, turns_of)
                load_out(l, a["mla_out_w"][0], 16)
            if KINDS[l] == "gdn":
                load_gdn(sp, l, load, turns_of)
                load_out(l, a["gdn_out_w"][0], 32)
        sp.wait_ge(E["out_rows"], 8)
        for c in range(2):
            sp.dma_start(a["out"][0, c * P:(c + 1) * P, :], xrows[:, c, :]).then_inc(E["out_done"], 16)
        sp.wait_ge(E["out_done"], 32)

    @block.tensor
    def _(pe):
        def contract(q, p, dst, rhs, ks, k_start=0, k_stop=KD - 1, waits=None, s=None):
            for k in ks:
                if k == ks[0] and k < KD // 2 and ks[0] == 0:
                    pe.wait_ge(lo0_ready, s + 1)
                if k == KD // 2:
                    pe.wait_ge(lo1_ready, s + 1)
                if waits is not None:
                    waits(k)
                w_hi = W_hi[:, p % 2, k * P:(k + 1) * P]
                x_hi, x_lo = rhs(k)
                nc.tensor.matmul(dst, w_hi, x_hi, start=k == k_start, stop=False)
                mm = nc.tensor.matmul(dst, w_hi, x_lo, start=False, stop=False)
                if k == KD // 2 - 1:
                    mm.then_inc(half_done, 1)
                mm = nc.tensor.matmul(dst, ring_lo[:, q, k * P:(k + 1) * P], x_hi, start=False, stop=k == k_stop)
            return mm

        def tile(q, p, dst, rhs, s, k_start=0, k_stop=KD - 1, waits=None):
            contract(q, p, dst, rhs, range(KD), k_start, k_stop, waits, s).then_inc(unit_done, 1)

        def head_tile(q, dst, s, waits=None):
            pe.wait_ge(lo1_ready, s + 1)
            contract(q, 0, dst, hidden, range(0, KD // 2), waits=waits, s=s).then_inc(unit_done, 1)
            pe.wait_ge(lo0_ready, s + 2)
            pe.wait_ge(lo1_ready, s + 2)
            for k in range(KD // 2, KD):
                if waits is not None:
                    waits(k)
                w_hi = W_hi[:, 1, k * P:(k + 1) * P]
                nc.tensor.matmul(dst, w_hi, H_hi[:, k, :], start=False, stop=False)
                mm = nc.tensor.matmul(dst, w_hi, H_lo[:, k, :], start=False, stop=False)
                if k == KD // 2:
                    mm.then_inc(half_done, 1)
                mm = nc.tensor.matmul(dst, ring_lo[:, q + 1, k * P:(k + 1) * P], H_hi[:, k, :], start=False,
                                      stop=k == KD - 1)
            mm.then_inc(unit_done, 1)

        def hidden(k):
            return H_hi[:, k, :], H_lo[:, k, :]

        def first_hidden(l):
            n = layer_no[l]
            return (lambda k: pe.wait_ge(E["h_ready"], KD * (n - 1) + k + 1)) if n else None

        def out_and_norm(l, kt):
            per = kt // KD
            n = layer_no[l]
            slots = OUT_SLOTS[kt]

            def body(i):
                for t in range(4):
                    if t >= 2 or not isinstance(i, int):
                        pe.wait_ge(E["pre_ready"], KD * n + i * 4 + t - 1)
                    for h in range(per):
                        p = t * per + h

                        def gated(k):
                            return Y_hi[:, h * KD + k, :], Y_lo[:, h * KD + k, :]
                        first = None
                        if isinstance(i, int) and t == 0:
                            first = lambda k: pe.wait_ge(E["ysplit"], y_split_base[l] + h * 4 + k // 4 + 1)
                        tile(slots[p], p, pj[t % 2], gated, first_split[l, "out"] + i * 4 * per + p,
                             k_start=0 if h == 0 else None, k_stop=KD - 1 if h == per - 1 else None, waits=first)
            body(0)
            with pe.Fori(1, 4) as i:
                body(i)
            pe.wait_ge(E["sum_ready"], n + 1)
            nc.tensor.matmul(bank[2][:, 0:T], C["ones"], ln["sum"], start=True, stop=True).then_inc(E["mean_done"], 1)
            for k in range(KD):
                pe.wait_ge(E["csq_ready"], KD * n + k + 1)
                mm = nc.tensor.matmul(bank[3][:, 0:T], C["ones"], ln["sq"][:, k % 2, :], start=k == 0, stop=k == KD - 1)
                mm.then_inc(E["csq_used"], 1)

        pe.wait_ge(E["consts_in"], 16)
        pe.wait_ge(E["prm_in"], 16 * N_PRM_DMA)
        for i, rows in enumerate(PROWS):
            if i >= 2:
                pe.wait_ge(E["prm_ready"], i - 1)
            nc.tensor.transpose(bank[2 + i % 2][:, 0:rows], prows[0:rows, i, :], ident[0:rows, 0:rows]
                                ).then_inc(E["prm_t"], 1)
        pe.wait_ge(E["x_in"], 32)
        for i in range(8):
            if i >= 4:
                pe.wait_ge(E["h_in"], i - 3)
            for j in range(4):
                c, k = i // 4, i % 4 * 4 + j
                mm = nc.tensor.transpose(bank[4 + i % 4][:, j * P:(j + 1) * P], xrows[:, c, k * P:(k + 1) * P], ident)
            mm.then_inc(E["x_t"], 1)
        pe.wait_ge(E["h_in"], 8)

        for l in layers:
            if KINDS[l] == "ssd":
                pe_ssd(pe, l, tile, contract, head_tile, hidden, first_hidden)
                out_and_norm(l, 32)
            if KINDS[l] == "mla":
                pe_mla(pe, l, tile, contract, head_tile, hidden, first_hidden)
                out_and_norm(l, 16)
            if KINDS[l] == "gdn":
                pe_gdn(pe, l, tile, contract, head_tile, hidden, first_hidden)
                out_and_norm(l, 32)
        for i in range(8):
            if i >= 4:
                pe.wait_ge(E["out_rows"], i - 3)
            if i < 4:
                pe.wait_ge(E["last_ready"], 4 * (i + 1))
            for j in range(4):
                c, k = i // 4, i % 4 * 4 + j
                mm = nc.tensor.transpose(bank[4 + i % 4][:, j * P:(j + 1) * P], pre[:, k, c * P:(c + 1) * P], ident)
            mm.then_inc(E["out_t"], 1)

    @block.vector
    def _(dve):
        step = Count()

        def link(ins):
            ins.then_inc(dve_step, 1)
            dve.wait_ge(dve_step, step.next())

        nc.vector.memset(hd[0:32, 8:9], 0.0).then_inc(E["zero_ready"], 1)
        dve.wait_ge(E["heads_in"], 16 * N_HEAD_DMA)
        for n in range(2):
            for e in range(2):
                nc.vector.tensor_copy(hd[64 * e:64 * e + 64, 16 + 32 * n:48 + 32 * n],
                                      dskip_rows[64 * e:64 * e + 64, n, e::2]).then_inc(E["dskip_ready"], 1)
        for i, rows in enumerate(PROWS):
            dve.wait_ge(E["prm_t"], i + 1)
            nc.vector.tensor_copy(params[:, i, 0:rows], bank[2 + i % 2][:, 0:rows]).then_inc(E["prm_ready"], 1)
        for i in range(8):
            dve.wait_ge(E["x_t"], i + 1)
            k4, cc = slice(i % 4 * 4, i % 4 * 4 + 4), slice(i // 4 * P, (i // 4 + 1) * P)
            link(nc.vector.tensor_copy(H_hi[:, k4, cc], as3(bank[4 + i % 4], 4)))
            nc.vector.tensor_tensor(H_lo[:, k4, cc], as3(bank[4 + i % 4], 4), H_hi[:, k4, cc].bitcast(F32), ALU.subtract
                                    ).then_inc(E["h_in"], 1)
        dve.wait_ge(E["h_in"], 8)
        splitter = Splitter(dve, "dve")
        for p in range(2):
            splitter.split(p, p, p)

        for l in layers:
            if KINDS[l] == "ssd":
                dve_ssd(dve, l, link, step, splitter)
            if KINDS[l] == "mla":
                dve_mla(dve, l, link, step, splitter)
            if KINDS[l] == "gdn":
                dve_gdn(dve, l, link, step, splitter)
            dve_gated_lo(dve, l)
            dve_norm(dve, l, link, step, splitter)
        dve.wait_ge(E["ln_mul"], KD * len(layers))
        for i in range(8):
            dve.wait_ge(E["out_t"], i + 1)
            nc.vector.tensor_copy(xrows[:, i // 4, i % 4 * 512:(i % 4 + 1) * 512], bank[4 + i % 4]
                                  ).then_inc(E["out_rows"], 1)

    @block.scalar
    def _(act):
        astep = Count()

        def link(ins):
            ins.then_inc(act_step, 1)
            act.wait_ge(act_step, astep.next())
        for dst, src in PRM_DMAS:
            act.dma_start(dst, src).then_inc(E["prm_in"], 16)
        for dst, src in HEAD_DMAS:
            act.dma_start(dst, src).then_inc(E["heads_in"], 16)
        act.wait_ge(E["heads_in"], 16 * N_HEAD_DMA)
        for n in range(2):
            link(nc.scalar.activation(hd[0:64, 4 * n + 2:4 * n + 3], hd[0:64, 4 * n + 1:4 * n + 2], ACT.Exp))
        link(nc.scalar.activation(hd[32:64, 10:11], hd[32:64, 9:10], ACT.Exp))
        splitter = Splitter(act, "act")
        for p in range(2):
            splitter.split(p, p, p)
        act.wait_ge(E["prm_ready"], len(PROWS))

        for l in layers:
            if KINDS[l] == "ssd":
                act_ssd(act, l, link, astep, splitter)
            if KINDS[l] == "mla":
                act_mla(act, l, link, astep, splitter)
            if KINDS[l] == "gdn":
                act_gdn(act, l, link, astep, splitter)
            act_gated_hi(act, l)
            act_norm(act, l, link, astep, splitter)

    @block.gpsimd
    def _(pool):
        splitter = Splitter(pool, "pool")
        for p in range(2):
            splitter.split(p, p, p)
        for l in layers:
            if KINDS[l] == "ssd":
                pool_ssd(pool, l, splitter)
            if KINDS[l] == "mla":
                pool_mla(pool, l, splitter)
            if KINDS[l] == "gdn":
                pool_gdn(pool, l, splitter)
            per = 1 if KINDS[l] == "mla" else 2
            with pool.Fori(0, 4 if l != last_layer else 3) as i:
                for p in range(4 * per):
                    look_ahead(splitter, l, i, p)
            if l == last_layer:
                for p in range(4 * per):
                    look_ahead(splitter, l, 3, p)


_INS = ["x", "positions", "ssd_in_w", "ssd_conv_w", "ssd_conv_b", "ssd_dt_bias", "ssd_a_log", "ssd_d", "ssd_norm_w",
        "ssd_out_w", "mla_in_w", "mla_q_norm_w", "mla_q_up_w", "mla_kv_norm_w", "mla_kv_up_w", "mla_out_w",
        "gdn_in_w", "gdn_conv_w", "gdn_a_log", "gdn_dt_bias", "gdn_norm_w", "gdn_out_w", "ln_g", "ln_b"]


def scratch(nc):
    return {"scr_ssd": nc.dram_tensor("scr_ssd", (2, SSD_HEADS, T), F32).ap(),
            "scr_gdn": nc.dram_tensor("scr_gdn", (2 * GDN_HV, T), F32).ap()}


def kernel(**inputs):
    import concourse.bacc as bacc
    from concourse.bass_utils import run_bass_kernel_spmd

    nc = bacc.Bacc("TRN2", target_bir_lowering=False, num_devices=1)
    arrays, args = {}, {}
    for name in _INS + ["consts"]:
        array = constants() if name == "consts" else np.ascontiguousarray(inputs[name])
        arrays[f"in_{name}"] = array
        args[name] = nc.dram_tensor(f"in_{name}", array.shape, mybir.dt.from_np(array.dtype), kind="ExternalInput").ap()
    args["out"] = nc.dram_tensor("out", (1, T, D), F32, kind="ExternalOutput").ap()
    args.update(scratch(nc))
    build(nc, args)
    r = run_bass_kernel_spmd(nc, [arrays], core_ids=[0])
    return r.results[0]["out"]
```

```python
from contextlib import contextmanager, ExitStack

import numpy as np
import concourse.bass as bass
from concourse import mybir

F32 = mybir.dt.float32
F32R = mybir.dt.float32r
I32 = mybir.dt.int32
ALU = mybir.AluOpType
ACT = mybir.ActivationFunctionType
AX = mybir.AxisListType
ds = bass.ds

P = 128
T = 256
D = 2048
KD = D // P
DEPTH = 4
ALPHA = (2.0 * DEPTH) ** 0.25
LN_EPS, RMS_EPS = 1e-5, 1e-6
KINDS = ["ssd", "mla", "gdn", "ssd"]

SSD_IN, SSD_HEADS, SSD_GROUPS = 4096, 64, 8
SSD_R = SSD_HEADS // SSD_GROUPS
SSD_CONV_DIM = SSD_IN + 2 * SSD_GROUPS * P
SSD_COL_X = SSD_IN
SSD_COL_B = SSD_COL_X + SSD_IN
SSD_COL_C = SSD_COL_B + SSD_GROUPS * P
SSD_COL_DT = SSD_COL_C + SSD_GROUPS * P
SSD_XT = SSD_IN // P
SSD_TILES = 10

MLA_H, MLA_QR, MLA_KVR, MLA_ROPE = 16, 768, 512, 64
MLA_QT, MLA_KVT = MLA_QR // P, MLA_KVR // P
MLA_COL_KR = MLA_QR + MLA_KVR
MLA_COL_Z = MLA_COL_KR + MLA_ROPE
MLA_SCALE = (128 + MLA_ROPE) ** -0.5

GDN_HK, GDN_HV = 16, 32
GDN_COL_K, GDN_COL_V, GDN_COL_Z = 2048, 4096, 8192
GDN_COL_B = 12288
GDN_TILES = 6
LEVELS = (2, 4, 8, 16, 32)

SLOTS, SLOT = 6, 2048
SSD_SLOTS, SSD_SLOTS_1 = [0, 1, 2, 3, 4, 0, 1, 2, 3, 4], [2, 3, 4, 5, 0, 1, 2, 3, 4, 5]
GDN_SLOTS, GDN_SLOTS_1 = [0, 1, 2, 3, 4, 5], [2, 3, 4, 5, 4, 5]
OUT_SLOTS = {32: [0, 1, 2, 3, 4, 5, 2, 3], 16: [0, 1, 2, 3]}
MLA_SLOTS = [p % SLOTS for p in range(12)]
Z_SLOTS = [0, 1, 2, 3]
UP_SLOT = 2
SQ_RING = 8
HI64 = slice(64, 128)
NEG = -1.0e30
MAGIC = 1.5 * 2.0 ** 23
TWO_PI_A = 6.28125
TWO_PI_B = float(np.float32(np.round((2 * np.pi - TWO_PI_A) * 2 ** 21) / 2 ** 21))
TWO_PI_C = float(np.float32(2 * np.pi - TWO_PI_A - TWO_PI_B))

CONST = ["ident", "ones", "tri128", "tri64", "blk64", "neg128", "neg64", "negq", "rot",
         "lev1", "lev2", "lev4", "lev8", "lev16", "lev32"]


def constants():
    r, c = np.arange(P)[:, None], np.arange(P)[None, :]
    same64 = r // 64 == c // 64
    m = {
        "ident": r == c,
        "ones": np.ones((P, P)),
        "tri128": r <= c,
        "tri64": (r <= c) & same64,
        "blk64": same64,
        "neg128": np.where(r <= c, 0.0, NEG),
        "neg64": np.where((r <= c) & same64, 0.0, NEG),
        "negq": np.where(c <= r, 0.0, NEG),
        "rot": np.where((c % 64 < 32) & (r == c + 32), -1.0, 0.0) + np.where((c % 64 >= 32) & (r == c - 32), 1.0, 0.0),
    }
    for b in (1,) + LEVELS:
        m[f"lev{b}"] = (r // (2 * b) == c // (2 * b)) & (c // b % 2 == 1) & (r // b % 2 == 0)
    inv = (10000.0 ** (-np.arange(0, MLA_ROPE, 2, dtype=np.float64) / MLA_ROPE)).astype(np.float32)
    cols = [np.asarray(m[n], np.float32) for n in CONST] + [np.tile(inv, 4)[:, None]]
    return np.ascontiguousarray(np.concatenate(cols, axis=1).astype(np.float32))


class Count:

    def __init__(self):
        self.n, self.turn, self.step = 0, 0, 0

    def next(self, by=1):
        self.n += by
        return self.n + self.turn * self.step if self.step else self.n


@contextmanager
def rolled(eng, start, end, steps):
    with eng.Fori(start, end) as i:
        at = [(c, c.n) for c, _ in steps]
        for c, by in steps:
            c.turn, c.step = i - start, by
        yield i
    for (c, n0), (_, by) in zip(at, steps):
        assert c.n - n0 == by, (c.n - n0, by)
        c.n, c.turn, c.step = n0 + by * (end - start), 0, 0


def build(nc, a, layers=range(DEPTH)):
    layers = list(layers)
    with ExitStack() as ctx:
        _program(nc, a, layers, ctx)


def _program(nc, a, layers, ctx):
    def sb(name, shape, dt=F32):
        return ctx.enter_context(nc.sbuf_tensor(name, shape, dt))

    def sem(name):
        return ctx.enter_context(nc.semaphore(name))

    def twins(name, shape):
        with nc.sbuf_tensor(name, shape, F32) as plain:
            pass
        return plain, sb(name + "_r", shape, F32R)

    H_hi = sb("H_hi", [P, KD, T], F32R)
    pre, H_lo = twins("pre", [P, KD, T])
    Y, Y_lo = twins("Y", [P, 32, T])
    ring, ring_lo = twins("ring", [P, SLOTS, SLOT])
    W_hi = sb("W_hi", [P, 2, SLOT], F32R)
    cst = sb("cst", [P, len(CONST) * P + 1])
    ARENA = 12100
    arena, arena_r = twins("arena", [P, ARENA])
    Y_hi = arena_r[:, ARENA - 32 * T:ARENA].rearrange("p (k t) -> p k t", t=T)
    params = sb("params", [P, 10, P])
    hd = sb("hd", [P, 16 + 2 * 32])
    posi = sb("posi", [P, T], I32)
    banks = [ctx.enter_context(nc.psum_tensor(f"bank{i}", [P, 512], F32)) for i in range(8)]
    C = {n: cst[:, P * i:P * (i + 1)] for i, n in enumerate(CONST)}
    inv_freq = cst[:, len(CONST) * P:len(CONST) * P + 1]
    ident = C["ident"]

    def carve(*shapes, base=0):
        at, out = base, []
        for s in shapes:
            n = int(np.prod(s))
            v = arena[:, at:at + n]
            if len(s) == 2:
                v = v.rearrange("p (a b) -> p a b", a=s[0])
            if len(s) == 3:
                v = v.rearrange("p (a b c) -> p a b c", a=s[0], b=s[1])
            out.append(v)
            at += n
        assert at <= ARENA, at
        return out

    def slot(p, k=KD):
        return ring[:, p, :].rearrange("p (k c) -> p k c", k=k)

    bank = [b[:] for b in banks]
    pj = [bank[0][:, 0:T], bank[1][:, 0:T]]

    def as3(ap, a):
        return ap.rearrange("p (a b) -> p a b", a=a)

    landed = [sem(f"landed{p}") for p in range(SLOTS)]
    up_landed = [sem(f"up_landed{p}") for p in range(3)]
    half_done = sem("half_done")
    hi_ready = sem("hi_ready")
    lo0_ready, lo1_ready = sem("lo0_ready"), sem("lo1_ready")
    unit_done = sem("unit_done")
    dve_step, act_step = sem("dve_step"), sem("act_step")
    class Events(dict):

        def __missing__(self, name):
            self[name] = sem(name)
            return self[name]

    E = Events()

    first_unit, first_split, layer_no, nth_ssd = {}, {}, {}, {}
    at = up = 0
    for n, l in enumerate(layers):
        kind = KINDS[l]
        layer_no[l] = n
        nth_ssd[l] = sum(KINDS[x] == "ssd" for x in layers[:n])
        first_unit[l], first_split[l] = at, at - up
        at += {"ssd": 2 + SSD_TILES * SSD_GROUPS, "mla": 12 + 16 + 3 * 8, "gdn": 2 + GDN_TILES * GDN_HK}[kind]
        up += 24 if kind == "mla" else 0
        first_unit[l, "out"], first_split[l, "out"] = at, at - up
        at += 16 if kind == "mla" else 32
    last_layer = layers[-1]

    def w_tile(w, col, width=P, k0=0, kn=KD):
        return w.rearrange("(k p) n -> p k n", p=P)[:, k0:k0 + kn, ds(col, width)]

    class Splitter:

        def __init__(self, eng, part):
            self.eng, self.part = eng, part
            self.both = False
            self.taken = [Count() for _ in range(SLOTS)]

        def split(self, p, par, s, freed=None, halves=(0, 1)):
            eng, h = self.eng, SLOT // 2
            if self.part == "act":
                if 0 in halves:
                    eng.wait_ge(landed[p], self.taken[p].next(16))
                for half in halves:
                    at = slice(half * h, half * h + h)
                    if freed is not None:
                        eng.wait_ge((half_done, unit_done)[half], freed[half])
                    nc.scalar.activation(W_hi[:, par, at], ring[:, p, at], ACT.Copy).then_inc(hi_ready, 1)
            if self.part == "dve" and not self.both:
                eng.wait_ge(hi_ready, s * 2 + 1)
                nc.vector.tensor_tensor(ring_lo[:, p, 0:h], ring[:, p, 0:h], W_hi[:, par, 0:h].bitcast(F32),
                                        ALU.subtract).then_inc(lo0_ready, 1)
            if self.part == "pool" and self.both:
                eng.wait_ge(hi_ready, s * 2 + 1)
                nc.gpsimd.tensor_tensor(ring_lo[:, p, 0:h], ring[:, p, 0:h], W_hi[:, par, 0:h].bitcast(F32),
                                        ALU.subtract).then_inc(lo0_ready, 1)
            if self.part == "pool":
                eng.wait_ge(hi_ready, s * 2 + 2)
                nc.gpsimd.tensor_tensor(ring_lo[:, p, h:SLOT], ring[:, p, h:SLOT], W_hi[:, par, h:SLOT].bitcast(F32),
                                        ALU.subtract).then_inc(lo1_ready, 1)

        def ahead(self, slots, p, s, u, halves=(0, 1)):
            self.split((slots + [0, 1])[p + 2], p % 2, s + 2, (s + 1, u + 1), halves)

        def hand_over(self, both, s):
            self.both = both
            if self.part == ("pool" if both else "dve"):
                self.eng.wait_ge(lo0_ready, s)

        def steps(self, slots):
            return [(self.taken[p], 16 * slots.count(p)) for p in range(SLOTS) if p in slots]

    ssd = {}
    (ssd["conv"], ssd["B"], ssd["C"], ssd["X"], ssd["Z"], ssd["xdt"], ssd["xds"], ssd["btok"], ssd["rows"],
     ssd["D"], ssd["E"], ssd["st"], ssd["YG"], ssd["rstd"], ssd["tok"], ssd["acol"], ssd["dst"]) = carve(
        (2, T), (T,), (T,), (4, T), (4, T), (2, 512), (512,), (P,), (SSD_R, T),
        (2, SSD_R, P), (SSD_R, P), (512,), (4, T), (T,), (4, 64), (2, 64), (64,))
    ssd["SQ"] = ssd["E"].rearrange("p r t -> p (r t)").rearrange("p (a b) -> p a b", a=4)
    dtv = [ssd["YG"][HI64, i, :] for i in range(4)] + [ssd["xdt"][HI64, 0, 0:T], ssd["xdt"][HI64, 0, T:2 * T],
                                                      ssd["xdt"][HI64, 1, 0:T], ssd["xdt"][HI64, 1, T:2 * T]]
    ln = {}
    ln["sum"], ln["rstd"], ln["sq"] = carve((T,), (T,), (SQ_RING, T))
    xrows = arena[:, 0:2 * D].rearrange("p (c n) -> p c n", c=2)
    prows = Y[:, 0:5, :].rearrange("p a (b c) -> p (a b) c", b=2)
    dskip_rows = Y[:, 5, 0:P].rearrange("p (n h) -> p n h", n=2)

    y_base, y_split_base, yb, yc = {}, {}, 0, 0
    for l in layers:
        y_base[l], y_split_base[l] = yb, yc
        yb += 32 if KINDS[l] == "ssd" else 0
        yc += 4 if KINDS[l] == "mla" else 8

    PCOL = {}
    for n, l in enumerate((0, 3)):
        for tap in range(4):
            PCOL[l, f"tap{tap}"] = (3 * n + tap // 2) * P + 48 * (tap % 2)
        PCOL[l, "g"], PCOL[l, "b"] = 3 * n * P + 96, 3 * n * P + 112
        PCOL[l, "norm"], PCOL[l, "cb"] = (3 * n + 1) * P + 96, (3 * n + 2) * P
    for tap in range(4):
        PCOL[2, f"tap{tap}"] = (6 + tap // 2) * P + 64 * (tap % 2)
    PCOL[2, "g"], PCOL[2, "b"], PCOL[2, "norm"] = 8 * P, 8 * P + 16, 8 * P + 32
    PCOL[1, "qn"], PCOL[1, "kvn"], PCOL[1, "g"], PCOL[1, "b"] = 9 * P, 9 * P + 6, 9 * P + 10, 9 * P + 26
    PROWS = [128, 128, 48, 128, 128, 48, 128, 128, 33, 42]

    def pcol(l, name, idx):
        flat = params[:].rearrange("p a b -> p (a b)")
        return flat[:, ds(PCOL[l, name] + idx, 1)]


    def rows128(ap):
        return ap.rearrange("(r c) -> r c", c=P)

    PRM_DMAS = []
    for n, l in enumerate((0, 3)):
        for tap in range(4):
            r0 = 48 * (tap % 2)
            PRM_DMAS.append((prows[r0:r0 + 48, 3 * n + tap // 2, :], rows128(a["ssd_conv_w"][n, tap])))
        PRM_DMAS += [(prows[96:112, 3 * n, :], rows128(a["ln_g"][l])), (prows[112:128, 3 * n, :], rows128(a["ln_b"][l])),
                     (prows[96:128, 3 * n + 1, :], rows128(a["ssd_norm_w"][n])),
                     (prows[0:48, 3 * n + 2, :], rows128(a["ssd_conv_b"][n]))]
    for tap in range(4):
        r0 = 64 * (tap % 2)
        PRM_DMAS.append((prows[r0:r0 + 64, 6 + tap // 2, :], rows128(a["gdn_conv_w"][0, tap])))
    PRM_DMAS += [(prows[0:16, 8, :], rows128(a["ln_g"][2])), (prows[16:32, 8, :], rows128(a["ln_b"][2])),
                 (prows[32:33, 8, :], a["gdn_norm_w"]),
                 (prows[0:6, 9, :], rows128(a["mla_q_norm_w"][0])), (prows[6:10, 9, :], rows128(a["mla_kv_norm_w"][0])),
                 (prows[10:26, 9, :], rows128(a["ln_g"][1])), (prows[26:42, 9, :], rows128(a["ln_b"][1]))]
    N_PRM_DMA = len(PRM_DMAS)

    def column(ap):
        return ap.rearrange("(h o) -> h o", o=1)

    HEAD_DMAS = []
    for n in range(2):
        HEAD_DMAS += [(hd[HI64, 4 * n:4 * n + 1], column(a["ssd_dt_bias"][n])),
                      (hd[HI64, 4 * n + 1:4 * n + 2], column(a["ssd_a_log"][n])),
                      (dskip_rows[:, n, :], a["ssd_d"][n].partition_broadcast(P))]
    HEAD_DMAS += [(hd[96:128, 8:9], column(a["gdn_dt_bias"][0])), (hd[96:128, 9:10], column(a["gdn_a_log"][0])),
                  (posi[:], a["positions"][0].partition_broadcast(P))]
    N_HEAD_DMA = len(HEAD_DMAS)

    def load_params(sp):
        sp.dma_start(cst[:, P:], a["consts"][:, P:]).then_inc(E["consts_in"], 16)
        for dst, src in PRM_DMAS:
            sp.dma_start(dst, src).then_inc(E["prm_in"], 16)

    def load_ssd(sp, l, load, turns_of):
        w, ns = a["ssd_in_w"][l // 3], nth_ssd[l]
        scr = a["scr_ssd"][ns]
        for p in range(2):
            load(p, w_tile(w, SSD_COL_DT - 64), first_unit[l] + p)
        if layer_no[l] == 0:
            load_params(sp)

        def rows_of(g):
            G = g + ns * SSD_GROUPS
            row = g * SSD_R if isinstance(g, int) else sp.snap(g * SSD_R)
            if not (isinstance(G, int) and G == 0):
                sp.wait_ge(unit_done, 1)
                sp.wait_ge(E["diff_ready"], G)
                sp.wait_ge(E["e_exp"], G)
            sp.dma_start(ssd["rows"], scr[ds(row, SSD_R), :].partition_broadcast(P)).then_inc(E["rows_in"], 16)

        def source(g, p):
            return w_tile(w, [SSD_COL_B + g * P, SSD_COL_C + g * P, SSD_COL_X + g * 512, SSD_COL_X + P + g * 512,
                              SSD_COL_X + 2 * P + g * 512, SSD_COL_X + 3 * P + g * 512,
                              g * 512, g * 512 + P, g * 512 + 2 * P, g * 512 + 3 * P][p])

        def beside(g, p):
            if p == 6 and not isinstance(g, int):
                rows_of(g)
            if p == 7 and isinstance(g, int):
                sp.wait_ge(E["acs_ready"], ns + 1)
                sp.dma_start(scr, dtv[7]).then_inc(E["scr_out"], 16)
                sp.wait_ge(E["scr_out"], 16 * (ns + 1))
                rows_of(0)
        turns_of(source, first_unit[l] + 2, SSD_SLOTS_1, SSD_SLOTS, SSD_GROUPS, beside)

    def pe_params(pe):
        pe.wait_ge(E["h_in"], 8)
        pe.wait_ge(E["consts_in"], 16)
        pe.wait_ge(E["prm_in"], 16 * N_PRM_DMA)
        for i, rows in enumerate(PROWS):
            if i >= 6:
                pe.wait_ge(E["prm_ready"], i - 5)
            nc.tensor.transpose(bank[2 + i % 6][:, 0:rows], prows[0:rows, i, :], ident[0:rows, 0:rows]
                                ).then_inc(E["prm_t"], 1)
        pe.wait_ge(E["prm_ready"], len(PROWS))

    def dve_params(dve):
        dve.wait_ge(E["consts_in"], 16)
        dve.wait_ge(E["heads_in"], 16 * N_HEAD_DMA)
        for n in range(2):
            for e in range(2):
                nc.vector.tensor_copy(hd[64 * e:64 * e + 64, 16 + 32 * n:48 + 32 * n],
                                      dskip_rows[64 * e:64 * e + 64, n, e::2])
        for i, rows in enumerate(PROWS):
            dve.wait_ge(E["prm_t"], i + 1)
            nc.vector.tensor_copy(params[:, i, 0:rows], bank[2 + i % 6][:, 0:rows]).then_inc(E["prm_ready"], 1)
        dve.wait_ge(E["prm_ready"], len(PROWS))

    def act_params(act, link):
        act.wait_ge(E["heads_in"], 16 * N_HEAD_DMA)
        for n in range(2):
            link(nc.scalar.activation(hd[HI64, 4 * n + 2:4 * n + 3], hd[HI64, 4 * n + 1:4 * n + 2], ACT.Exp))
        link(nc.scalar.activation(hd[96:128, 10:11], hd[96:128, 9:10], ACT.Exp))
        act.wait_ge(E["prm_ready"], len(PROWS))

    def pe_ssd(pe, l, tile, head_tile, hidden, first_hidden):
        ns = nth_ssd[l]
        S = ssd

        def mean_square(G):
            pe.wait_ge(E["sq_sum"], 2 * (G - ns))
            nc.tensor.matmul(bank[7][:, 0:T], C["ones"], S["SQ"][:, 0, :], start=True, stop=True
                             ).then_inc(E["stat_done"], 1)

        def body(g):
            G = g + ns * SSD_GROUPS
            head = isinstance(g, int)

            def proj(p):
                if p in (0, 1):
                    if not head:
                        pe.wait_ge(E["z_ready"], G * 4 + p - 1)
                    if head and p == 1:
                        pe.wait_ge(E["dt_x"], ns + 1)
                elif p < 8:
                    pe.wait_ge(E["conv_ready"], G * 6 + p - 1)
                else:
                    pe.wait_ge(E["z_ready"], G * 4 + p - 7)
                tile(slots[p], p, pj[p % 2], hidden, first_split[l] + 2 + g * SSD_TILES + p)

            slots = SSD_SLOTS_1 if head else SSD_SLOTS
            proj(0)
            proj(1)
            if not head:
                mean_square(G)
            if head:
                pe.wait_ge(E["dt_a"], ns + 1)
                for j in range(4):
                    src = (dtv[5] if j < 2 else dtv[6])[:, j % 2 * P:(j % 2 + 1) * P]
                    mm = nc.tensor.transpose(bank[2][:, j * 64:(j + 1) * 64], src, ident[HI64, HI64])
                mm.then_inc(E["dt_t"], 1)
            proj(2)
            if head:
                pe.wait_ge(E["dt_tok"], ns + 1)
                for c in range(2):
                    nc.tensor.matmul(bank[3][HI64, c * P:(c + 1) * P], S["tok"][:, 2 + c, :], C["tri128"],
                                     start=True, stop=True)
                nc.tensor.matmul(bank[4][:, 0:P], C["tri128"], S["tok"][:, 2:4, :], start=True, stop=True)
                nc.tensor.matmul(bank[4][:, P:P + 64], C["ones"], S["tok"][:, 2, :], start=True, stop=True
                                 ).then_inc(E["cum_done"], 1)
            proj(3)
            proj(4)
            pe.wait_ge(E["conv_silu"], G * 6 + 2)
            if head:
                pe.wait_ge(E["acs_ready"], ns + 1)
            for c in range(2):
                mm = nc.tensor.matmul(bank[6][:, c * P:(c + 1) * P], S["B"][:, c * P:(c + 1) * P],
                                      S["C"][:, c * P:(c + 1) * P], start=True, stop=True)
            mm.then_inc(E["cb_done"], 1)
            proj(5)
            proj(6)
            pe.wait_ge(E["conv_silu"], G * 6 + 6)
            for c in range(2):
                for t in range(4):
                    mm = nc.tensor.transpose(bank[2 + c][:, t * P:(t + 1) * P], S["X"][:, t, c * P:(c + 1) * P], ident)
                mm.then_inc(E["tx_done"], 1)
            if not head:
                pe.wait_ge(E["rstd_ready"], G)
            nc.tensor.transpose(bank[7][:, 0:P], S["B"][:, 0:P], ident).then_inc(E["bt_done"], 1)
            proj(7)
            pe.wait_ge(E["btok_ready"], G + 1)
            pe.wait_ge(E["xds_ready"], G + 1)
            nc.tensor.matmul(bank[7], S["btok"], S["xds"], start=True, stop=True).then_inc(E["st_done"], 1)
            pe.wait_ge(E["m_ready"], G * 2 + 1)
            for r in range(SSD_R):
                o = bank[4 + r // 4][64 * (r % 2):64 * (r % 2) + 64, r // 2 % 2 * T:r // 2 % 2 * T + P]
                nc.tensor.matmul(o, S["xdt"][:, 0, r * 64:(r + 1) * 64], S["D"][:, 0, r, :], start=True, stop=True)
            proj(8)
            pe.wait_ge(E["m_ready"], G * 2 + 2)
            pe.wait_ge(E["cdec_ready"], G + 1)
            pe.wait_ge(E["st_ready"], G + 1)
            for r in range(SSD_R):
                o = bank[4 + r // 4][64 * (r % 2):64 * (r % 2) + 64, r // 2 % 2 * T + P:r // 2 % 2 * T + 2 * P]
                nc.tensor.matmul(o, S["xdt"][:, 1, r * 64:(r + 1) * 64], S["D"][:, 1, r, :], start=True, stop=False)
                mm = nc.tensor.matmul(o, S["st"][:, r * 64:(r + 1) * 64], S["E"][:, r, :], start=False, stop=True)
            mm.then_inc(E["y_done"], 1)
            proj(9)

        head_tile(0, pj[1], first_split[l], first_hidden(l))
        if layer_no[l] == 0:
            pe_params(pe)
        body(0)
        with pe.Fori(1, SSD_GROUPS) as g:
            body(g)
        G = ns * SSD_GROUPS + SSD_GROUPS
        for i in range(4):
            pe.wait_ge(E["sq_ready"], (G - 1) * 4 + i + 1)
            mm = nc.tensor.matmul(bank[7][:, 0:T], C["ones"], S["SQ"][:, i, :], start=i == 0, stop=i == 3)
        mm.then_inc(E["stat_done"], 1)

    def conv(dve, link, src, dst, l, tile_no):
        link(nc.vector.tensor_scalar(dst, src, pcol(l, "tap3", tile_no), None, ALU.mult))
        for s in (1, 2, 3):
            ins = nc.vector.scalar_tensor_tensor(out=dst[:, s:T], in0=src[:, 0:T - s],
                                                 scalar=pcol(l, f"tap{3 - s}", tile_no), in1=dst[:, s:T],
                                                 op0=ALU.mult, op1=ALU.add)
            if s < 3:
                link(ins)
        return ins

    def dve_ssd(dve, l, link, step, splitter):
        ns, S = nth_ssd[l], ssd
        U, S0 = first_unit[l], first_split[l]
        for e in range(2):
            splitter.ahead([0, 1] + SSD_SLOTS_1, e, S0 + e, U + e)
        if layer_no[l] == 0:
            dve_params(dve)
        raw, absx, ex, w1, lnw, dt, da, arow = dtv
        hcol = hd[HI64, 4 * (l // 3):4 * (l // 3) + 3]
        dve.wait_ge(unit_done, U + 2)
        nc.vector.tensor_scalar(raw, pj[1][HI64], hcol[:, 0:1], None, ALU.add).then_inc(E["dt_x"], 1)
        dve.wait_ge(E["dt_exp"], ns + 1)
        nc.vector.tensor_scalar(w1, ex, 1.0, None, ALU.add).then_inc(E["dt_w"], 1)
        dve.wait_ge(E["dt_w"], ns + 1)
        link(nc.vector.tensor_scalar(dt, w1, 1.0, 0.0, ALU.subtract, ALU.is_equal))
        link(nc.vector.scalar_tensor_tensor(out=da, in0=w1, scalar=-1.0, in1=dt, op0=ALU.add, op1=ALU.add))
        link(nc.vector.reciprocal(da, da))
        link(nc.vector.tensor_tensor(da, da, ex, ALU.mult))
        dve.wait_ge(E["dt_ln"], ns + 1)
        link(nc.vector.tensor_tensor(dt, dt, lnw, ALU.add))
        link(nc.vector.tensor_tensor(da, da, dt, ALU.mult))
        link(nc.vector.scalar_tensor_tensor(out=dt, in0=raw, scalar=0.0, in1=da, op0=ALU.max, op1=ALU.add))
        nc.vector.tensor_scalar(da, dt, hcol[:, 2:3], -1.0, ALU.mult, ALU.mult).then_inc(E["dt_a"], 1)

        def body(g):
            G = g + ns * SSD_GROUPS
            head = isinstance(g, int)

            def ahead(p):
                splitter.ahead(SSD_SLOTS_1 if head else SSD_SLOTS, p, S0 + 2 + g * SSD_TILES + p, U + 2 + g * SSD_TILES + p)

            def conv_of(k, tile_no):
                if k != 4:
                    ahead(k)
                dve.wait_ge(unit_done, U + 3 + g * SSD_TILES + k)
                if not (isinstance(G, int) and G == 0 and k < 2):
                    dve.wait_ge(E["conv_silu"], G * 6 + k - 1)
                conv(dve, link, pj[k % 2], S["conv"][:, k % 2, :], l, tile_no).then_inc(E["conv_ready"], 1)
            conv_of(0, SSD_XT + g)
            if head:
                dve.wait_ge(E["dt_t"], ns + 1)
                nc.vector.tensor_copy(S["tok"], as3(bank[2][:, 0:256], 4)).then_inc(E["dt_tok"], 1)
            conv_of(1, SSD_XT + SSD_GROUPS + g)
            if head:
                dve.wait_ge(E["cum_done"], ns + 1)
                link(nc.vector.tensor_copy(S["acol"], as3(bank[4][:, 0:P], 2)))
                nc.vector.tensor_tensor(S["dst"], bank[4][:, P:P + 64], S["acol"][:, 0, :], ALU.subtract
                                        ).then_inc(E["dst_pre"], 1)
                nc.vector.tensor_copy(arow, bank[3][HI64, 0:T]).then_inc(E["acs_ready"], 1)
                dve.wait_ge(E["acs_ready"], ns + 1)
            conv_of(2, g * 4)
            conv_of(3, g * 4 + 1)
            dve.wait_ge(E["rows_in"], (G + 1) * 16)
            for c in range(2):
                for r in range(SSD_R):
                    ins = nc.vector.scalar_tensor_tensor(
                        out=S["D"][:, c, r, :], in0=S["rows"][:, r, c * P:(c + 1) * P],
                        scalar=S["acol"][:, c, ds(g * SSD_R + r, 1)], in1=C["neg128"], op0=ALU.subtract, op1=ALU.min)
            ins.then_inc(E["diff_ready"], 1)
            ahead(4)
            conv_of(4, g * 4 + 2)
            if not head:
                ssd_norm(G, g)
            conv_of(5, g * 4 + 3)
            dve.wait_ge(E["cb_done"], G + 1)
            for c in range(2):
                dve.wait_ge(E["d_exp"], G * 2 + c + 1)
                cb = bank[6][:, c * P:(c + 1) * P].rearrange("p (o l) -> p o l", o=1).broadcast_to([P, SSD_R, P])
                nc.vector.tensor_tensor(S["D"][:, c], S["D"][:, c], cb, ALU.mult).then_inc(E["m_ready"], 1)
            ahead(6)
            for c in range(2):
                dve.wait_ge(E["tx_done"], G * 2 + c + 1)
                by = S["tok"][:, c, ds(g * SSD_R, SSD_R)].rearrange("p (r o) -> p r o", o=1).broadcast_to([P, SSD_R, 64])
                nc.vector.tensor_tensor(as3(S["xdt"][:, c, :], SSD_R), as3(bank[2 + c], SSD_R), by, ALU.mult
                                        ).then_inc(E["xdt_ready"], 1)
            dve.wait_ge(E["xdt_ready"], G * 2 + 2)
            if head:
                dve.wait_ge(E["dst_ready"], ns + 1)
            by = S["dst"][:, ds(g * SSD_R, SSD_R)].rearrange("p (r o) -> p r o", o=1).broadcast_to([P, SSD_R, 64])
            nc.vector.tensor_tensor(as3(S["xds"], SSD_R), as3(S["xdt"][:, 0, :], SSD_R), by, ALU.mult
                                    ).then_inc(E["xds_ready"], 1)
            ahead(7)
            ahead(8)
            dve.wait_ge(E["y_done"], G + 1)
            for i in range(4):
                link(nc.vector.scalar_tensor_tensor(
                    out=S["YG"][:, i, :], in0=S["X"][:, i, :], scalar=hd[:, ds(16 + 32 * (l // 3) + g * 4 + i, 1)],
                    in1=bank[4 + i // 2][:, i % 2 * T:(i % 2 + 1) * T], op0=ALU.mult, op1=ALU.add))
            ahead(9)
            for i in range(4):
                dve.wait_ge(E["z_ready"], G * 4 + i + 1)
                nc.vector.tensor_tensor(S["YG"][:, i, :], S["YG"][:, i, :], S["Z"][:, i, :], ALU.mult
                                        ).then_inc(E["yg_ready"], 1)

        def ssd_norm(G, g):
            dve.wait_ge(E["yg_ready"], G * 4)
            dve.wait_ge(E["rstd_ready"], G)
            for i in range(4):
                t = g * 4 - 4 + i
                nc.vector.scalar_tensor_tensor(out=Y[:, t, :], in0=S["YG"][:, i, :], scalar=pcol(l, "norm", t),
                                               in1=S["rstd"], op0=ALU.mult, op1=ALU.mult).then_inc(E["y_ready"], 1)
        body(0)
        with rolled(dve, 1, SSD_GROUPS, [(step, 6 * 3 + 4)]) as g:
            body(g)
        ssd_norm(ns * SSD_GROUPS + SSD_GROUPS, SSD_GROUPS)

    def look_ahead(splitter, l, i, p):
        per = 1 if KINDS[l] == "mla" else 2
        slots = OUT_SLOTS[per * KD]
        if not (l == last_layer and isinstance(i, int) and i == 3 and p >= 4 * per - 2):
            done = i * 4 * per + p
            splitter.ahead(slots, p, first_split[l, "out"] + done, first_unit[l, "out"] + done)

    def gated_ready(eng, l):
        if KINDS[l] == "ssd":
            eng.wait_ge(E["y_ready"], y_base[l] + 32)
        if KINDS[l] == "mla":
            eng.wait_ge(E["o_ready"], 16)
        if KINDS[l] == "gdn":
            eng.wait_ge(E["gy_ready"], 17)

    def act_gated_hi(act, l):
        gated_ready(act, l)
        for c in range(4 if KINDS[l] == "mla" else 8):
            nc.scalar.activation(Y_hi[:, 4 * c:4 * c + 4, :], Y[:, 4 * c:4 * c + 4, :], ACT.Copy).then_inc(E["yhi_ready"], 1)

    def dve_gated_lo(dve, l, splitter):
        if KINDS[l] == "gdn":
            splitter.hand_over(False, first_split[l, "out"] + 2)
        for c in range(3 if KINDS[l] == "mla" else 6):
            dve.wait_ge(E["yhi_ready"], y_split_base[l] + c + 1)
            nc.vector.tensor_tensor(Y_lo[:, 4 * c:4 * c + 4, :], Y[:, 4 * c:4 * c + 4, :],
                                    Y_hi[:, 4 * c:4 * c + 4, :].bitcast(F32), ALU.subtract).then_inc(E["ysplit"], 1)

    def pool_gated_lo(pool, l):
        for c in range(3, 4) if KINDS[l] == "mla" else range(6, 8):
            pool.wait_ge(E["yhi_ready"], y_split_base[l] + c + 1)
            nc.gpsimd.tensor_tensor(Y_lo[:, 4 * c:4 * c + 4, :], Y[:, 4 * c:4 * c + 4, :],
                                    Y_hi[:, 4 * c:4 * c + 4, :].bitcast(F32), ALU.subtract).then_inc(E["ysplit_end"], 1)

    def dve_norm(dve, l, link, step, splitter):
        n = layer_no[l]
        U, per = first_unit[l, "out"], (1 if KINDS[l] == "mla" else 2)
        link(nc.vector.memset(ln["sum"], 0.0))

        def body(i):
            for t in range(4):
                d = ds(i * 4 + t, 1)
                for p in range(t * per, (t + 1) * per):
                    look_ahead(splitter, l, i, p)
                dve.wait_ge(unit_done, U + (i * 4 + t + 1) * per)
                link(nc.vector.scalar_tensor_tensor(out=pre[:, d, :], in0=H_lo[:, d, :].bitcast(F32), scalar=ALPHA,
                                                    in1=pj[t % 2], op0=ALU.mult, op1=ALU.add))
                nc.vector.scalar_tensor_tensor(out=pre[:, d, :], in0=H_hi[:, d, :].bitcast(F32), scalar=ALPHA,
                                               in1=pre[:, d, :], op0=ALU.mult, op1=ALU.add).then_inc(E["pre_ready"], 1)
                dve.wait_ge(E["pre_ready"], KD * n + i * 4 + t + 1)
                link(nc.vector.tensor_tensor(ln["sum"], ln["sum"], pre[:, d, :], ALU.add))
        turns = 4 if l != last_layer else 3
        with rolled(dve, 0, turns, [(step, 8)]) as i:
            body(i)
        if l == last_layer:
            body(3)
        nc.vector.tensor_scalar(ln["sum"], ln["sum"], 1.0 / D, None, ALU.mult).then_inc(E["sum_ready"], 1)
        dve.wait_ge(E["mean_done"], n + 1)
        for k in range(KD):
            nc.vector.tensor_tensor(pre[:, k, :], pre[:, k, :], bank[2][:, 0:T], ALU.subtract
                                    ).then_inc(E["cent_ready"], 1)
        dve.wait_ge(E["cent_ready"], KD * (n + 1))
        dve.wait_ge(E["lrstd_ready"], n + 1)
        for k in range(KD + 2):
            if k < KD:
                nc.vector.scalar_tensor_tensor(out=pre[:, k, :], in0=pre[:, k, :], scalar=pcol(l, "g", k),
                                               in1=ln["rstd"], op0=ALU.mult, op1=ALU.mult).then_inc(E["ln_mul"], 1)
            if k >= 2 and l != last_layer:
                dve.wait_ge(E["hhi_ready"], KD * n + k - 1)
                nc.vector.scalar_tensor_tensor(out=H_lo[:, k - 2, :], in0=pre[:, k - 2, :], scalar=pcol(l, "b", k - 2),
                                               in1=H_hi[:, k - 2, :].bitcast(F32), op0=ALU.add, op1=ALU.subtract
                                               ).then_inc(E["h_ready"], 1)

    def act_rstd(act, link, dst, src, scale, eps):
        link(nc.scalar.activation(dst, src, ACT.Ln, bias=eps, scale=scale))
        return nc.scalar.activation(dst, dst, ACT.Exp, scale=-0.5)

    def act_ssd(act, l, link, astep, splitter):
        ns, S = nth_ssd[l], ssd
        U, S0 = first_unit[l], first_split[l]
        for e in range(2):
            splitter.ahead([0, 1] + SSD_SLOTS_1, e, S0 + e, U + e)
        if layer_no[l] == 0:
            act_params(act, link)
        raw, absx, ex, w1, lnw, dt, da, arow = dtv
        act.wait_ge(E["dt_x"], ns + 1)
        link(nc.scalar.activation(absx, raw, ACT.Abs))
        nc.scalar.activation(ex, absx, ACT.Exp, scale=-1.0).then_inc(E["dt_exp"], 1)
        act.wait_ge(E["dt_w"], ns + 1)
        nc.scalar.activation(lnw, w1, ACT.Ln).then_inc(E["dt_ln"], 1)

        def body(g):
            G = g + ns * SSD_GROUPS
            head = isinstance(g, int)

            def ahead(p, halves=(0, 1)):
                splitter.ahead(SSD_SLOTS_1 if head else SSD_SLOTS, p, S0 + 2 + g * SSD_TILES + p,
                               U + 2 + g * SSD_TILES + p, halves)

            def silu_of(k, dst, tile_no):
                if k < 4:
                    ahead(k)
                act.wait_ge(E["conv_ready"], G * 6 + k + 1)
                nc.scalar.activation(dst, S["conv"][:, k % 2, :], ACT.Silu, bias=pcol(l, "cb", tile_no)
                                     ).then_inc(E["conv_silu"], 1)

            def z_of(i):
                ahead(6 + i)
                act.wait_ge(unit_done, U + 3 + g * SSD_TILES + 6 + i)
                nc.scalar.activation(S["Z"][:, i, :], pj[i % 2], ACT.Silu).then_inc(E["z_ready"], 1)
            silu_of(0, S["B"], SSD_XT + g)
            if not head:
                act.wait_ge(E["cdec_ready"], G)
            silu_of(1, S["C"], SSD_XT + SSD_GROUPS + g)
            silu_of(2, S["X"][:, 0, :], g * 4)
            silu_of(3, S["X"][:, 1, :], g * 4 + 1)
            ahead(4, [0])
            if head:
                act.wait_ge(E["dst_pre"], ns + 1)
                nc.scalar.activation(S["dst"], S["dst"], ACT.Exp).then_inc(E["dst_ready"], 1)
            else:
                act.wait_ge(E["stat_done"], G)
                act_rstd(act, link, S["rstd"], bank[7][:, 0:T], 1.0 / 512, RMS_EPS).then_inc(E["rstd_ready"], 1)
            ahead(4, [1])
            act.wait_ge(E["diff_ready"], G + 1)
            for c in range(2):
                nc.scalar.activation(S["D"][:, c], S["D"][:, c], ACT.Exp).then_inc(E["d_exp"], 1)
            ahead(5, [0])
            nc.scalar.activation(S["E"], S["rows"][:, :, P:T], ACT.Exp).then_inc(E["e_exp"], 1)
            silu_of(4, S["X"][:, 2, :], g * 4 + 2)
            ahead(5, [1])
            silu_of(5, S["X"][:, 3, :], g * 4 + 3)
            z_of(0)
            act.wait_ge(E["bt_done"], G + 1)
            nc.scalar.activation(S["btok"], bank[7][:, 0:P], ACT.Copy).then_inc(E["btok_ready"], 1)
            z_of(1)
            act.wait_ge(E["st_done"], G + 1)
            nc.scalar.activation(S["st"], bank[7], ACT.Copy).then_inc(E["st_ready"], 1)
            z_of(2)
            z_of(3)
            for i in range(4):
                act.wait_ge(E["yg_ready"], G * 4 + i + 1)
                nc.scalar.activation(S["SQ"][:, i, :], S["YG"][:, i, :], ACT.Square).then_inc(E["sq_ready"], 1)
        body(0)
        with rolled(act, 1, SSD_GROUPS, [(astep, 1)] + splitter.steps(SSD_SLOTS)) as g:
            body(g)
        G = (ns + 1) * SSD_GROUPS
        act.wait_ge(E["stat_done"], G)
        act_rstd(act, link, S["rstd"], bank[7][:, 0:T], 1.0 / 512, RMS_EPS).then_inc(E["rstd_ready"], 1)

    def act_norm(act, l, link, splitter):
        n = layer_no[l]
        per = 1 if KINDS[l] == "mla" else 2
        slots = OUT_SLOTS[per * KD]
        turns = 4 if l != last_layer else 3
        with rolled(act, 0, turns, splitter.steps(slots)) as i:
            for p in range(4 * per):
                look_ahead(splitter, l, i, p)
        if l == last_layer:
            for p in range(4 * per):
                look_ahead(splitter, l, 3, p)
        nc.scalar.preload_act_table_set("natural_log")
        for k in range(KD):
            act.wait_ge(E["cent_ready"], KD * n + k + 1)
            if k >= SQ_RING:
                act.wait_ge(E["csq_used"], KD * n + k - SQ_RING + 1)
            nc.scalar.activation(ln["sq"][:, k % SQ_RING, :], pre[:, k, :], ACT.Square).then_inc(E["csq_ready"], 1)
        act.wait_ge(E["csq_used"], KD * (n + 1))
        act_rstd(act, link, ln["rstd"], bank[3][:, 0:T], 1.0 / D, LN_EPS).then_inc(E["lrstd_ready"], 1)
        for k in range(KD):
            act.wait_ge(E["ln_mul"], KD * n + k + 1)
            dst, done = (H_hi, E["hhi_ready"]) if l != last_layer else (pre, E["last_ready"])
            nc.scalar.activation(dst[:, k, :], pre[:, k, :], ACT.Identity, bias=pcol(l, "b", k)).then_inc(done, 1)


    mla = {}
    (mla["qkv"], mla["sq"], mla["rs"], mla["kr0"], mla["kr"], mla["cos"], mla["sin"], mla["rt"], mla["kT"], mla["qn"],
     mla["qr0"], mla["qr"], mla["V"], mla["S"], mla["mask"], mla["pT"], mla["mx"], mla["acc"]) = carve(
        (10, T), (10, T), (2, T), (T,), (T,), (T,), (T,), (2, T), (2, T), (2, T),
        (T,), (T,), (2, T), (2, 384), (384,), (2, 384), (16,), (16,))

    up_q = [ring[:, UP_SLOT + e, 0:MLA_QT * P].rearrange("p (k c) -> p k c", k=MLA_QT) for e in range(2)]
    up_rot = ring[:, UP_SLOT, MLA_QT * P:2 * MLA_QT * P].rearrange("p (k c) -> p k c", k=MLA_QT)

    def load_mla(sp, l, load, turns_of):
        w = a["mla_in_w"][0]
        U = first_unit[l]
        for p in range(MLA_QT + MLA_KVT):
            load(p % SLOTS, w_tile(w, p * P), U + p)
        for p in (10, 11):
            load(p % SLOTS, w_tile(w, MLA_COL_KR, 64), U + p)
        turns_of(lambda i, p: w_tile(w, MLA_COL_Z + p * P + i * 4 * P), U + 12, Z_SLOTS, Z_SLOTS, 4)
        for p in range(2):
            load(p, w_tile(a["mla_out_w"][0], p * P), first_unit[l, "out"] + p)
        qw = a["mla_q_up_w"][0].rearrange("(k p) n -> p k n", p=P)
        kvw = a["mla_kv_up_w"][0].rearrange("(k p) n -> p k n", p=P)

        def source(i, p):
            if p == 2:
                return [(ring[:, UP_SLOT + 2, :].rearrange("p (k c) -> p k c", k=MLA_KVT), kvw[:, :, ds(i * 512, 512)])]
            return [(up_q[p], qw[:, :, ds((2 * i + p) * 192, P)]),
                    (up_rot[:, :, p * 64:p * 64 + 64], qw[:, :, ds((2 * i + p) * 192 + P, 64)])]
        turns_of(source, U + 28, [2, 3, 4], [2, 3, 4], MLA_H // 2, sems=up_landed)

    def pe_mla(pe, l, tile, head_tile, hidden, first_hidden):
        M = mla
        S0 = first_split[l]
        for p in range(10):
            if p >= 2:
                pe.wait_ge(E["qkv_raw"], p - 1)
            tile(p % SLOTS, p, pj[p % 2], hidden, S0 + p, waits=first_hidden(l) if p == 0 else None)
        pe.wait_ge(E["qkv_raw"], 9)
        head_tile(4, pj[0], S0 + 10)

        def z_body(i):
            for p in range(4):
                if isinstance(i, int) and p < 2:
                    pe.wait_ge(E["qkv_raw"], 10)
                    if p == 1:
                        pe.wait_ge(E["kr_raw"], 1)
                else:
                    pe.wait_ge(E["mz_ready"], i * 4 + p - 1)
                tile(Z_SLOTS[p], p, pj[(p + 1) % 2], hidden, S0 + 12 + i * 4 + p)
        z_body(0)
        for j, (i0, i1) in enumerate(((0, MLA_QT), (MLA_QT, 10))):
            for i in range(i0, i1):
                pe.wait_ge(E["qkv_sq"], i + 1)
                mm = nc.tensor.matmul(bank[2 + j][:, 0:T], C["ones"], M["sq"][:, i, :], start=i == i0, stop=i == i1 - 1)
            mm.then_inc(E["qkv_stat"], 1)
        nc.tensor.matmul(bank[4][:, 0:T], C["rot"], M["kr0"], start=True, stop=True).then_inc(E["kr_rot"], 1)
        with pe.Fori(1, 4) as i:
            z_body(i)
        pe.wait_ge(E["qkv_ready"], 10)
        pe.wait_ge(E["kr_ready"], 1)
        pe.wait_ge(E["mz_ready"], 16)

        def attend(h):
            for e in range(2):
                pe.wait_ge(E["p_ready"], h * 2 + e + 1)
                for b in range(3):
                    mm = nc.tensor.transpose(bank[6 + e][:, b * P:(b + 1) * P], M["S"][:, e, b * P:(b + 1) * P], ident)
                mm.then_inc(E["pt_done"], 1)
            for e in range(2):
                pe.wait_ge(E["pt_ready"], h * 2 + e + 1)
                v0, v1 = M["V"][:, 0, e * P:(e + 1) * P], M["V"][:, 1, e * P:(e + 1) * P]
                nc.tensor.matmul(bank[6 + e][:, 0:P], v0, M["pT"][:, e, 0:P], start=True, stop=True)
                nc.tensor.matmul(bank[6 + e][:, P:T], v0, M["pT"][:, e, P:T], start=True, stop=False)
                nc.tensor.matmul(bank[6 + e][:, P:T], v1, M["pT"][:, e, T:T + P], start=False, stop=True
                                 ).then_inc(E["pv_done"], 1)

        def body(h):
            first = isinstance(h, int)
            for e in range(2):
                pe.wait_ge(up_landed[e], (h + 1) * 32)
                for k in range(MLA_QT):
                    mm = nc.tensor.matmul(bank[2 + e][:, 0:T], up_q[e][:, k, :], M["qkv"][:, k, :], start=k == 0,
                                          stop=k == MLA_QT - 1)
                mm.then_inc(E["up_done"], 1)
            for k in range(MLA_QT):
                mm = nc.tensor.matmul(bank[4][:, 0:T], up_rot[:, k, :], M["qkv"][:, k, :], start=k == 0,
                                      stop=k == MLA_QT - 1)
            mm.then_inc(unit_done, 2)
            pe.wait_ge(up_landed[2], (h + 1) * 16)
            w = ring[:, UP_SLOT + 2, :].rearrange("p (k c) -> p k c", k=MLA_KVT)
            for e in range(2):
                for k in range(MLA_KVT):
                    mm = nc.tensor.matmul(pj[e], w[:, k, e * T:e * T + P], M["qkv"][:, MLA_QT + k, :],
                                          start=k == 0, stop=k == MLA_KVT - 1)
                mm.then_inc(E["up_done"], 1)
            pe.wait_ge(E["qr_raw"], h + 1)
            nc.tensor.matmul(bank[4][:, T:2 * T], C["rot"], M["qr0"], start=True, stop=True).then_inc(E["rot_done"], 1)
            if not first:
                attend(h - 1)
            wv = w.rearrange("p k (e c) -> p k e c", e=2)
            for c in range(2):
                for k in range(MLA_KVT):
                    mm = nc.tensor.matmul(bank[5][:, c * T:(c + 1) * T], M["qkv"][:, MLA_QT + k, c * P:(c + 1) * P],
                                          wv[:, k, :, P:T], start=k == 0, stop=k == MLA_KVT - 1)
            mm.then_inc(unit_done, 1)
            pe.wait_ge(E["qr_ready"], h + 1)
            for e in range(2):
                pe.wait_ge(E["kt_ready"], h * 2 + e + 1)
                pe.wait_ge(E["qn_ready"], h * 2 + e + 1)
                if not first:
                    pe.wait_ge(E["o_ready"], h * 2 - 1 + e)
                r0 = 64 * e
                for qt, (c0, n) in enumerate(((0, P), (P, T))):
                    nc.tensor.matmul(bank[6 + e][:, c0:c0 + n], M["qn"][:, e, qt * P:(qt + 1) * P], M["kT"][:, e, 0:n],
                                     start=True, stop=False)
                    mm = nc.tensor.matmul(bank[6 + e][:, c0:c0 + n], M["qr"][r0:r0 + 64, qt * P:(qt + 1) * P],
                                          M["kr"][r0:r0 + 64, 0:n], start=False, stop=True)
                mm.then_inc(E["sc_done"], 1)
        body(0)
        with pe.Fori(1, MLA_H // 2) as h:
            body(h)
        attend(MLA_H // 2 - 1)

    def dve_mla(dve, l, link, step, splitter):
        M = mla
        U, S0 = first_unit[l], first_split[l]
        if layer_no[l]:
            dve.wait_ge(E["h_ready"], KD * layer_no[l])
        def angles():
            ang, n1 = M["S"][:, 0, 0:T], M["S"][:, 1, 0:T]
            link(nc.vector.tensor_copy(n1, posi[:]))
            link(nc.vector.tensor_scalar(ang, n1, inv_freq, None, ALU.mult))
            for dst, quarter in ((M["sin"], 0.0), (M["cos"], 0.25)):
                link(nc.vector.tensor_scalar(n1, ang, 1.0 / (2 * np.pi), quarter, ALU.mult, ALU.add))
                link(nc.vector.tensor_scalar(n1, n1, MAGIC, -MAGIC, ALU.add, ALU.add))
                link(nc.vector.scalar_tensor_tensor(out=dst, in0=n1, scalar=-TWO_PI_A, in1=ang, op0=ALU.mult, op1=ALU.add))
                link(nc.vector.scalar_tensor_tensor(out=dst, in0=n1, scalar=-TWO_PI_B, in1=dst, op0=ALU.mult, op1=ALU.add))
                link(nc.vector.scalar_tensor_tensor(out=dst, in0=n1, scalar=-TWO_PI_C, in1=dst, op0=ALU.mult, op1=ALU.add))
                link(nc.vector.tensor_scalar(dst, dst, 2 * np.pi * quarter, 3.1415925, ALU.add, ALU.min))
                nc.vector.tensor_scalar(dst, dst, -3.1415925, None, ALU.max).then_inc(E["trig_arg"], 1)
            nc.vector.tensor_copy(M["mask"][:, 0:P], C["negq"])
            nc.vector.memset(M["mask"][:, P:T], 0.0)
            nc.vector.tensor_copy(M["mask"][:, T:T + P], C["negq"])

        for p in range(10):
            splitter.ahead(MLA_SLOTS, p, S0 + p, U + p)
            dve.wait_ge(unit_done, U + p + 1)
            nc.vector.tensor_copy(M["qkv"][:, p, :], pj[p % 2]).then_inc(E["qkv_raw"], 1)
            if p == 4:
                angles()
        for p in (10, 11):
            splitter.ahead(MLA_SLOTS, p, S0 + p, U + p)
        dve.wait_ge(unit_done, U + 12)
        nc.vector.tensor_copy(M["kr0"], pj[0]).then_inc(E["kr_raw"], 1)
        for p in range(4):
            splitter.ahead(Z_SLOTS, p, S0 + 12 + p, U + 12 + p)

        def rotary(dst, x, rot):
            link(nc.vector.tensor_tensor(M["rt"][:, 0, :], rot, M["sin"], ALU.mult))
            link(nc.vector.tensor_tensor(M["rt"][:, 1, :], x, M["cos"], ALU.mult))
            return nc.vector.tensor_tensor(dst, M["rt"][:, 0, :], M["rt"][:, 1, :], ALU.add)
        dve.wait_ge(E["kr_rot"], 1)
        dve.wait_ge(E["trig"], 2)
        rotary(M["kr"], M["kr0"], bank[4][:, 0:T]).then_inc(E["kr_ready"], 1)
        for i in range(10):
            j = int(i >= MLA_QT)
            dve.wait_ge(E["qkv_rstd"], j + 1)
            nc.vector.scalar_tensor_tensor(out=M["qkv"][:, i, :], in0=M["qkv"][:, i, :],
                                           scalar=pcol(l, "kvn" if j else "qn", i - MLA_QT * j), in1=M["rs"][:, j, :],
                                           op0=ALU.mult, op1=ALU.mult).then_inc(E["qkv_ready"], 1)
        with dve.Fori(1, 4) as i:
            for p in range(4):
                splitter.ahead(Z_SLOTS, p, S0 + 12 + i * 4 + p, U + 12 + i * 4 + p)

        def gate(h):
            for e in range(2):
                dve.wait_ge(E["pv_done"], h * 2 + e + 1)
                nc.vector.tensor_tensor(Y[:, ds(h * 2 + e, 1), :], bank[6 + e][:, 0:T], Y[:, ds(h * 2 + e + 16, 1), :],
                                        ALU.mult).then_inc(E["o_ready"], 1)

        def body(h):
            for e in range(2):
                dve.wait_ge(E["up_done"], h * 4 + e + 3)
                nc.vector.tensor_copy(M["kT"][:, e, :], pj[e]).then_inc(E["kt_ready"], 1)
            dve.wait_ge(E["rot_done"], h + 1)
            rotary(M["qr"], M["qr0"], bank[4][:, T:2 * T]).then_inc(E["qr_ready"], 1)
            if not isinstance(h, int):
                gate(h - 1)
            for e in range(2):
                mx = M["mx"][:, 4 * e:4 * e + 2]
                dve.wait_ge(E["sc_done"], h * 2 + e + 1)
                link(nc.vector.tensor_tensor(M["S"][:, e, :], bank[6 + e][:, 0:384], M["mask"], ALU.add))
                link(nc.vector.tensor_reduce(mx[:, 0:1], M["S"][:, e, 0:P], AX.X, ALU.max))
                link(nc.vector.tensor_reduce(mx[:, 1:2], M["S"][:, e, P:384], AX.X, ALU.max))
                nc.vector.tensor_scalar(M["mx"][:, 4 * e + 2:4 * e + 4], mx, -MLA_SCALE, None, ALU.mult
                                        ).then_inc(E["sc_max"], 1)
            for e in range(2):
                dve.wait_ge(E["p_exp"], h * 2 + e + 1)
                link(nc.vector.reciprocal(M["acc"][:, 4 * e + 2:4 * e + 4], M["acc"][:, 4 * e:4 * e + 2]))
                link(nc.vector.tensor_scalar(M["S"][:, e, 0:P], M["S"][:, e, 0:P], M["acc"][:, 4 * e + 2:4 * e + 3], None,
                                             ALU.mult))
                nc.vector.tensor_scalar(M["S"][:, e, P:384], M["S"][:, e, P:384], M["acc"][:, 4 * e + 3:4 * e + 4], None,
                                        ALU.mult).then_inc(E["p_ready"], 1)
        body(0)
        with rolled(dve, 1, MLA_H // 2, [(step, 12)]) as h:
            body(h)
        gate(MLA_H // 2 - 1)

    def act_mla(act, l, link, astep, splitter):
        M = mla
        U, S0 = first_unit[l], first_split[l]
        U2 = U + 12 + 16
        for i in range(10):
            if i == 6:
                for j, dst in enumerate((M["sin"], M["cos"])):
                    act.wait_ge(E["trig_arg"], j + 1)
                    nc.scalar.activation(dst, dst, ACT.Sin).then_inc(E["trig"], 1)
            splitter.ahead(MLA_SLOTS, i, S0 + i, U + i)
            act.wait_ge(E["qkv_raw"], i + 1)
            nc.scalar.activation(M["sq"][:, i, :], M["qkv"][:, i, :], ACT.Square).then_inc(E["qkv_sq"], 1)
        for p in (10, 11):
            splitter.ahead(MLA_SLOTS, p, S0 + p, U + p)

        def z_body(i):
            for p in range(4):
                splitter.ahead(Z_SLOTS, p, S0 + 12 + i * 4 + p, U + 12 + i * 4 + p)
                act.wait_ge(unit_done, U + 12 + i * 4 + p + 1)
                nc.scalar.activation(Y[:, ds(i * 4 + (16 + p), 1), :], pj[(p + 1) % 2], ACT.Silu).then_inc(E["mz_ready"], 1)
        z_body(0)
        for j, n in enumerate((MLA_QR, MLA_KVR)):
            act.wait_ge(E["qkv_stat"], j + 1)
            act_rstd(act, link, M["rs"][:, j, :], bank[2 + j][:, 0:T], 1.0 / n, RMS_EPS).then_inc(E["qkv_rstd"], 1)
        with rolled(act, 1, 4, splitter.steps(Z_SLOTS)) as i:
            z_body(i)

        def probs_t(h):
            for e in range(2):
                act.wait_ge(E["pt_done"], h * 2 + e + 1)
                nc.scalar.activation(M["pT"][:, e, :], bank[6 + e][:, 0:384], ACT.Copy).then_inc(E["pt_ready"], 1)

        def body(h):
            for e in range(2):
                act.wait_ge(E["up_done"], h * 4 + e + 1)
                nc.scalar.activation(M["qn"][:, e, :], bank[2 + e][:, 0:T], ACT.Copy).then_inc(E["qn_ready"], 1)
            act.wait_ge(unit_done, U2 + h * 3 + 2)
            nc.scalar.activation(M["qr0"], bank[4][:, 0:T], ACT.Copy).then_inc(E["qr_raw"], 1)
            if not isinstance(h, int):
                probs_t(h - 1)
            act.wait_ge(unit_done, U2 + h * 3 + 3)
            nc.scalar.activation(M["V"], as3(bank[5], 2), ACT.Copy)
            for e in range(2):
                act.wait_ge(E["sc_max"], h * 2 + e + 1)
                link(nc.scalar.activation(M["S"][:, e, 0:P], M["S"][:, e, 0:P], ACT.Exp, scale=MLA_SCALE,
                                          bias=M["mx"][:, 4 * e + 2:4 * e + 3], accum_out=M["acc"][:, 4 * e:4 * e + 1]))
                nc.scalar.activation(M["S"][:, e, P:384], M["S"][:, e, P:384], ACT.Exp, scale=MLA_SCALE,
                                     bias=M["mx"][:, 4 * e + 3:4 * e + 4], accum_out=M["acc"][:, 4 * e + 1:4 * e + 2]
                                     ).then_inc(E["p_exp"], 1)
        body(0)
        with rolled(act, 1, MLA_H // 2, [(astep, 2)]) as h:
            body(h)
        probs_t(MLA_H // 2 - 1)

    gdn = {}
    (gdn["conv"], gdn["qk"], gdn["v"], gdn["sqk"], gdn["rs"], gdn["qkn"], gdn["rows"], gdn["D"], gdn["A"], gdn["kbe"],
     gdn["kdec"], gdn["vb"], gdn["vn"], gdn["S"], gdn["eg"], gdn["qdec"], gdn["sc"], gdn["tok"], gdn["gcol"],
     gdn["lev"], gdn["U"], gdn["T"], gdn["PM"], gdn["osq"]) = carve(
        (2, T), (2, T), (2, T), (2, T), (2, T), (2, T), (4, T), (4, P), (4, P), (4, P),
        (4, P), (4, P), (2, P), (2, P), (2, T), (2, T), (3, 2, 32), (2, 64), (2, 32),
        (2, 4 * P), (4, P), (4, P), (4, P), (2, T))
    gdn["lev"] = gdn["lev"].rearrange("p n (x l) -> p n x l", x=4)
    gdn["wT"], gdn["u"], gdn["ors"] = gdn["kbe"], gdn["vb"], gdn["rs"]
    gba = [gdn[n][HI64].rearrange("p x l -> p (x l)")[:, 0:T] for n in ("kbe", "kdec", "vb", "U", "PM", "A")]

    GDN_PLAN = {1: "turns", 2: "inv0", 13: "wu", 14: "out0", 21: "square", 22: "norm"}
    for n in range(5):
        GDN_PLAN[3 + 2 * n], GDN_PLAN[4 + 2 * n] = f"left{n}", f"right{n}"
    for c in (1, 2, 3):
        GDN_PLAN[13 + 2 * c], GDN_PLAN[14 + 2 * c] = f"new{c}", f"out{c}"
    DECAYS_AT, GRAMS_AT = 21, 23
    STATS_AT = 12

    def load_gdn(sp, l, load, turns_of):
        w, scr = a["gdn_in_w"][0], a["scr_gdn"]
        for p in range(2):
            load(p, w_tile(w, GDN_COL_B - 64), first_unit[l] + p)

        def rows_of(j):
            row = 2 * j if isinstance(j, int) else sp.snap(2 * j)
            if not isinstance(j, int):
                sp.wait_ge(unit_done, 1)
                sp.wait_ge(E["rows_used"], j)
                sp.wait_ge(E["eg_ready"], j)
            for half in range(2):
                sp.dma_start(gdn["rows"][:, 2 * half:2 * half + 2, :],
                             scr[ds(row + half * GDN_HV, 2), :].partition_broadcast(P)).then_inc(E["grows_in"], 16)

        def source(j, p):
            return w_tile(w, [j * P, GDN_COL_K + j * P, GDN_COL_V + j * T, GDN_COL_V + P + j * T, GDN_COL_Z + j * T,
                              GDN_COL_Z + P + j * T][p])

        def beside(j, p):
            if p < 5:
                return
            if isinstance(j, int):
                sp.wait_ge(E["gscr_ready"], 1)
                sp.dma_start(scr[0:32, :], gba[4][0:32]).then_inc(E["gscr_out"], 16)
                sp.dma_start(scr[32:64, :], gba[5][0:32]).then_inc(E["gscr_out"], 16)
                sp.wait_ge(E["gscr_out"], 32)
            rows_of(j)
        turns_of(source, first_unit[l] + 2, GDN_SLOTS_1, GDN_SLOTS, GDN_HK, beside)

    def pe_gdn(pe, l, contract, head_tile, hidden, first_hidden):
        S = gdn

        def halves(c):
            return c // 2, slice(64 * (c % 2), 64 * (c % 2) + 64)

        def chain(name, j):
            n = int(name[-1]) if name[-1].isdigit() else 0
            step = name.rstrip("0123456789")
            b2, b3, b4, b5, b6, b7 = (as3(bank[i], 4) for i in range(2, 8))
            if step == "grams":
                pe.wait_ge(E["nrm_ready"], 2 * (j + 1))
                for c in range(2):
                    cc = slice(c * P, (c + 1) * P)
                    nc.tensor.matmul(b2[:, c, :], S["qkn"][:, 1, cc], S["qkn"][:, 1, cc], start=True, stop=True)
                    mm = nc.tensor.matmul(b2[:, 2 + c, :], S["qkn"][:, 1, cc], S["qkn"][:, 0, cc], start=True, stop=True)
                mm.then_inc(E["kk_done"], 1)
            if step == "turns":
                pe.wait_ge(E["gy_ready"], j + 1)
                for c in range(2):
                    mm = nc.tensor.transpose(b3[:, c, :], S["qkn"][:, 1, c * P:(c + 1) * P], ident)
                mm.then_inc(E["kt_done"], 1)
                pe.wait_ge(E["gconv_silu"], 4 * (j + 1))
                for e in range(2):
                    for c in range(2):
                        mm = nc.tensor.transpose(b4[:, 2 * e + c, :], S["v"][:, e, c * P:(c + 1) * P], ident)
                mm.then_inc(E["vt_done"], 1)
            if step == "inv":
                pe.wait_ge(E["u_ready"], 6 * j + 1)
                for x in range(4):
                    mm = nc.tensor.transpose(b5[:, x, :], S["U"][:, x, :], ident)
                mm.then_inc(E["t0_done"], 1)
            if step == "left":
                pe.wait_ge(E["t_ready"], 5 * j + n + 1)
                pe.wait_ge(E["lev_ready"], 5 * j + n + 1)
                for x in range(4):
                    mm = nc.tensor.matmul(b5[:, x, :], S["lev"][:, n % 2, x, :], S["T"][:, x, :], start=True, stop=True)
                mm.then_inc(E["left_done"], 1)
            if step == "right":
                pe.wait_ge(E["pm_ready"], 5 * j + n + 1)
                for x in range(4):
                    mm = nc.tensor.matmul(b7[:, x, :], S["PM"][:, x, :], S["U"][:, x, :], start=True, stop=True)
                mm.then_inc(E["ru_done"], 1)
                if n < 4:
                    for x in range(4):
                        mm = nc.tensor.matmul(b6[:, x, :], S["U"][:, x, :], S["PM"][:, x, :], start=True, stop=True)
                    mm.then_inc(E["rt_done"], 1)
            if step == "wu":
                pe.wait_ge(E["u_ready"], 6 * j + 6)
                pe.wait_ge(E["kbe_ready"], j + 1)
                for x in range(4):
                    mm = nc.tensor.matmul(b5[:, x, :], S["kbe"][:, x, :], S["U"][:, x, :], start=True, stop=True)
                mm.then_inc(E["w_done"], 1)
                pe.wait_ge(E["vb_ready"], j + 1)
                for x in range(4):
                    mm = nc.tensor.matmul(b6[:, x, :], S["U"][:, x, :], S["vb"][:, x, :], start=True, stop=True)
                mm.then_inc(E["uv_done"], 1)
            if step == "new":
                c, h = halves(n)
                pe.wait_ge(E["s_ready"], 6 * j + 2 * n)
                for e in range(2):
                    mm = nc.tensor.matmul(b7[h, e, :], S["wT"][:, 2 * e + c, h], S["S"][:, e, :], start=True, stop=True)
                mm.then_inc(E["ws_done"], 1)
            if step == "out":
                c, h = halves(n)
                pe.wait_ge(E["vn_ready"], 4 * j + n + 1)
                if n == 0:
                    pe.wait_ge(E["qdec_ready"], 2 * (j + 1))
                    pe.wait_ge(E["kdec_ready"], j + 1)
                if n < 3:
                    for e in range(2):
                        mm = nc.tensor.matmul(b4[:, e, :], S["kdec"][h, 2 * e + c, :], S["vn"][h, e, :], start=True, stop=True)
                    mm.then_inc(E["ds_done"], 1)
                for e in range(2):
                    o = bank[3][:, e * T + n * 64:e * T + n * 64 + 64]
                    if n:
                        nc.tensor.matmul(o, S["S"][:, e, :], S["qdec"][:, e, n * 64:n * 64 + 64], start=True, stop=False)
                    mm = nc.tensor.matmul(o, S["vn"][h, e, :], S["D"][h, 2 * e + c, h], start=n == 0, stop=True)
                mm.then_inc(E["os_done"], 1)
            if step == "norm":
                pe.wait_ge(E["osq_ready"], j + 1)
                nc.tensor.matmul(bank[7], C["ones"], S["osq"].rearrange("p e t -> p (e t)"), start=True, stop=True
                                 ).then_inc(E["ostat_done"], 1)

        def body(j):
            first = isinstance(j, int)
            slots = GDN_SLOTS_1 if first else GDN_SLOTS
            for q in range(4 * GDN_TILES):
                p = q // 4
                if not first and q in GDN_PLAN:
                    chain(GDN_PLAN[q], j - 1)
                if q == GRAMS_AT:
                    chain("grams", j)
                if q == STATS_AT:
                    pe.wait_ge(E["sqk_ready"], 2 * (j + 1))
                    nc.tensor.matmul(bank[2], C["ones"], S["sqk"].rearrange("p e t -> p (e t)"), start=True, stop=True
                                     ).then_inc(E["nstat_done"], 1)
                if q % 4 == 0:
                    if p < 2:
                        if first:
                            if p == 1:
                                pe.wait_ge(E["ba_raw"], 1)
                        else:
                            pe.wait_ge(E["gz_ready"], 2 * j - 1 + p)
                    elif p < 6:
                        pe.wait_ge(E["gconv_ready"], 4 * j + p - 1)
                mm = contract(slots[p], p, pj[p % 2], hidden, range(4 * (q % 4), 4 * (q % 4) + 4),
                              s=first_split[l] + 2 + j * GDN_TILES + p)
                if q % 4 == 3:
                    mm.then_inc(unit_done, 1)
                if first and q == 7:
                    pe.wait_ge(E["ba_ready"], 1)
                    for c in range(2):
                        mm = nc.tensor.transpose(bank[2][:, c * 64:(c + 1) * 64], gba[5][:, c * P:(c + 1) * P],
                                                 ident[HI64, HI64])
                    mm.then_inc(E["ba_t"], 1)
                if first and q == 13:
                    pe.wait_ge(E["ba_tok"], 1)
                    for c in range(2):
                        nc.tensor.matmul(bank[5][64:96, c * P:(c + 1) * P], S["tok"][:, c, 32:64], C["tri64"],
                                         start=True, stop=True)
                    nc.tensor.matmul(bank[6][:, 0:64], C["tri64"], S["tok"][:, :, 32:64], start=True, stop=True)
                    nc.tensor.matmul(bank[6][:, 64:128], C["blk64"], S["tok"][:, :, 32:64], start=True, stop=True
                                     ).then_inc(E["gc_done"], 1)

        head_tile(0, pj[1], first_split[l], first_hidden(l))
        body(0)
        with pe.Fori(1, GDN_HK) as j:
            body(j)
        for q in sorted(GDN_PLAN):
            chain(GDN_PLAN[q], GDN_HK - 1)

    def gdn_ahead(splitter, l, j, p):
        splitter.ahead(GDN_SLOTS_1 if isinstance(j, int) else GDN_SLOTS, p, first_split[l] + 2 + j * GDN_TILES + p,
                       first_unit[l] + 2 + j * GDN_TILES + p)

    def dve_gdn(dve, l, link, step):
        S = gdn
        U, S0 = first_unit[l], first_split[l]
        flat = lambda ap: ap.rearrange("p x l -> p (x l)")
        if layer_no[l]:
            dve.wait_ge(E["h_ready"], KD * layer_no[l])
        raw, ab, ex, w1, sig, bg = gba
        lnw = S["osq"][HI64, 0, :]
        da, dt = S["ors"][HI64, 0, :], S["ors"][HI64, 1, :]
        sg = S["osq"][64:96, 1, :]
        nc.vector.memset(hd[:, 15:16], 0.0).then_inc(E["gy_ready"], 1)
        dve.wait_ge(unit_done, U + 2)
        nc.vector.tensor_scalar(raw, pj[1][HI64], hd[HI64, 8:9], None, ALU.add).then_inc(E["ba_raw"], 1)
        dve.wait_ge(E["ba_exp"], 1)
        nc.vector.tensor_scalar(w1, ex, 1.0, None, ALU.add).then_inc(E["ba_w"], 1)
        dve.wait_ge(E["ba_w"], 1)
        link(nc.vector.tensor_scalar(dt, w1, 1.0, 0.0, ALU.subtract, ALU.is_equal))
        link(nc.vector.scalar_tensor_tensor(out=da, in0=w1, scalar=-1.0, in1=dt, op0=ALU.add, op1=ALU.add))
        link(nc.vector.reciprocal(da, da))
        link(nc.vector.tensor_tensor(da, da, ex, ALU.mult))
        dve.wait_ge(E["ba_ln"], 1)
        link(nc.vector.tensor_tensor(dt, dt, lnw, ALU.add))
        link(nc.vector.tensor_tensor(da, da, dt, ALU.mult))
        link(nc.vector.scalar_tensor_tensor(out=dt, in0=raw, scalar=0.0, in1=da, op0=ALU.max, op1=ALU.add))
        link(nc.vector.tensor_scalar(bg[32:64], dt[32:64], hd[96:128, 10:11], -1.0, ALU.mult, ALU.mult))
        dve.wait_ge(E["ba_sig"], 1)
        link(nc.vector.tensor_scalar(sg, sg, 1.0, None, ALU.add))
        nc.vector.reciprocal(bg[0:32], sg).then_inc(E["ba_ready"], 1)

        def k_scaled(j, name, at):
            dve.wait_ge(E["kt_done"], j + 1)
            for e in range(2):
                for c in range(2):
                    ins = nc.vector.tensor_scalar(S[name][:, 2 * e + c, :], as3(bank[3], 4)[:, c, :],
                                                  S["sc"][:, at, c, ds(2 * j + e, 1)], None, ALU.mult)
            ins.then_inc(E[name + "_ready"], 1)

        def v_scaled(j):
            dve.wait_ge(E["vt_done"], j + 1)
            for e in range(2):
                for c in range(2):
                    ins = nc.vector.tensor_scalar(S["vb"][:, 2 * e + c, :], as3(bank[4], 4)[:, 2 * e + c, :],
                                                  S["tok"][:, c, ds(2 * j + e, 1)], None, ALU.mult)
            ins.then_inc(E["vb_ready"], 1)

        def q_scaled(j):
            dve.wait_ge(E["eg_ready"], j + 1)
            for e in range(2):
                nc.vector.tensor_tensor(S["qdec"][:, e, :], S["qkn"][:, 0, :], S["eg"][:, e, :], ALU.mult
                                        ).then_inc(E["qdec_ready"], 1)

        def exponents(j):
            dve.wait_ge(E["grows_in"], 32 * (j + 1))
            if not isinstance(j, int):
                dve.wait_ge(E["os_done"], 4 * j)
            for e in range(2):
                for c in range(2):
                    ins = nc.vector.scalar_tensor_tensor(
                        out=S["D"][:, 2 * e + c, :], in0=S["rows"][:, e, c * P:(c + 1) * P],
                        scalar=S["gcol"][:, c, ds(2 * j + e, 1)], in1=C["neg64"], op0=ALU.subtract, op1=ALU.min)
            ins.then_inc(E["gdiff_ready"], 1)

        def respond(name, j):
            n = int(name[-1]) if name[-1].isdigit() else 0
            kind = name.rstrip("0123456789")
            b2, b3, b4, b5, b6, b7 = (as3(bank[i], 4) for i in range(2, 8))
            if kind == "grams":
                dve.wait_ge(E["kk_done"], j + 1)
                dve.wait_ge(E["gdecay"], j + 1)
                D4 = S["D"].rearrange("p (e c) l -> p e c l", e=2)
                A4 = S["A"].rearrange("p (e c) l -> p e c l", e=2)
                for e in range(2):
                    ins = nc.vector.tensor_tensor(A4[:, e], D4[:, e], b2[:, 0:2, :], ALU.mult)
                link(ins)
                link(nc.vector.tensor_tensor(flat(S["A"]), flat(S["A"]), S["rows"][:, 2:4, :].rearrange("p e t -> p (e t)"),
                                             ALU.mult))
                lev1 = C["lev1"].rearrange("p (o l) -> p o l", o=1).broadcast_to([P, 4, P])
                idb = ident.rearrange("p (o l) -> p o l", o=1).broadcast_to([P, 4, P])
                link(nc.vector.tensor_tensor(S["U"], S["A"], lev1, ALU.mult))
                nc.vector.tensor_tensor(S["U"], idb, S["U"], ALU.subtract).then_inc(E["u_ready"], 1)
                for e in range(2):
                    ins = nc.vector.tensor_tensor(D4[:, e], D4[:, e], b2[:, 2:4, :], ALU.mult)
                ins.then_inc(E["rows_used"], 1)
            if kind == "inv":
                dve.wait_ge(E["t0_done"], j + 1)
                nc.vector.tensor_copy(flat(S["T"]), bank[5]).then_inc(E["t_ready"], 1)
            if kind == "left":
                dve.wait_ge(E["left_done"], 5 * j + n + 1)
                nc.vector.tensor_copy(flat(S["PM"]), bank[5]).then_inc(E["pm_ready"], 1)
                if n == 0:
                    k_scaled(j, "kbe", 0)
                if n == 1:
                    k_scaled(j, "kdec", 1)
                if n == 2:
                    v_scaled(j)
                if n == 3:
                    q_scaled(j)
            if kind == "right":
                dve.wait_ge(E["ru_done"], 5 * j + n + 1)
                if n < 4:
                    dve.wait_ge(E["rt_done"], 4 * j + n + 1)
                    nc.vector.tensor_tensor(flat(S["T"]), flat(S["T"]), bank[6], ALU.subtract).then_inc(E["t_ready"], 1)
                nc.vector.tensor_tensor(flat(S["U"]), flat(S["U"]), bank[7], ALU.subtract).then_inc(E["u_ready"], 1)
            if kind == "wu":
                dve.wait_ge(E["w_done"], j + 1)
                link(nc.vector.tensor_copy(flat(S["wT"]), bank[5]))
                dve.wait_ge(E["uv_done"], j + 1)
                nc.vector.tensor_copy(flat(S["u"]), bank[6]).then_inc(E["u2_ready"], 1)
                dve.wait_ge(E["u2_ready"], j + 1)
                us = S["u"].rearrange("p (e c) l -> p e c l", e=2)
                nc.vector.tensor_copy(S["vn"][0:64], us[0:64, :, 0, :]).then_inc(E["vn_ready"], 1)
            if kind == "new":
                c, h = n // 2, slice(64 * (n % 2), 64 * (n % 2) + 64)
                us = S["u"].rearrange("p (e c) l -> p e c l", e=2)
                dve.wait_ge(E["ws_done"], 3 * j + n)
                nc.vector.tensor_tensor(S["vn"][h], us[h, :, c, :], b7[h, 0:2, :], ALU.subtract).then_inc(E["vn_ready"], 1)
            if kind == "out" and n < 3:
                dve.wait_ge(E["ds_done"], 3 * j + n + 1)
                dve.wait_ge(E["os_done"], 4 * j + n + 1)
                for e in range(2):
                    last = n * 64 + 63
                    if n == 0:
                        nc.vector.tensor_copy(S["S"][:, e, :], b4[:, e, :]).then_inc(E["s_ready"], 1)
                    else:
                        nc.vector.scalar_tensor_tensor(out=S["S"][:, e, :], in0=S["S"][:, e, :],
                                                       scalar=S["eg"][:, e, last:last + 1], in1=b4[:, e, :],
                                                       op0=ALU.mult, op1=ALU.add).then_inc(E["s_ready"], 1)
            if kind == "norm":
                dve.wait_ge(E["ors_ready"], j + 1)
                link(nc.vector.scalar_tensor_tensor(out=flat(S["osq"]), in0=bank[3], scalar=pcol(l, "norm", 0),
                                                    in1=flat(S["ors"]), op0=ALU.mult, op1=ALU.mult))
                dve.wait_ge(E["gz_ready"], 2 * (j + 1))
                yy = Y[:, ds(2 * j, 2), :]
                nc.vector.tensor_tensor(yy, S["osq"], yy, ALU.mult).then_inc(E["gy_ready"], 1)

        def body(j):
            first = isinstance(j, int)
            for q in range(4 * GDN_TILES):
                p = q // 4 - 1
                if 0 <= p < 4 and q % 4 < 3:
                    src, dst = pj[p % 2], S["conv"][:, p % 2, :]
                    tile_no = [j, GDN_HK + j, 2 * GDN_HK + 2 * j, 2 * GDN_HK + 2 * j + 1][p]
                    if q % 4 == 0:
                        dve.wait_ge(unit_done, U + 3 + j * GDN_TILES + p)
                        if not (first and p < 2):
                            dve.wait_ge(E["gconv_silu"], 4 * j + p - 1)
                        link(nc.vector.tensor_scalar(dst, src, pcol(l, "tap3", tile_no), None, ALU.mult))
                    t = q % 4 + 1
                    ins = nc.vector.scalar_tensor_tensor(out=dst[:, t:T], in0=src[:, 0:T - t],
                                                         scalar=pcol(l, f"tap{3 - t}", tile_no), in1=dst[:, t:T],
                                                         op0=ALU.mult, op1=ALU.add)
                    if t < 3:
                        link(ins)
                    else:
                        ins.then_inc(E["gconv_ready"], 1)
                if q == DECAYS_AT:
                    exponents(j)
                if not first and q in GDN_PLAN:
                    respond(GDN_PLAN[q], j - 1)
                if q == GRAMS_AT:
                    respond("grams", j)
                if q == STATS_AT + 2:
                    dve.wait_ge(E["rs_ready"], j + 1)
                    nc.vector.scalar_tensor_tensor(out=S["qkn"][:, 0, :], in0=S["qk"][:, 0, :], scalar=P ** -0.5,
                                                   in1=S["rs"][:, 0, :], op0=ALU.mult, op1=ALU.mult
                                                   ).then_inc(E["nrm_ready"], 1)
                    nc.vector.tensor_tensor(S["qkn"][:, 1, :], S["qk"][:, 1, :], S["rs"][:, 1, :], ALU.mult
                                            ).then_inc(E["nrm_ready"], 1)
                if first and q == 7:
                    dve.wait_ge(E["ba_t"], 1)
                    nc.vector.tensor_copy(S["tok"], as3(bank[2][:, 0:P], 2)).then_inc(E["ba_tok"], 1)
                if first and q == 13:
                    dve.wait_ge(E["gc_done"], 1)
                    link(nc.vector.tensor_copy(S["gcol"], as3(bank[6][:, 0:64], 2)))
                    nc.vector.tensor_tensor(S["sc"][:, 1], as3(bank[6][:, 64:128], 2), S["gcol"], ALU.subtract
                                            ).then_inc(E["gsc_pre"], 1)
                    nc.vector.tensor_copy(gba[4][0:32], bank[5][64:96, 0:T]).then_inc(E["gscr_ready"], 1)
                    dve.wait_ge(E["gsc_exp"], 2)
                    link(nc.vector.tensor_tensor(S["sc"][:, 0], S["sc"][:, 0], S["tok"][:, :, 0:32], ALU.mult))
        body(0)
        with rolled(dve, 1, GDN_HK, [(step, 17)]) as j:
            body(j)
        for q in sorted(GDN_PLAN):
            respond(GDN_PLAN[q], GDN_HK - 1)

    def act_gdn(act, l, link, astep, splitter):
        S = gdn
        U, S0 = first_unit[l], first_split[l]
        for e in range(2):
            splitter.ahead([0, 1] + GDN_SLOTS_1, e, S0 + e, U + e)
        flat = lambda ap: ap.rearrange("p x l -> p (x l)")
        raw, ab, ex, w1, sig, bg = gba
        lnw, sg = S["osq"][HI64, 0, :], S["osq"][64:96, 1, :]
        act.wait_ge(E["ba_raw"], 1)
        link(nc.scalar.activation(ab, raw, ACT.Abs))
        nc.scalar.activation(ex, ab, ACT.Exp, scale=-1.0).then_inc(E["ba_exp"], 1)
        nc.scalar.activation(sg, raw[0:32], ACT.Exp, scale=-1.0).then_inc(E["ba_sig"], 1)
        act.wait_ge(E["ba_w"], 1)
        nc.scalar.activation(lnw, w1, ACT.Ln).then_inc(E["ba_ln"], 1)

        def ln_and_exp():
            nc.scalar.preload_act_table_set("natural_log_exp_and_others")

        def decays(j):
            act.wait_ge(E["gdiff_ready"], j + 1)
            nc.scalar.activation(flat(S["D"]), flat(S["D"]), ACT.Exp).then_inc(E["gdecay"], 1)
            nc.scalar.activation(flat(S["eg"]), S["rows"][:, 0:2, :].rearrange("p e t -> p (e t)"), ACT.Exp
                                 ).then_inc(E["eg_ready"], 1)

        def respond(name, j, following=None):
            if name == "square":
                ln_and_exp()
                act.wait_ge(E["os_done"], 4 * (j + 1))
                nc.scalar.activation(flat(S["osq"]), bank[3], ACT.Square).then_inc(E["osq_ready"], 1)
                if following is not None:
                    decays(following)
            if name == "norm":
                act.wait_ge(E["ostat_done"], j + 1)
                act.wait_ge(E["nrm_ready"], 2 * (j + 1) if isinstance(j, int) else 2 * j + 4)
                act_rstd(act, link, flat(S["ors"]), bank[7], 1.0 / P, RMS_EPS).then_inc(E["ors_ready"], 1)

        def body(j):
            first = isinstance(j, int)
            for q in range(4 * GDN_TILES + 1):
                if q and q % 4 == 0:
                    gdn_ahead(splitter, l, j, q // 4 - 1)
                if first and q == DECAYS_AT:
                    ln_and_exp()
                    decays(j)
                if not first and q in GDN_PLAN:
                    respond(GDN_PLAN[q], j - 1, following=j)
                if q == STATS_AT:
                    ln_and_exp()
                    act.wait_ge(E["nstat_done"], j + 1)
                    act_rstd(act, link, flat(S["rs"]), bank[2], 1.0, RMS_EPS).then_inc(E["rs_ready"], 1)
                if first and q == 14:
                    act.wait_ge(E["gsc_pre"], 1)
                    nc.scalar.activation(S["sc"][:, 0], S["gcol"], ACT.Exp).then_inc(E["gsc_exp"], 1)
                    nc.scalar.activation(S["sc"][:, 1], S["sc"][:, 1], ACT.Exp).then_inc(E["gsc_exp"], 1)
                if q % 4 == 3 and 4 <= q <= 19:
                    p = q // 4 - 1
                    act.wait_ge(E["gconv_ready"], 4 * j + p + 1)
                    if p == 2 and not first:
                        act.wait_ge(E["vt_done"], j)
                    dst = S["qk"][:, p, :] if p < 2 else S["v"][:, p - 2, :]
                    nc.scalar.activation(dst, S["conv"][:, p % 2, :], ACT.Silu).then_inc(E["gconv_silu"], 1)
                    if p < 2:
                        act.wait_ge(E["gconv_silu"], 4 * j + p + 1)
                        nc.scalar.activation(S["sqk"][:, p, :], dst, ACT.Square).then_inc(E["sqk_ready"], 1)
                if q in (20, 24):
                    e = (q - 20) // 4
                    act.wait_ge(unit_done, U + 3 + j * GDN_TILES + 4 + e)
                    nc.scalar.activation(Y[:, ds(2 * j + e, 1), :], pj[e], ACT.Silu).then_inc(E["gz_ready"], 1)
        body(0)
        with rolled(act, 1, GDN_HK, [(astep, 2)] + splitter.steps(GDN_SLOTS)) as j:
            body(j)
        respond("square", GDN_HK - 1)
        respond("norm", GDN_HK - 1)

    def pool_gdn(pool, l, splitter):
        U, S0 = first_unit[l], first_split[l]

        def level(j, n):
            if n == 0:
                pool.wait_ge(E["u_ready"], 6 * j + 1)
            if n >= 2:
                pool.wait_ge(E["left_done"], 5 * j + n - 1)
            by = C[f"lev{LEVELS[n]}"].rearrange("p (o l) -> p o l", o=1).broadcast_to([P, 4, P])
            nc.gpsimd.tensor_tensor(gdn["lev"][:, n % 2], gdn["A"], by, ALU.mult).then_inc(E["lev_ready"], 1)
        splitter.hand_over(True, S0 + 2)
        for e in range(2):
            splitter.ahead([0, 1] + GDN_SLOTS_1, e, S0 + e, U + e)
        for p in range(GDN_TILES):
            gdn_ahead(splitter, l, 0, p)
        with pool.Fori(1, GDN_HK) as j:
            for p, levels in enumerate(((0, 1, 2, 3), (4,), (), (), (), ())):
                for n in levels:
                    level(j - 1, n)
                gdn_ahead(splitter, l, j, p)
        splitter.hand_over(False, None)
        for n in range(5):
            level(GDN_HK - 1, n)

    def pool_ssd(pool, l, splitter):
        U, S0, ns = first_unit[l], first_split[l], nth_ssd[l]
        for e in range(2):
            splitter.ahead([0, 1] + SSD_SLOTS_1, e, S0 + e, U + e)

        def square_sum(G):
            pool.wait_ge(E["sq_ready"], 4 * G)
            nc.gpsimd.tensor_tensor(ssd["SQ"][:, 0:2, :], ssd["SQ"][:, 0:2, :], ssd["SQ"][:, 2:4, :], ALU.add
                                    ).then_inc(E["sq_sum"], 1)
            pool.wait_ge(E["sq_sum"], 2 * (G - ns) - 1)
            nc.gpsimd.tensor_tensor(ssd["SQ"][:, 0, :], ssd["SQ"][:, 0, :], ssd["SQ"][:, 1, :], ALU.add
                                    ).then_inc(E["sq_sum"], 1)

        def body(g):
            G = g + ns * SSD_GROUPS
            if not isinstance(g, int):
                square_sum(G)
            for p in range(SSD_TILES):
                splitter.ahead(SSD_SLOTS_1 if isinstance(g, int) else SSD_SLOTS, p, S0 + 2 + g * SSD_TILES + p,
                               U + 2 + g * SSD_TILES + p)
                if p == 4:
                    pool.wait_ge(E["e_exp"], G + 1)
                    pool.wait_ge(E["conv_silu"], G * 6 + 2)
                    by = ssd["C"][:, P:T].rearrange("p (o l) -> p o l", o=1).broadcast_to([P, SSD_R, P])
                    nc.gpsimd.tensor_tensor(ssd["E"], ssd["E"], by, ALU.mult).then_inc(E["cdec_ready"], 1)
        body(0)
        with pool.Fori(1, SSD_GROUPS) as g:
            body(g)

    def pool_mla(pool, l, splitter):
        U, S0 = first_unit[l], first_split[l]
        for p in range(12):
            splitter.ahead(MLA_SLOTS, p, S0 + p, U + p)
        with pool.Fori(0, 4) as i:
            for p in range(4):
                splitter.ahead(Z_SLOTS, p, S0 + 12 + i * 4 + p, U + 12 + i * 4 + p)

    block = ctx.enter_context(nc.Block())

    @block.sync
    def _(sp):
        last = [0] * SLOTS
        copies = [0]

        def load(p, src, u, free=None, landed_as=None):
            free = last[p] if free is None else free
            if not isinstance(free, int):
                sp.wait_ge(unit_done, 1)
            if not (isinstance(free, int) and free == 0):
                sp.wait_ge(unit_done, free)
            if isinstance(src, list):
                for to, part in src:
                    sp.dma_start(to, part).then_inc(landed_as, 16)
                if isinstance(u, int):
                    last[p] = u + 1
                return
            dst = slot(p)
            if src.shape[-1] == 64:
                sp.dma_start(dst[:, :, 64:P], src).then_inc(E["copy_in"], 16)
                copies[0] += 16
                sp.wait_ge(E["copy_in"], copies[0])
                dst = dst[:, :, 0:64]
            sp.dma_start(dst, src).then_inc(landed[p], 16)
            if isinstance(u, int):
                last[p] = u + 1

        def turns_of(source, u0, slots_1, slots, turns, beside=None, sems=None, skip=0):
            n = len(slots)
            for p, q in enumerate(slots_1):
                if p >= skip:
                    load(q, source(0, p), u0 + p, landed_as=sems and sems[p])
                if beside:
                    beside(0, p)
            with sp.Fori(1, turns) as i:
                free = []
                for p, q in enumerate(slots):
                    same = [r for r in range(p) if slots[r] == q]
                    before = [r for r in range(n) if slots[r] == q]
                    assert same or all(r <= before[-1] for r in range(n) if slots_1[r] == q)
                    free.append(i * n + (u0 + same[-1] + 1) if same else (i - 1) * n + (u0 + before[-1] + 1))
                if n == SSD_TILES:
                    free[5] = free[6] = sp.snap(free[6])
                for p, q in enumerate(slots):
                    load(q, source(i, p), None, free[p], landed_as=sems and sems[p])
                    if beside:
                        beside(i, p)
            for p, q in enumerate(slots):
                last[q] = u0 + (turns - 1) * n + p + 1

        def load_out(l, w, kt):
            per = kt // KD
            slots = OUT_SLOTS[kt]

            def source(i, p):
                return w_tile(w, i * 512 + p // per * P, k0=p % per * KD)
            turns_of(source, first_unit[l, "out"], slots, slots, 4, skip=2 if KINDS[l] == "mla" else 0)

        sp.dma_start(cst[:, 0:P], a["consts"][:, 0:P]).then_inc(E["ident_in"], 16)
        sp.dma_start(xrows[:, 0, :], a["x"][0, 0:P, :]).then_inc(E["x_in"], 16)
        for l in layers:
            if KINDS[l] == "ssd":
                load_ssd(sp, l, load, turns_of)
                load_out(l, a["ssd_out_w"][l // 3], 32)
            if KINDS[l] == "mla":
                load_mla(sp, l, load, turns_of)
                load_out(l, a["mla_out_w"][0], 16)
            if KINDS[l] == "gdn":
                load_gdn(sp, l, load, turns_of)
                load_out(l, a["gdn_out_w"][0], 32)
        sp.wait_ge(E["out_rows"], 8)
        for c in range(2):
            sp.dma_start(a["out"][0, c * P:(c + 1) * P, :], xrows[:, c, :]).then_inc(E["out_done"], 16)
        sp.wait_ge(E["out_done"], 32)

    @block.tensor
    def _(pe):
        def contract(q, p, dst, rhs, ks, k_start=0, k_stop=KD - 1, waits=None, s=None):
            for k in ks:
                if k == ks[0] and k < KD // 2 and ks[0] == 0:
                    pe.wait_ge(lo0_ready, s + 1)
                if k == KD // 2:
                    pe.wait_ge(lo1_ready, s + 1)
                if waits is not None:
                    waits(k)
                w_hi = W_hi[:, p % 2, k * P:(k + 1) * P]
                x_hi, x_lo = rhs(k)
                nc.tensor.matmul(dst, w_hi, x_hi, start=k == k_start, stop=False)
                mm = nc.tensor.matmul(dst, w_hi, x_lo, start=False, stop=False)
                if k == KD // 2 - 1:
                    mm.then_inc(half_done, 1)
                mm = nc.tensor.matmul(dst, ring_lo[:, q, k * P:(k + 1) * P], x_hi, start=False, stop=k == k_stop)
            return mm

        def tile(q, p, dst, rhs, s, k_start=0, k_stop=KD - 1, waits=None):
            contract(q, p, dst, rhs, range(KD), k_start, k_stop, waits, s).then_inc(unit_done, 1)

        def head_tile(q, dst, s, waits=None):
            pe.wait_ge(lo1_ready, s + 1)
            contract(q, 0, dst, hidden, range(0, KD // 2), waits=waits, s=s).then_inc(unit_done, 1)
            pe.wait_ge(lo0_ready, s + 2)
            pe.wait_ge(lo1_ready, s + 2)
            for k in range(KD // 2, KD):
                if waits is not None:
                    waits(k)
                w_hi = W_hi[:, 1, k * P:(k + 1) * P]
                nc.tensor.matmul(dst, w_hi, H_hi[:, k, :], start=False, stop=False)
                mm = nc.tensor.matmul(dst, w_hi, H_lo[:, k, :], start=False, stop=False)
                if k == KD // 2:
                    mm.then_inc(half_done, 1)
                mm = nc.tensor.matmul(dst, ring_lo[:, q + 1, k * P:(k + 1) * P], H_hi[:, k, :], start=False,
                                      stop=k == KD - 1)
            mm.then_inc(unit_done, 1)

        def hidden(k):
            return H_hi[:, k, :], H_lo[:, k, :]

        def first_hidden(l):
            n = layer_no[l]
            return lambda k: pe.wait_ge(*((E["h_ready"], KD * (n - 1) + k + 1) if n else (E["h_in"], k // 4 * 2 + 2)))

        def out_and_norm(l, kt):
            per = kt // KD
            n = layer_no[l]
            slots = OUT_SLOTS[kt]

            def body(i):
                for t in range(4):
                    if t >= 2 or not isinstance(i, int):
                        pe.wait_ge(E["pre_ready"], KD * n + i * 4 + t - 1)
                    for h in range(per):
                        p = t * per + h

                        def gated(k):
                            return Y_hi[:, h * KD + k, :], Y_lo[:, h * KD + k, :]
                        first = None
                        if isinstance(i, int) and t == 0:
                            def first(k):
                                c, n_dve = h * 4 + k // 4, 3 * per
                                if c < n_dve:
                                    pe.wait_ge(E["ysplit"], y_split_base[l] * 3 // 4 + c + 1)
                                else:
                                    pe.wait_ge(E["ysplit_end"], y_split_base[l] // 4 + c - n_dve + 1)
                        tile(slots[p], p, pj[t % 2], gated, first_split[l, "out"] + i * 4 * per + p,
                             k_start=0 if h == 0 else None, k_stop=KD - 1 if h == per - 1 else None, waits=first)
            body(0)
            with pe.Fori(1, 4) as i:
                body(i)
            pe.wait_ge(E["sum_ready"], n + 1)
            nc.tensor.matmul(bank[2][:, 0:T], C["ones"], ln["sum"], start=True, stop=True).then_inc(E["mean_done"], 1)
            for k in range(KD):
                pe.wait_ge(E["csq_ready"], KD * n + k + 1)
                mm = nc.tensor.matmul(bank[3][:, 0:T], C["ones"], ln["sq"][:, k % SQ_RING, :], start=k == 0, stop=k == KD - 1)
                mm.then_inc(E["csq_used"], 1)

        pe.wait_ge(E["ident_in"], 16)
        pe.wait_ge(E["x_in"], 32)
        for i in range(8):
            if i >= 4:
                pe.wait_ge(E["h_in"], i - 3)
            for j in range(4):
                c, k = i % 2, i // 2 * 4 + j
                mm = nc.tensor.transpose(bank[4 + i % 4][:, j * P:(j + 1) * P], xrows[:, c, k * P:(k + 1) * P], ident)
            mm.then_inc(E["x_t"], 1)

        for l in layers:
            if KINDS[l] == "ssd":
                pe_ssd(pe, l, tile, head_tile, hidden, first_hidden)
                out_and_norm(l, 32)
            if KINDS[l] == "mla":
                pe_mla(pe, l, tile, head_tile, hidden, first_hidden)
                out_and_norm(l, 16)
            if KINDS[l] == "gdn":
                pe_gdn(pe, l, contract, head_tile, hidden, first_hidden)
                out_and_norm(l, 32)
        for i in range(8):
            if i >= 4:
                pe.wait_ge(E["out_rows"], i - 3)
            if i < 4:
                pe.wait_ge(E["last_ready"], 4 * (i + 1))
            for j in range(4):
                c, k = i // 4, i % 4 * 4 + j
                mm = nc.tensor.transpose(bank[4 + i % 4][:, j * P:(j + 1) * P], pre[:, k, c * P:(c + 1) * P], ident)
            mm.then_inc(E["out_t"], 1)

    @block.vector
    def _(dve):
        step = Count()

        def link(ins):
            ins.then_inc(dve_step, 1)
            dve.wait_ge(dve_step, step.next())

        nc.vector.memset(hd[64:96, 8:9], 0.0)
        for i in range(8):
            dve.wait_ge(E["hhi_in"], i + 1)
            k4, cc = slice(i // 2 * 4, i // 2 * 4 + 4), slice(i % 2 * P, (i % 2 + 1) * P)
            nc.vector.tensor_tensor(H_lo[:, k4, cc], as3(bank[4 + i % 4], 4), H_hi[:, k4, cc].bitcast(F32), ALU.subtract
                                    ).then_inc(E["h_in"], 1)
        dve.wait_ge(E["h_in"], 8)
        splitter = Splitter(dve, "dve")
        for p in range(2):
            splitter.split(p, p, p)

        for l in layers:
            if KINDS[l] == "ssd":
                dve_ssd(dve, l, link, step, splitter)
            if KINDS[l] == "mla":
                dve_mla(dve, l, link, step, splitter)
            if KINDS[l] == "gdn":
                dve_gdn(dve, l, link, step)
            dve_gated_lo(dve, l, splitter)
            dve_norm(dve, l, link, step, splitter)
        dve.wait_ge(E["ln_mul"], KD * len(layers))
        for i in range(8):
            dve.wait_ge(E["out_t"], i + 1)
            nc.vector.tensor_copy(xrows[:, i // 4, i % 4 * 512:(i % 4 + 1) * 512], bank[4 + i % 4]
                                  ).then_inc(E["out_rows"], 1)

    @block.scalar
    def _(act):
        astep = Count()

        def link(ins):
            ins.then_inc(act_step, 1)
            act.wait_ge(act_step, astep.next())
        act.dma_start(xrows[:, 1, :], a["x"][0, P:T, :]).then_inc(E["x_in"], 16)
        for dst, src in HEAD_DMAS:
            act.dma_start(dst, src).then_inc(E["heads_in"], 16)
        for i in range(8):
            act.wait_ge(E["x_t"], i + 1)
            k4, cc = slice(i // 2 * 4, i // 2 * 4 + 4), slice(i % 2 * P, (i % 2 + 1) * P)
            nc.scalar.activation(H_hi[:, k4, cc], as3(bank[4 + i % 4], 4), ACT.Copy).then_inc(E["hhi_in"], 1)
        splitter = Splitter(act, "act")
        for p in range(2):
            splitter.split(p, p, p)

        for l in layers:
            if KINDS[l] == "ssd":
                act_ssd(act, l, link, astep, splitter)
            if KINDS[l] == "mla":
                act_mla(act, l, link, astep, splitter)
            if KINDS[l] == "gdn":
                act_gdn(act, l, link, astep, splitter)
            act_gated_hi(act, l)
            act_norm(act, l, link, splitter)

    @block.gpsimd
    def _(pool):
        splitter = Splitter(pool, "pool")
        for p in range(2):
            splitter.split(p, p, p)
        for l in layers:
            if KINDS[l] == "ssd":
                pool_ssd(pool, l, splitter)
            if KINDS[l] == "mla":
                pool_mla(pool, l, splitter)
            if KINDS[l] == "gdn":
                pool_gdn(pool, l, splitter)
            pool_gated_lo(pool, l)
            per = 1 if KINDS[l] == "mla" else 2
            with pool.Fori(0, 4 if l != last_layer else 3) as i:
                for p in range(4 * per):
                    look_ahead(splitter, l, i, p)
            if l == last_layer:
                for p in range(4 * per):
                    look_ahead(splitter, l, 3, p)


_INS = ["x", "positions", "ssd_in_w", "ssd_conv_w", "ssd_conv_b", "ssd_dt_bias", "ssd_a_log", "ssd_d", "ssd_norm_w",
        "ssd_out_w", "mla_in_w", "mla_q_norm_w", "mla_q_up_w", "mla_kv_norm_w", "mla_kv_up_w", "mla_out_w",
        "gdn_in_w", "gdn_conv_w", "gdn_a_log", "gdn_dt_bias", "gdn_norm_w", "gdn_out_w", "ln_g", "ln_b"]


def scratch(nc):
    return {"scr_ssd": nc.dram_tensor("scr_ssd", (2, SSD_HEADS, T), F32).ap(),
            "scr_gdn": nc.dram_tensor("scr_gdn", (2 * GDN_HV, T), F32).ap()}


def kernel(**inputs):
    import concourse.bacc as bacc
    from concourse.bass_utils import run_bass_kernel_spmd

    nc = bacc.Bacc("TRN2", target_bir_lowering=False, num_devices=1)
    arrays, args = {}, {}
    for name in _INS + ["consts"]:
        array = constants() if name == "consts" else np.ascontiguousarray(inputs[name])
        arrays[f"in_{name}"] = array
        args[name] = nc.dram_tensor(f"in_{name}", array.shape, mybir.dt.from_np(array.dtype), kind="ExternalInput").ap()
    args["out"] = nc.dram_tensor("out", (1, T, D), F32, kind="ExternalOutput").ap()
    args.update(scratch(nc))
    build(nc, args)
    r = run_bass_kernel_spmd(nc, [arrays], core_ids=[0])
    return r.results[0]["out"]
```
